# Optimizing a Trainium2 kernel written in Bass

```python
import jax, jax.numpy as jnp
from jax import lax
import numpy as np
import math

D_MODEL = 2048
BATCH = 1
SEQ = 256
DEPTH = 2

GRID_W = 64
CTX_LEN = 256
ROPE_THETA = 10000.0
Q_BLOCK = 128
LN_EPS = 1e-6
RMS_EPS = 1e-6

A_HEADS = 8
A_Q_LORA = 768
A_KV_LORA = 512
A_NOPE = 128
A_ROPE = 64
A_V = 128
A_SCALE = (A_NOPE + A_ROPE) ** -0.5
B_HEADS = 8
B_KV_HEADS = 2
B_GROUP = B_HEADS // B_KV_HEADS
B_HEAD_DIM = 128
B_SCALE = B_HEAD_DIM ** -0.5
A_WIDTH = A_HEADS * A_V
B_WIDTH = B_HEADS * B_HEAD_DIM
ATTN_WIDTH = A_WIDTH + B_WIDTH
ATTN_IN = A_Q_LORA + A_KV_LORA + A_ROPE + B_WIDTH + 2 * B_KV_HEADS * B_HEAD_DIM + ATTN_WIDTH
C_EXPAND = 2
C_WIDTH = C_EXPAND * D_MODEL
C_GROUPS = 16
C_GROUP_DIM = C_WIDTH // C_GROUPS

N_EVEN = (DEPTH + 1) // 2
N_ODD = DEPTH // 2
DEEPNORM_ALPHA = (2.0 * DEPTH) ** 0.25
DEEPNORM_BETA = (8.0 * DEPTH) ** -0.25


def layer_norm(x):
    xf = x.astype(jnp.float32)
    mu = jnp.mean(xf, axis=-1, keepdims=True)
    var = jnp.mean(jnp.square(xf - mu), axis=-1, keepdims=True)
    return ((xf - mu) * lax.rsqrt(var + LN_EPS)).astype(x.dtype)

def rms_norm(x, g):
    xf = x.astype(jnp.float32)
    y = xf * lax.rsqrt(jnp.mean(xf * xf, axis=-1, keepdims=True) + RMS_EPS)
    return (y * g.astype(jnp.float32)).astype(x.dtype)

def axial_rope_angles(rows, rot_dim):
    r, col = jnp.meshgrid(jnp.arange(rows), jnp.arange(GRID_W), indexing="ij")
    r = r.reshape(-1).astype(jnp.float32)
    col = col.reshape(-1).astype(jnp.float32)
    n_freq = rot_dim // 4
    inv = ROPE_THETA ** (-jnp.arange(n_freq, dtype=jnp.float32) / n_freq)
    return jnp.concatenate([r[:, None] * inv, col[:, None] * inv], axis=-1)

def apply_rope(x, ang):
    cos = jnp.cos(ang)[None, :, None, :]
    sin = jnp.sin(ang)[None, :, None, :]
    xf = x.astype(jnp.float32).reshape(*x.shape[:-1], -1, 2)
    x1, x2 = xf[..., 0], xf[..., 1]
    out = jnp.stack([x1 * cos - x2 * sin, x1 * sin + x2 * cos], axis=-1)
    return out.reshape(x.shape).astype(x.dtype)

def block_attention(q, k, v, scale):
    b, s, g, r, dk = q.shape
    nblk = s // Q_BLOCK
    qb = jnp.moveaxis(q.reshape(b, nblk, Q_BLOCK, g, r, dk), 1, 0)

    def one_block(qi):
        sc = jnp.einsum("bqgrd,bkgd->bgrqk", qi, k, preferred_element_type=jnp.float32) * scale
        p = jax.nn.softmax(sc, axis=-1).astype(v.dtype)
        return jnp.einsum("bgrqk,bkge->bqgre", p, v)

    out = lax.map(one_block, qb)
    return jnp.moveaxis(out, 0, 1).reshape(b, s, g, r, v.shape[-1])

def attn_project(h, w_in, wq_b, q_lora_g, kv_lora_g, wkv_b, qn_g, kn_g):
    b, l, _ = h.shape
    splits = np.cumsum([A_Q_LORA, A_KV_LORA, A_ROPE, B_WIDTH,
                        B_KV_HEADS * B_HEAD_DIM, B_KV_HEADS * B_HEAD_DIM]).tolist()
    z = h @ w_in
    c_q, c_kv, k_pe, q_b, k_b, v_b, gate = jnp.split(z, splits, axis=-1)
    q_a = (rms_norm(c_q, q_lora_g) @ wq_b).reshape(b, l, A_HEADS, A_NOPE + A_ROPE)
    kv_a = (rms_norm(c_kv, kv_lora_g) @ wkv_b).reshape(b, l, A_HEADS, A_NOPE + A_V)
    q_nope, q_pe = q_a[..., :A_NOPE], q_a[..., A_NOPE:]
    k_nope, v_a = kv_a[..., :A_NOPE], kv_a[..., A_NOPE:]
    k_pe = k_pe.reshape(b, l, 1, A_ROPE)
    q_b = rms_norm(q_b.reshape(b, l, B_HEADS, B_HEAD_DIM), qn_g)
    k_b = rms_norm(k_b.reshape(b, l, B_KV_HEADS, B_HEAD_DIM), kn_g)
    v_b = v_b.reshape(b, l, B_KV_HEADS, B_HEAD_DIM)
    return q_nope, q_pe, k_nope, k_pe, v_a, q_b, k_b, v_b, gate

def mla_qk(q_nope, q_pe, k_nope, k_pe):
    b, l, h, _ = q_nope.shape
    q = jnp.concatenate([q_nope, q_pe], axis=-1)[:, :, :, None, :]
    k = jnp.concatenate([k_nope, jnp.broadcast_to(k_pe, (b, l, h, A_ROPE))], axis=-1)
    return q, k

def gated_out(y_a, y_b, gate, w_out):
    b, l = y_a.shape[:2]
    y = jnp.concatenate([y_a.reshape(b, l, A_WIDTH), y_b.reshape(b, l, B_WIDTH)], axis=-1)
    return (y * jax.nn.silu(gate)) @ w_out

def attention_mixer(h_lat, h_ctx, ang_a, ang_b, w_in, wq_b, q_lora_g, kv_lora_g, wkv_b,
                    qn_g, kn_g, w_out, with_ctx_queries):
    b, s, _ = h_lat.shape
    lqn, lqp, lkn, lkp, lva, lqb, lkb, lvb, lgate = attn_project(
        h_lat, w_in, wq_b, q_lora_g, kv_lora_g, wkv_b, qn_g, kn_g)
    cqn, cqp, ckn, ckp, cva, cqb, ckb, cvb, cgate = attn_project(
        h_ctx, w_in, wq_b, q_lora_g, kv_lora_g, wkv_b, qn_g, kn_g)
    lqp, lkp = apply_rope(lqp, ang_a), apply_rope(lkp, ang_a)
    lqb, lkb = apply_rope(lqb, ang_b), apply_rope(lkb, ang_b)
    lq_a, lk_a = mla_qk(lqn, lqp, lkn, lkp)
    cq_a, ck_a = mla_qk(cqn, cqp, ckn, ckp)
    k_a_all = jnp.concatenate([ck_a, lk_a], axis=1)
    v_a_all = jnp.concatenate([cva, lva], axis=1)
    k_b_all = jnp.concatenate([ckb, lkb], axis=1)
    v_b_all = jnp.concatenate([cvb, lvb], axis=1)
    y_a = block_attention(lq_a, k_a_all, v_a_all, A_SCALE)
    y_b = block_attention(lqb.reshape(b, s, B_KV_HEADS, B_GROUP, B_HEAD_DIM), k_b_all, v_b_all, B_SCALE)
    out_lat = gated_out(y_a, y_b, lgate, w_out)
    out_ctx = None
    if with_ctx_queries:
        lc = h_ctx.shape[1]
        yc_a = block_attention(cq_a, ck_a, cva, A_SCALE)
        yc_b = block_attention(cqb.reshape(b, lc, B_KV_HEADS, B_GROUP, B_HEAD_DIM), ckb, cvb, B_SCALE)
        out_ctx = gated_out(yc_a, yc_b, cgate, w_out)
    return out_lat, out_ctx

def fourier_mixer(h, w_in, w_out):
    b, l, _ = h.shape
    u, gate = jnp.split(h @ w_in, 2, axis=-1)
    ug = u.reshape(b, l, C_GROUPS, C_GROUP_DIM).astype(jnp.float32)
    f = jnp.fft.fft2(ug, axes=(1, 3), norm="ortho").real.astype(h.dtype)
    y = f.reshape(b, l, C_WIDTH) * jax.nn.silu(gate)
    return y @ w_out

def modulation(cvec, ada_w, ada_b):
    m = jax.nn.silu(cvec) @ ada_w + ada_b
    return jnp.split(m, 3, axis=-1)

def modulate(x, shift, scale):
    return layer_norm(x) * (1.0 + scale) + shift

def post_norm(x, out, gate, g, bias):
    return layer_norm(DEEPNORM_ALPHA * x + gate * out) * g + bias

def first_inputs(seed: int = 0) -> dict:
    key = jax.random.key(seed)
    ks = jax.random.split(key, 24)

    def nrm(k, shape, s):
        return jax.random.normal(k, shape, jnp.float32) * s

    def gain(k, shape):
        return 1.0 + 0.02 * jax.random.normal(k, shape, jnp.float32)

    return {
        "x": nrm(ks[0], (BATCH, SEQ, D_MODEL), 1.0),
        "c": nrm(ks[1], (BATCH, D_MODEL), 1.0),
        "ctx": nrm(ks[2], (BATCH, CTX_LEN, D_MODEL), 1.0),
        "c_ctx": nrm(ks[3], (D_MODEL,), 1.0),
        "ada_w": nrm(ks[4], (DEPTH, D_MODEL, 3 * D_MODEL), 0.5 * D_MODEL ** -0.5),
        "ada_b": nrm(ks[5], (DEPTH, 3 * D_MODEL), 0.01),
        "ln_g": gain(ks[6], (DEPTH, D_MODEL)),
        "ln_b": nrm(ks[7], (DEPTH, D_MODEL), 0.01),
        "w_in_attn": nrm(ks[8], (N_EVEN, D_MODEL, ATTN_IN), D_MODEL ** -0.5),
        "wq_b": nrm(ks[9], (N_EVEN, A_Q_LORA, A_HEADS * (A_NOPE + A_ROPE)), A_Q_LORA ** -0.5),
        "q_lora_norm": gain(ks[10], (N_EVEN, A_Q_LORA)),
        "kv_lora_norm": gain(ks[11], (N_EVEN, A_KV_LORA)),
        "wkv_b": nrm(ks[12], (N_EVEN, A_KV_LORA, A_HEADS * (A_NOPE + A_V)), A_KV_LORA ** -0.5),
        "q_norm_b": gain(ks[13], (N_EVEN, B_HEAD_DIM)),
        "k_norm_b": gain(ks[14], (N_EVEN, B_HEAD_DIM)),
        "w_out_attn": nrm(ks[15], (N_EVEN, ATTN_WIDTH, D_MODEL), DEEPNORM_BETA * ATTN_WIDTH ** -0.5),
        "w_in_fourier": nrm(ks[16], (N_ODD, D_MODEL, 2 * C_WIDTH), D_MODEL ** -0.5),
        "w_out_fourier": nrm(ks[17], (N_ODD, C_WIDTH, D_MODEL), DEEPNORM_BETA * C_WIDTH ** -0.5),
    }

def first_block(x, c, ctx, c_ctx, ada_w, ada_b, ln_g, ln_b, w_in_attn, wq_b, q_lora_norm,
              kv_lora_norm, wkv_b, q_norm_b, k_norm_b, w_out_attn, w_in_fourier, w_out_fourier):
    rows = x.shape[1] // GRID_W
    ang_a = axial_rope_angles(rows, A_ROPE)
    ang_b = axial_rope_angles(rows, B_HEAD_DIM)
    xc = ctx
    for i in range(DEPTH):
        j = i // 2
        ctx_needed = i < DEPTH - 1
        sh_l, sc_l, g_l = [m[:, None, :] for m in modulation(c, ada_w[i], ada_b[i])]
        h_lat = modulate(x, sh_l, sc_l)
        o_ctx = None
        g_c = None
        if i % 2 == 0:
            sh_c, sc_c, g_c = modulation(c_ctx, ada_w[i], ada_b[i])
            h_ctx = modulate(xc, sh_c, sc_c)
            o_lat, o_ctx = attention_mixer(
                h_lat, h_ctx, ang_a, ang_b, w_in_attn[j], wq_b[j], q_lora_norm[j],
                kv_lora_norm[j], wkv_b[j], q_norm_b[j], k_norm_b[j], w_out_attn[j], ctx_needed)
        else:
            o_lat = fourier_mixer(h_lat, w_in_fourier[j], w_out_fourier[j])
            if ctx_needed:
                sh_c, sc_c, g_c = modulation(c_ctx, ada_w[i], ada_b[i])
                o_ctx = fourier_mixer(modulate(xc, sh_c, sc_c), w_in_fourier[j], w_out_fourier[j])
        x = post_norm(x, o_lat, g_l, ln_g[i], ln_b[i])
        if ctx_needed:
            xc = post_norm(xc, o_ctx, g_c, ln_g[i], ln_b[i])
    return x


DEPTH_2 = 1

CHUNK = 64
D_MIX = D_MODEL
D_CONV = D_MIX // 2
D_SSM = D_MIX - D_CONV
CONV_WIDTH = 31
SSM_GROUP = 16
SSM_GROUPS = D_SSM // SSM_GROUP
SSM_STATE = 64
N_MEM = 256
MEM_HEADS = 4
MEM_HEAD_DIM = D_MODEL // MEM_HEADS
PEER_HEADS = 8
PEER_KEYS = 128
PEER_EXPERTS = PEER_KEYS * PEER_KEYS
PEER_DKEY = 128
PEER_HALF = PEER_DKEY // 2
PEER_TOPK = 16
PEER_BLOCK = 128
EPS = 1e-6


F32 = jnp.float32

def rms_norm_2(x, g):
    xf = x.astype(F32)
    y = xf * lax.rsqrt(jnp.mean(xf * xf, axis=-1, keepdims=True) + EPS)
    return (y * g.astype(F32)).astype(x.dtype)

def layer_norm_2(x, g, b):
    xf = x.astype(F32)
    mu = jnp.mean(xf, axis=-1, keepdims=True)
    xc = xf - mu
    y = xc * lax.rsqrt(jnp.mean(xc * xc, axis=-1, keepdims=True) + EPS)
    return (y * g.astype(F32) + b.astype(F32)).astype(x.dtype)

def causal_depthwise_conv(x, w, b):
    k = w.shape[0]
    y = lax.conv_general_dilated(
        x, w[:, None, :].astype(x.dtype), window_strides=(1,), padding=[(k - 1, 0)],
        dimension_numbers=("NWC", "WIO", "NWC"), feature_group_count=x.shape[-1])
    return y + b.astype(x.dtype)

def conformer_conv_group(a, gate, conv_w, conv_b, ln_g, ln_b):
    c = a * jax.nn.sigmoid(gate)
    c = causal_depthwise_conv(c, conv_w, conv_b)
    c = layer_norm_2(c, ln_g, ln_b)
    return c * jax.nn.sigmoid(c)

def s5_group(u, lam_re, lam_im, log_dt, b_re, b_im, c_re, c_im, d, glu_w):
    bsz, length, _ = u.shape
    uf = u.astype(F32).reshape(bsz, length, SSM_GROUPS, SSM_GROUP)
    lam = lax.complex(lam_re.astype(F32), lam_im.astype(F32))
    dt = jnp.exp(log_dt.astype(F32))[:, None]
    lam_bar = jnp.exp(lam * dt)
    b = lax.complex(b_re.astype(F32), b_im.astype(F32))
    b_bar = ((lam_bar - 1.0) / lam)[..., None] * b
    bu = jnp.einsum("blgh,gph->blgp", uf.astype(jnp.complex64), b_bar)
    a = jnp.broadcast_to(lam_bar, bu.shape)

    def combine(left, right):
        a_l, s_l = left
        a_r, s_r = right
        return a_r * a_l, a_r * s_l + s_r

    _, states = lax.associative_scan(combine, (a, bu), axis=1)
    c = lax.complex(c_re.astype(F32), c_im.astype(F32))
    y = jnp.real(jnp.einsum("blgp,ghp->blgh", states, c))
    y = y + d.astype(F32).reshape(SSM_GROUPS, SSM_GROUP) * uf
    y = y.reshape(bsz, length, D_SSM).astype(u.dtype)
    z = jax.nn.gelu(y)
    return z * jax.nn.sigmoid(z @ glu_w)

def mem_cross_attention(h, mem_n, w_q, w_kv, w_o):
    bsz, length, _ = h.shape
    q = (h @ w_q).reshape(bsz, length, MEM_HEADS, MEM_HEAD_DIM)
    kv = (mem_n @ w_kv).reshape(bsz, mem_n.shape[1], 2, MEM_HEADS, MEM_HEAD_DIM)
    k, v = kv[:, :, 0], kv[:, :, 1]
    s = jnp.einsum("blhd,bmhd->bhlm", q, k).astype(F32) * (1.0 / math.sqrt(MEM_HEAD_DIM))
    p = jax.nn.softmax(s, axis=-1).astype(h.dtype)
    o = jnp.einsum("bhlm,bmhd->blhd", p, v).reshape(bsz, length, D_MODEL)
    return o @ w_o

def peer(h, w_q, sub_keys, u_tab, v_tab):
    bsz, length, dm = h.shape
    q = (h @ w_q).astype(F32).reshape(bsz, length, PEER_HEADS, 2, PEER_HALF)
    s = jnp.einsum("blhsk,hsnk->blhsn", q, sub_keys.astype(F32))
    s1, i1 = lax.top_k(s[..., 0, :], PEER_TOPK)
    s2, i2 = lax.top_k(s[..., 1, :], PEER_TOPK)
    cand_s = (s1[..., :, None] + s2[..., None, :]).reshape(bsz, length, PEER_HEADS, PEER_TOPK * PEER_TOPK)
    cand_i = (i1[..., :, None] * PEER_KEYS + i2[..., None, :]).reshape(bsz, length, PEER_HEADS, PEER_TOPK * PEER_TOPK)
    top_s, pos = lax.top_k(cand_s, PEER_TOPK)
    idx = jnp.take_along_axis(cand_i, pos, axis=-1)
    g = jax.nn.softmax(top_s, axis=-1)
    n_tok = bsz * length
    nb = n_tok // PEER_BLOCK
    xb = h.reshape(nb, PEER_BLOCK, dm)
    ib = idx.reshape(nb, PEER_BLOCK, PEER_HEADS * PEER_TOPK)
    gb = g.astype(h.dtype).reshape(nb, PEER_BLOCK, PEER_HEADS * PEER_TOPK)

    def block(args):
        xt, it, gt = args
        u = jnp.take(u_tab, it, axis=0)
        act = jax.nn.gelu(jnp.einsum("td,tkd->tk", xt, u))
        v = jnp.take(v_tab, it, axis=0)
        return jnp.einsum("tk,tkd->td", gt * act, v)

    out = lax.map(block, (xb, ib, gb))
    return out.reshape(bsz, length, dm)

def second_inputs(seed: int = 0) -> dict:
    key = jax.random.key(seed)
    ks = iter(jax.random.split(key, 40))
    nrm = lambda shape, scale: jax.random.normal(next(ks), shape, F32) * scale
    gain = lambda shape: 1.0 + 0.05 * jax.random.normal(next(ks), shape, F32)
    L = DEPTH_2
    n_in = 2 * D_CONV + D_SSM
    lam_re = -0.5 + 0.01 * jax.random.normal(next(ks), (L, SSM_GROUPS, SSM_STATE), F32)
    lam_im = (math.pi * jnp.arange(SSM_STATE, dtype=F32))[None, None, :] + 0.01 * jax.random.normal(next(ks), (L, SSM_GROUPS, SSM_STATE), F32)
    log_dt = jax.random.uniform(next(ks), (L, SSM_GROUPS), F32, math.log(1e-3), math.log(1e-1))
    return {
        "x": nrm((BATCH, SEQ, D_MODEL), 1.0),
        "mem": nrm((BATCH, N_MEM, D_MODEL), 1.0),
        "norm_mix_g": gain((L, D_MODEL)),
        "w_in": nrm((L, D_MODEL, n_in), D_MODEL ** -0.5),
        "conv_w": nrm((L, CONV_WIDTH, D_CONV), CONV_WIDTH ** -0.5),
        "conv_b": nrm((L, D_CONV), 0.02),
        "conv_ln_g": gain((L, D_CONV)),
        "conv_ln_b": nrm((L, D_CONV), 0.02),
        "ssm_lam_re": lam_re,
        "ssm_lam_im": lam_im,
        "ssm_log_dt": log_dt,
        "ssm_b_re": nrm((L, SSM_GROUPS, SSM_STATE, SSM_GROUP), (2.0 * SSM_GROUP) ** -0.5),
        "ssm_b_im": nrm((L, SSM_GROUPS, SSM_STATE, SSM_GROUP), (2.0 * SSM_GROUP) ** -0.5),
        "ssm_c_re": nrm((L, SSM_GROUPS, SSM_GROUP, SSM_STATE), (2.0 * SSM_STATE) ** -0.5),
        "ssm_c_im": nrm((L, SSM_GROUPS, SSM_GROUP, SSM_STATE), (2.0 * SSM_STATE) ** -0.5),
        "ssm_d": nrm((L, D_SSM), 1.0),
        "ssm_glu_w": nrm((L, D_SSM, D_SSM), D_SSM ** -0.5),
        "grp_norm_conv_g": gain((L, D_CONV)),
        "grp_norm_ssm_g": gain((L, D_SSM)),
        "w_out": nrm((L, D_MIX, D_MODEL), D_MIX ** -0.5),
        "norm_mem_g": gain((L, D_MODEL)),
        "mem_norm_g": gain((L, D_MODEL)),
        "w_q_mem": nrm((L, D_MODEL, D_MODEL), D_MODEL ** -0.5),
        "w_kv_mem": nrm((L, D_MODEL, 2 * D_MODEL), D_MODEL ** -0.5),
        "w_o_mem": nrm((L, D_MODEL, D_MODEL), D_MODEL ** -0.5),
        "norm_ffn_g": gain((L, D_MODEL)),
        "peer_w_q": nrm((L, D_MODEL, PEER_HEADS * PEER_DKEY), D_MODEL ** -0.5),
        "peer_keys": nrm((L, PEER_HEADS, 2, PEER_KEYS, PEER_HALF), PEER_HALF ** -0.5),
        "peer_u": nrm((L, PEER_EXPERTS, D_MODEL), D_MODEL ** -0.5),
        "peer_v": nrm((L, PEER_EXPERTS, D_MODEL), PEER_TOPK ** -0.5),
        "final_norm_g": gain((D_MODEL,)),
    }

def second_block(x, mem, norm_mix_g, w_in, conv_w, conv_b, conv_ln_g, conv_ln_b,
              ssm_lam_re, ssm_lam_im, ssm_log_dt, ssm_b_re, ssm_b_im, ssm_c_re, ssm_c_im,
              ssm_d, ssm_glu_w, grp_norm_conv_g, grp_norm_ssm_g, w_out,
              norm_mem_g, mem_norm_g, w_q_mem, w_kv_mem, w_o_mem,
              norm_ffn_g, peer_w_q, peer_keys, peer_u, peer_v, final_norm_g):
    h = x
    for i in range(DEPTH_2):
        hn = rms_norm_2(h, norm_mix_g[i])
        proj = hn @ w_in[i]
        conv_a = proj[..., :D_CONV]
        conv_gate = proj[..., D_CONV:2 * D_CONV]
        ssm_u = proj[..., 2 * D_CONV:]
        yc = conformer_conv_group(conv_a, conv_gate, conv_w[i], conv_b[i], conv_ln_g[i], conv_ln_b[i])
        ys = s5_group(ssm_u, ssm_lam_re[i], ssm_lam_im[i], ssm_log_dt[i], ssm_b_re[i], ssm_b_im[i],
                      ssm_c_re[i], ssm_c_im[i], ssm_d[i], ssm_glu_w[i])
        y = jnp.concatenate([rms_norm_2(yc, grp_norm_conv_g[i]), rms_norm_2(ys, grp_norm_ssm_g[i])], axis=-1)
        h = h + y @ w_out[i]
        hn = rms_norm_2(h, norm_mem_g[i])
        mem_n = rms_norm_2(mem, mem_norm_g[i])
        h = h + mem_cross_attention(hn, mem_n, w_q_mem[i], w_kv_mem[i], w_o_mem[i])
        hn = rms_norm_2(h, norm_ffn_g[i])
        h = h + peer(hn, peer_w_q[i], peer_keys[i], peer_u[i], peer_v[i])
    return rms_norm_2(h, final_norm_g)


def setup_inputs(seed=0):
    out = dict(first_inputs(seed))
    for name, value in second_inputs(seed + 1).items():
        if name != "x":
            out[name + "_2"] = value
    return out


def reference(
    x, c, ctx, c_ctx, ada_w, ada_b, ln_g, ln_b, w_in_attn, wq_b, q_lora_norm, kv_lora_norm,
    wkv_b, q_norm_b, k_norm_b, w_out_attn, w_in_fourier, w_out_fourier, mem_2, norm_mix_g_2,
    w_in_2, conv_w_2, conv_b_2, conv_ln_g_2, conv_ln_b_2, ssm_lam_re_2, ssm_lam_im_2,
    ssm_log_dt_2, ssm_b_re_2, ssm_b_im_2, ssm_c_re_2, ssm_c_im_2, ssm_d_2, ssm_glu_w_2,
    grp_norm_conv_g_2, grp_norm_ssm_g_2, w_out_2, norm_mem_g_2, mem_norm_g_2, w_q_mem_2,
    w_kv_mem_2, w_o_mem_2, norm_ffn_g_2, peer_w_q_2, peer_keys_2, peer_u_2, peer_v_2,
    final_norm_g_2,
):
    x = first_block(
        x, c, ctx, c_ctx, ada_w, ada_b, ln_g, ln_b, w_in_attn, wq_b, q_lora_norm, kv_lora_norm,
        wkv_b, q_norm_b, k_norm_b, w_out_attn, w_in_fourier, w_out_fourier,
    )
    return second_block(
        x, mem_2, norm_mix_g_2, w_in_2, conv_w_2, conv_b_2, conv_ln_g_2, conv_ln_b_2,
        ssm_lam_re_2, ssm_lam_im_2, ssm_log_dt_2, ssm_b_re_2, ssm_b_im_2, ssm_c_re_2,
        ssm_c_im_2, ssm_d_2, ssm_glu_w_2, grp_norm_conv_g_2, grp_norm_ssm_g_2, w_out_2,
        norm_mem_g_2, mem_norm_g_2, w_q_mem_2, w_kv_mem_2, w_o_mem_2, norm_ffn_g_2, peer_w_q_2,
        peer_keys_2, peer_u_2, peer_v_2, final_norm_g_2,
    )


_drawn_inputs = setup_inputs


def setup_inputs(seed=0):
    import zlib

    import numpy as np

    out = dict(_drawn_inputs(seed))
    spreads = {}
    factors = {'ctx': 7.685,
     'c_ctx': 4.068,
     'ada_b': 8.0,
     'ln_b': 3.04,
     'wq_b': 7.668,
     'q_lora_norm': 8.0,
     'kv_lora_norm': 8.0,
     'wkv_b': 3.464,
     'q_norm_b': 8.0,
     'k_norm_b': 8.0,
     'conv_ln_b_2': 4.048,
     'ssm_lam_re_2': 64.0,
     'norm_mem_g_2': 8.0,
     'mem_norm_g_2': 6.256,
     'norm_ffn_g_2': 8.0,
     'peer_w_q_2': 2.935,
     'peer_keys_2': 2.911,
     'peer_u_2': 3.246,
     'peer_v_2': 2.948}
    for name, (base, spread) in spreads.items():
        noise = np.random.default_rng([zlib.crc32(name.encode()), seed]).standard_normal(out[name].shape)
        drawn = base * np.exp(spread * noise) if base else spread * noise
        out[name] = __import__('jax').numpy.asarray(drawn.astype(out[name].dtype))
    for name, factor in factors.items():
        out[name] = (out[name] * factor).astype(out[name].dtype)
    return out
```

```python
from contextlib import ExitStack

import numpy as np
import concourse.bass as bass
from concourse import mybir

F32 = mybir.dt.float32
U32 = mybir.dt.uint32
ACT = mybir.ActivationFunctionType
ALU = mybir.AluOpType
AX_X = mybir.AxisListType.X

P = 128
D = 2048
KD = D // P
SEQ = 256
NT = SEQ // P
EPS = 1e-6
ALPHA = (2.0 * 2) ** 0.25

Q_LORA, KV_LORA, ROPE_A, HEADS, HD = 768, 512, 64, 8, 128
KV_HEADS = 2
A_SCALE = (HD + ROPE_A) ** -0.5
B_SCALE = HD ** -0.5
C_WIDTH, C_GROUPS, C_DIM = 4096, 16, 256

D_CONV, TAPS = 1024, 31
S_GROUPS, S_DIM, S_STATE = 64, 16, 64
S_TILES = S_GROUPS * S_STATE // P
S_BATCH = 8
MEM_HEADS, MEM_HD = 4, 512
E_HEADS, E_KEYS, E_HALF, TOPK = 8, 128, 64, 16
E_SLOTS = E_HEADS * TOPK

SLOT = 4096
RING = 4
ARENA = 30 * 1024
LOWEST = -3.0e38

COLS = {}
_n = 0
for _name, _w in [("cvec", 32), ("ada_b0", 48), ("ada_b1", 48), ("q_lora", 6), ("kv_lora", 4), ("mix_g", 16),
                  ("conv_b", 8), ("conv_ln_g", 8), ("conv_ln_b", 8), ("grp_conv", 8), ("grp_ssm", 8),
                  ("ssm_d", 8), ("mem_g", 16), ("memn_g", 16), ("conv_w", 8 * TAPS),
                  ("lam_re", S_TILES), ("lam_im", S_TILES), ("log_dt", S_TILES)]:
    COLS[_name] = (_n, _w)
    _n += _w
NCOLS = _n


class Engine:

    def __init__(self, eng, sem):
        self.eng, self.sem, self.count, self.seen = eng, sem, 0, {}

    def wait(self, *marks):
        for m in marks:
            if m is None:
                continue
            if isinstance(m, list):
                self.wait(*m)
                continue
            sem, value = m
            if self.seen.get(sem.name, 0) < value:
                self.eng.wait_ge(sem, value)
                self.seen[sem.name] = value

    def done(self, ins):
        self.count += 1
        ins.then_inc(self.sem, 1)
        return (self.sem, self.count)

    def last(self):
        return (self.sem, self.count) if self.count else None


class DmaSem:

    def __init__(self, sem):
        self.sem, self.count = sem, 0

    def done(self, ins):
        self.count += 16
        ins.then_inc(self.sem, 16)
        return (self.sem, self.count)


class Banks:

    def __init__(self, banks):
        self.banks, self.free, self.at = banks, [None] * len(banks), 0

    def take(self):
        i = self.at
        self.at = (i + 1) % len(self.banks)
        return i


class Core:
    def __init__(self, nc, ctx):
        self.nc, self.ctx = nc, ctx
        self.PE = Engine(nc.tensor, self.sem("pe_done"))
        self.V = Engine(nc.vector, self.sem("dve_done"))
        self.A = Engine(nc.scalar, self.sem("act_done"))
        self.G = Engine(nc.gpsimd, self.sem("pool_done"))
        self.S = Engine(nc.sync, self.sem("sp_done"))
        self.ring = self.sb("ring", [P, RING, SLOT])
        self.ring_sems = [DmaSem(self.sem(f"ring_slot{i}")) for i in range(RING)]
        self.ring_free = [None] * RING
        self.ring_at = 0
        self.ring_held = [False] * RING
        self.arena = self.sb("arena", [P, ARENA])
        self.lin = Banks([self.ps(f"lin{i}") for i in range(4)])
        self.aux = Banks([self.ps(f"aux{i}") for i in range(4)])
        self.flip = 0

    def sem(self, name):
        return self.ctx.enter_context(self.nc.semaphore(name))

    def sb(self, name, shape, dt=F32):
        return self.ctx.enter_context(self.nc.sbuf_tensor(name, shape, dt))

    def ps(self, name):
        return self.ctx.enter_context(self.nc.psum_tensor(name, [P, 512], F32))

    def at(self, first, *shape):
        n = 1
        for s in shape:
            n *= s
        assert first + n <= ARENA, (first, shape)
        ap = self.arena[:, first:first + n]
        if len(shape) == 2:
            return ap.rearrange("p (a b) -> p a b", a=shape[0])
        if len(shape) == 3:
            return ap.rearrange("p (a b c) -> p a b c", a=shape[0], b=shape[1])
        return ap

    def barrier(self):
        marks = [e.last() for e in (self.PE, self.V, self.A, self.G)]
        for e in (self.PE, self.V, self.A, self.G):
            e.wait(marks)

    def load(self, src, *shape, after=None):
        i = self.take_slot()
        n = 1
        for s in shape:
            n *= s
        ap = self.ring[:, i, 0:n]
        if len(shape) == 2:
            ap = ap.rearrange("p (a b) -> p a b", a=shape[0])
        self.S.wait(after)
        return ap, self.ring_sems[i].done(self.nc.sync.dma_start(ap, src)), i

    def take_slot(self):
        while self.ring_held[self.ring_at]:
            self.ring_at = (self.ring_at + 1) % RING
        i = self.ring_at
        self.ring_at = (i + 1) % RING
        self.ring_held[i] = True
        self.S.wait(self.ring_free[i])
        return i

    def release(self, slot, *marks):
        self.ring_free[slot] = list(marks)
        self.ring_held[slot] = False

    def evac(self, dst, src, ready, scale=None, bias=None, same=False):
        if not same:
            self.flip ^= 1
        if self.flip:
            self.V.wait(ready)
            if scale is None:
                return self.V.done(self.nc.vector.tensor_copy(dst, src))
            if bias is None:
                return self.V.done(self.nc.vector.tensor_scalar(dst, src, scale, None, ALU.mult))
            return self.V.done(self.nc.vector.tensor_scalar(dst, src, scale, bias, ALU.mult, ALU.add))
        self.A.wait(ready)
        if scale is None:
            return self.A.done(self.nc.scalar.copy(dst, src))
        if bias is None:
            return self.A.done(self.nc.scalar.activation(dst, src, ACT.Identity, scale=scale))
        return self.A.done(self.nc.scalar.activation(dst, src, ACT.Identity, bias=bias, scale=scale))

    def linear_rows(self, W, n0, n1, lhs, tiles, lhs_ready, evac, kc=8):
        nc, PE = self.nc, self.PE
        K = W.shape[0] // P
        PE.wait(lhs_ready)
        for n in range(n0, n1, 512):
            w = min(512, n1 - n)
            ids = [self.lin.take() for _ in tiles]
            for i in ids:
                PE.wait(self.lin.free[i])
            for c in range(0, K, kc):
                wt, arrived, slot = self.load(
                    W[c * P:(c + kc) * P, n:n + w].rearrange("(k p) n -> p k n", p=P), kc, w)
                PE.wait(arrived)
                for i, t in zip(ids, tiles):
                    for k in range(kc):
                        mm = nc.tensor.matmul(self.lin.banks[i][:, 0:w], lhs(c + k, t), wt[:, k, :],
                                              start=(c + k == 0), stop=(c + k == K - 1))
                    mark = PE.done(mm)
                    if c + kc == K:
                        self.lin.free[i] = evac(t, n, w, self.lin.banks[i][:, 0:w], mark)
                self.release(slot, mark)

    def linear_cols(self, W, n0, n1, rhs, R, rhs_ready, evac, kc=8):
        nc, PE = self.nc, self.PE
        K = W.shape[0] // P
        per = min(4, 512 // R)
        PE.wait(rhs_ready)
        for n in range(n0, n1, 512):
            w = min(512, n1 - n)
            nj = w // P
            ids = [self.lin.take() for _ in range(0, nj, per)]
            for i in ids:
                PE.wait(self.lin.free[i])
            for c in range(0, K, kc):
                wt, arrived, slot = self.load(
                    W[c * P:(c + kc) * P, n:n + w].rearrange("(k p) n -> p k n", p=P), kc, w)
                PE.wait(arrived)
                for j in range(nj):
                    i = ids[j // per]
                    out = self.lin.banks[i][:, (j % per) * R:(j % per + 1) * R]
                    for k in range(kc):
                        mm = nc.tensor.matmul(out, wt[:, k, j * P:(j + 1) * P], rhs(c + k),
                                              start=(c + k == 0 and j % per == 0), stop=(c + k == K - 1),
                                              skip_group_check=True)
                    if j % per == per - 1 or j == nj - 1:
                        mark = PE.done(mm)
                        if c + kc == K:
                            j0 = j - j % per
                            cnt = j - j0 + 1
                            self.lin.free[i] = evac((n - n0) // P + j0, cnt, self.lin.banks[i][:, 0:cnt * R], mark)
                self.release(slot, mark)

    def turn(self, src, dst, nk, nt, ready, gain=None, shift=None):
        nc, PE = self.nc, self.PE
        PE.wait(ready)
        kk = max(1, 4 // nt)
        for k0 in range(0, nk, kk):
            i = self.aux.take()
            PE.wait(self.aux.free[i])
            ks = range(k0, min(nk, k0 + kk))
            for k in ks:
                for t in range(nt):
                    a = src(k, t)
                    f = a.shape[1]
                    mm = nc.tensor.transpose(
                        self.aux.banks[i][0:f, ((k - k0) * nt + t) * P:((k - k0) * nt + t + 1) * P], a, self.ident[:, :])
            mark = PE.done(mm)
            free = []
            for k in ks:
                d = dst(k)
                free.append(self.evac(d, self.aux.banks[i][0:f, (k - k0) * nt * P:(k - k0 + 1) * nt * P], mark,
                                      None if gain is None else gain(k), None if shift is None else shift(k),
                                      same=k > k0))
            self.aux.free[i] = free
        return [self.V.last(), self.A.last()]

    def rstd(self, dst, src, ready, mul, tmp):
        nc, V, A = self.nc, self.V, self.A
        v, s = tmp
        V.wait(ready)
        m = V.done(nc.vector.tensor_scalar(v, src, mul, EPS, ALU.mult, ALU.add))
        A.wait(m)
        m = A.done(nc.scalar.activation(s, v, ACT.Sqrt))
        V.wait(m)
        V.wait(V.done(nc.vector.reciprocal(dst, s)))
        V.wait(V.done(nc.vector.tensor_tensor(s, dst, dst, ALU.mult)))
        V.wait(V.done(nc.vector.tensor_tensor(s, s, v, ALU.mult)))
        V.wait(V.done(nc.vector.tensor_scalar(s, s, -0.5, 1.5, ALU.mult, ALU.add)))
        m = V.done(nc.vector.tensor_tensor(dst, dst, s, ALU.mult))
        V.wait(m)
        return m

    def layer_norm_rows(self, src, dst, ready):
        nc, V = self.nc, self.V
        V.wait(ready)
        for t in range(NT):
            for j in range(4):
                m = V.done(nc.vector.bn_stats(self.bn[:, t, j, :], src(t)[:, j * 512:(j + 1) * 512]))
        V.wait(m)
        for t in range(NT):
            m = V.done(nc.vector.bn_aggr(self.mv[:, t, :], self.bn[:, t, :, :].rearrange("p a b -> p (a b)")))
        self.rstd(self.st[:, 0:NT], self.mv[:, :, 1], m, 1.0, (self.st[:, 8:8 + NT], self.st[:, 16:16 + NT]))
        for t in range(NT):
            m = V.done(nc.vector.tensor_scalar(dst(t), src(t), self.mv[:, t, 0:1], self.st[:, t:t + 1],
                                               ALU.subtract, ALU.mult))
        V.wait(m)
        return m

    def rms_rows(self, src, dst, ready, junk):
        nc, V, A = self.nc, self.V, self.A
        A.wait(ready, V.last())
        for t in range(NT):
            m = A.done(nc.scalar.activation(junk, src(t), ACT.Square, accum_out=self.st[:, 24 + t:25 + t]))
            A.wait(m)
        self.rstd(self.st[:, 0:NT], self.st[:, 24:24 + NT], m, 1.0 / D,
                  (self.st[:, 8:8 + NT], self.st[:, 16:16 + NT]))
        for t in range(NT):
            m = V.done(nc.vector.tensor_scalar(dst(t), src(t), self.st[:, t:t + 1], None, ALU.mult))
        V.wait(m)
        return m

    def spread_column(self, col, dst, ready):
        nc, PE, V = self.nc, self.PE, self.V
        for b in range(4):
            i = self.aux.take()
            V.wait(ready, PE.last())
            for j in range(4):
                m = V.done(nc.vector.tensor_scalar(self.diag[:, j, :], self.ident[:, :],
                                                   col[:, b * 4 + j:b * 4 + j + 1], None, ALU.mult))
            PE.wait(m, self.aux.free[i])
            mm = nc.tensor.matmul(self.aux.banks[i][:, :], self.ones[:, :],
                                  self.diag[:, :, :].rearrange("p a b -> p (a b)"), start=True, stop=True)
            m = PE.done(mm)
            V.wait(m)
            m = V.done(nc.vector.tensor_copy(dst[:, b * 512:(b + 1) * 512], self.aux.banks[i][:, :]))
            self.aux.free[i] = [m]
        return m

    def col(self, name, j=None):
        a, w = COLS[name]
        return self.colpack[:, a:a + w] if j is None else self.colpack[:, a + j:a + j + 1]


def constants(c, I):
    nc = c.nc
    c.ident = c.sb("ident", [P, P])
    c.ones = c.sb("ones", [P, P])
    c.diag = c.sb("diag", [P, 4, P])
    c.colpack = c.sb("colpack_sb", [P, NCOLS])
    c.rope = c.sb("rope_sb", [P, NT, 192])
    c.bn = c.sb("bn", [P, NT, 4, 6])
    c.mv = c.sb("mv", [P, NT, 2])
    c.st = c.sb("st", [P, 64])
    c.iota = c.sb("iota_sb", [P, 16])
    c.mod = c.sb("mod", [P, 2, 48, 2])
    s = DmaSem(c.sem("constants"))
    for dst, src in ((c.ident, I["ident"]), (c.colpack, I["colpack"]), (c.iota, I["iota"]), (c.ones, I["ones"]),
                     (c.rope, I["rope"])):
        m = s.done(nc.sync.dma_start(dst[:], src))
    for e in (c.PE, c.V, c.A, c.G):
        e.wait(m)


def softmax_rows(c, psum, ready, scale, prob, n, tmp):
    nc, V, A = c.nc, c.V, c.A
    V.wait(ready)
    V.wait(V.done(nc.vector.tensor_reduce(tmp[:, 0:1], psum, AX_X, ALU.max)))
    m = V.done(nc.vector.tensor_scalar(tmp[:, 1:2], tmp[:, 0:1], -scale, None, ALU.mult))
    A.wait(m)
    m = A.done(nc.scalar.activation(prob, psum, ACT.Exp, bias=tmp[:, 1:2], scale=scale, accum_out=tmp[:, 2:3]))
    V.wait(m)
    V.wait(V.done(nc.vector.reciprocal(tmp[:, 3:4], tmp[:, 2:3])))
    return V.done(nc.vector.tensor_scalar(prob, prob, tmp[:, 3:4], None, ALU.mult)), m


def stage_start(c, I, dr):
    nc, PE, V, A = c.nc, c.PE, c.V, c.A
    memT = c.at(0, KD, SEQ)
    KT = c.at(4096, KD, SEQ)
    VV = c.at(8192, NT, D)
    junk = c.at(12288, D)
    cv = c.at(16384, 2, KD)
    mem, arrived, slot = c.load(I["mem_2"][0].rearrange("(t p) d -> p t d", p=P), NT, D)
    A.wait(arrived)
    m_cv = A.done(nc.scalar.activation(cv, c.col("cvec").rearrange("p (a b) -> p a b", a=2), ACT.Silu))
    V.wait(arrived)
    m = c.rms_rows(lambda t: mem[:, t, :], lambda t: mem[:, t, :], arrived, junk)
    mT = c.turn(lambda k, t: mem[:, t, k * P:(k + 1) * P], lambda k: memT[:, k, :], KD, NT, m,
                gain=lambda k: c.col("memn_g", k))
    c.release(slot, PE.last())

    def evac_mod(layer):
        def go(j, cnt, ps, ready):
            V.wait(ready)
            b = c.col("ada_b%d" % layer)[:, j:j + cnt].unsqueeze(2).broadcast_to([P, cnt, 2])
            return [V.done(nc.vector.tensor_tensor(c.mod[:, layer, j:j + cnt, :],
                                                   ps.rearrange("p (a b) -> p a b", b=2), b, ALU.add))]
        return go

    def ada(layer, n):
        W = I["ada_w"][layer]
        c.linear_cols(W, n, n + 512, lambda k: cv[:, :, k], 2, m_cv,
                      lambda j, cnt, ps, r: evac_mod(layer)(n // P + j, cnt, ps, r))

    blocks = [(l, n) for l in range(2) for n in range(0, 3 * D, 512)]
    Wkv = I["w_kv_mem_2"][0]
    for i in range(8):
        for l, n in blocks[3 * i:3 * i + 3]:
            ada(l, n)
        n = i * 512
        if i < 4:
            c.linear_cols(Wkv, n, n + 512, lambda k: memT[:, k, :], SEQ, mT,
                          lambda j, cnt, ps, r: [c.evac(KT[:, n // P + j:n // P + j + cnt, :],
                                                        ps.rearrange("p (a b) -> p a b", b=SEQ), r)])
        else:
            c.linear_rows(Wkv, n, n + 512, lambda k, t: memT[:, k, t * P:(t + 1) * P], range(NT), mT,
                          lambda t, nn, w, ps, r: [c.evac(VV[:, t, nn - D:nn - D + w], ps, r)])
    V.wait(V.last())
    for l in range(2):
        m = V.done(nc.vector.tensor_scalar(c.mod[:, l, 16:32, :], c.mod[:, l, 16:32, :], 1.0, None, ALU.add))
    V.wait(m)
    c.m_mod = m
    c.S.wait(V.last(), A.last())
    s = DmaSem(c.sem("mem_kv_stored"))
    s.done(nc.sync.dma_start(dr["memk"], KT))
    c.mem_kv_stored = s.done(nc.sync.dma_start(dr["memv"], VV))


def stage_phases(c, I, dr):
    nc, V, A, G = c.nc, c.V, c.A, c.G
    c.rho = c.sb("rho", [P, S_TILES])
    c.kap = c.sb("kap", [P, 2, S_TILES])
    T = c.at(16448, 10, S_TILES)
    dt, x, th, cs, sn, t0, t1, t2 = (T[:, i, :] for i in range(8))
    lr, li = c.col("lam_re"), c.col("lam_im")

    def v(ins):
        m = V.done(ins)
        V.wait(m)
        return m

    vt = nc.vector.tensor_tensor
    vs = nc.vector.tensor_scalar
    A.wait(A.done(nc.scalar.activation(dt, c.col("log_dt"), ACT.Exp)))
    V.wait(A.last())
    v(vt(x, lr, dt, ALU.mult))
    m = v(vt(th, li, dt, ALU.mult))
    A.wait(m)
    m = A.done(nc.scalar.activation(c.rho[:, :], x, ACT.Exp))
    V.wait(m)
    big = 12582912.0
    two_pi = 2 * np.pi
    p1 = 6.28125
    p2 = float(np.float32(np.round((two_pi - p1) * 2 ** 22) / 2 ** 22))
    p3 = float(two_pi - p1 - p2)
    v(vs(t0, th, 1.0 / two_pi, big, ALU.mult, ALU.add))
    v(vs(t0, t0, -big, None, ALU.add))
    for part in (p1, p2, p3):
        v(nc.vector.scalar_tensor_tensor(out=th, in0=t0, scalar=-part, in1=th, op0=ALU.mult, op1=ALU.add))
    lim = 3.1415925
    m = v(vs(th, th, lim, -lim, ALU.min, ALU.max))
    A.wait(m)
    A.done(nc.scalar.activation(sn, th, ACT.Sin))
    m = A.done(nc.scalar.activation(t1, th, ACT.Sin, scale=0.5))
    V.wait(m)
    v(vt(t1, t1, t1, ALU.mult))
    v(vs(cs, t1, -2.0, 1.0, ALU.mult, ALU.add))
    v(vt(t0, c.rho[:, :], cs, ALU.mult))
    v(vs(t0, t0, -1.0, None, ALU.add))
    v(vt(t1, c.rho[:, :], sn, ALU.mult))
    kr, ki = c.kap[:, 0, :], c.kap[:, 1, :]
    v(vt(kr, t0, lr, ALU.mult))
    v(vt(t2, t1, li, ALU.mult))
    v(vt(kr, kr, t2, ALU.add))
    v(vt(ki, t1, lr, ALU.mult))
    v(vt(t2, t0, li, ALU.mult))
    v(vt(ki, ki, t2, ALU.subtract))
    v(vt(t0, lr, lr, ALU.mult))
    v(vt(t1, li, li, ALU.mult))
    v(vt(t0, t0, t1, ALU.add))
    v(nc.vector.reciprocal(t1, t0))
    v(vt(kr, kr, t1, ALU.mult))
    v(vt(ki, ki, t1, ALU.mult))
    s = DmaSem(c.sem("phases_stored"))
    E = c.at(17408, 2, S_BATCH, SEQ)
    tmp = c.at(17408 + 4096, 2, S_BATCH, SEQ // 2)
    stored = None
    for b in range(S_TILES // S_BATCH):
        lo, hi = b * S_BATCH, (b + 1) * S_BATCH
        V.wait(stored)
        v(nc.vector.memset(E[:, 0, :, 0:1], 1.0))
        v(nc.vector.memset(E[:, 1, :, 0:1], 0.0))
        v(nc.vector.tensor_copy(E[:, 0, :, 1], cs[:, lo:hi]))
        v(nc.vector.tensor_copy(E[:, 1, :, 1], sn[:, lo:hi]))
        n = 2
        cn, sq, tt, uu = T[:, 6, 0:S_BATCH], T[:, 7, 0:S_BATCH], T[:, 8, 0:S_BATCH], T[:, 9, 0:S_BATCH]
        while n < SEQ:
            a, d = E[:, 0, :, n - 1], E[:, 1, :, n - 1]
            v(vt(tt, a, cs[:, lo:hi], ALU.mult))
            v(vt(uu, d, sn[:, lo:hi], ALU.mult))
            v(vt(cn, tt, uu, ALU.subtract))
            v(vt(tt, a, sn[:, lo:hi], ALU.mult))
            v(vt(uu, d, cs[:, lo:hi], ALU.mult))
            v(vt(sq, tt, uu, ALU.add))
            C = cn.unsqueeze(2).broadcast_to([P, S_BATCH, n])
            S = sq.unsqueeze(2).broadcast_to([P, S_BATCH, n])
            e0, e1 = E[:, 0, :, 0:n], E[:, 1, :, 0:n]
            x0, x1 = tmp[:, 0, :, 0:n], tmp[:, 1, :, 0:n]
            V.done(vt(x0, e0, C, ALU.mult))
            v(vt(x1, e1, S, ALU.mult))
            v(vt(E[:, 0, :, n:2 * n], x0, x1, ALU.subtract))
            V.done(vt(x0, e0, S, ALU.mult))
            v(vt(x1, e1, C, ALU.mult))
            m = v(vt(E[:, 1, :, n:2 * n], x0, x1, ALU.add))
            n *= 2
        G = c.G
        G.wait(m)
        stored = s.done(nc.gpsimd.dma_start(dr["phase"][b].rearrange("p (e x) -> p e x", e=2),
                                            E.rearrange("p e a b -> p e (a b)")))
    c.phases_stored = stored
    V.wait(stored)


def rope_rows(c, x, cos, sin, heads, half, tmp):
    nc, V = c.nc, c.V
    xe = x.rearrange("p h (f two) -> p h f two", two=2)
    x1, x2 = xe[:, :, :, 0], xe[:, :, :, 1]
    C = cos.unsqueeze(1).broadcast_to([P, heads, half])
    S = sin.unsqueeze(1).broadcast_to([P, heads, half])
    n = heads * half
    t = [tmp[:, i * n:(i + 1) * n].rearrange("p (h f) -> p h f", h=heads) for i in range(4)]
    V.done(nc.vector.tensor_tensor(t[0], x1, C, ALU.mult))
    V.done(nc.vector.tensor_tensor(t[1], x2, S, ALU.mult))
    V.done(nc.vector.tensor_tensor(t[2], x1, S, ALU.mult))
    V.wait(V.done(nc.vector.tensor_tensor(t[3], x2, C, ALU.mult)))
    V.done(nc.vector.tensor_tensor(x1, t[0], t[1], ALU.subtract))
    m = V.done(nc.vector.tensor_tensor(x2, t[2], t[3], ALU.add))
    V.wait(m)
    return m


def post_norm(c, H, gate_row, g_slot, m_g, base_ready):
    nc, V = c.nc, c.V
    m = c.layer_norm_rows(lambda t: H[:, t, :], lambda t: H[:, t, :], base_ready)
    gb, arrived, slot = g_slot
    V.wait(arrived, m)
    for t in range(NT):
        V.done(nc.vector.tensor_tensor(H[:, t, :], H[:, t, :], gb[:, 0:D], ALU.mult))
    V.wait(V.last())
    for t in range(NT):
        V.done(nc.vector.tensor_tensor(H[:, t, :], H[:, t, :], gb[:, D:2 * D], ALU.add))
    V.wait(V.last())
    c.release(slot, V.last())
    return V.last()


def load_gb(c, I, layer):
    i = c.take_slot()
    s = c.ring_sems[i]
    s.done(c.nc.sync.dma_start(c.ring[:, i, 0:D], I["ln_g"][layer].partition_broadcast(P)))
    m = s.done(c.nc.sync.dma_start(c.ring[:, i, D:2 * D], I["ln_b"][layer].partition_broadcast(P)))
    return c.ring[:, i, :], m, i


def stage_attention(c, I):
    nc, PE, V, A = c.nc, c.PE, c.V, c.A
    K1 = 1024
    hT = c.at(0, KD, 2 * SEQ)
    gT = c.at(8 * K1, KD, SEQ)
    cq = c.at(12 * K1, NT, Q_LORA)
    qb = c.at(12 * K1 + 1536, NT, 1024)
    kb = c.at(12 * K1 + 3584, 4, 256)
    ckv = c.at(12 * K1 + 4608, 4, KV_LORA)
    vb = c.at(12 * K1 + 6656, 4, 256)
    kpe = c.at(12 * K1 + 7680, 4, ROPE_A)
    base = 20 * K1
    cqT = c.at(base, 6, SEQ)
    qa = c.at(base + 1536, NT, HEADS * 192)
    ckvT = c.at(base + 4608, 4, 2 * SEQ)
    qbT = c.at(base + 6656, HEADS, SEQ)
    kbT = c.at(base + 8704, KV_HEADS, 2 * SEQ)
    kpeT = c.at(base + 9728, 2 * SEQ)
    qn = c.sb("qk_norm", [P, 2, HD])
    ss = c.sb("head_ss", [P, 3, 24])

    s = DmaSem(c.sem("qk_norm_loaded"))
    s.done(nc.gpsimd.dma_start(qn[:, 0, :], I["q_norm_b"][0].partition_broadcast(P)))
    m_qn = s.done(nc.gpsimd.dma_start(qn[:, 1, :], I["k_norm_b"][0].partition_broadcast(P)))

    ready = []
    for w, (name, who) in enumerate((("x", 0), ("ctx", 1))):
        rows, arrived, slot = c.load(I[name][0].rearrange("(t p) d -> p t d", p=P), NT, D)
        m = c.layer_norm_rows(lambda t: rows[:, t, :], lambda t: rows[:, t, :], arrived)
        A.wait(c.m_mod)
        ready += c.turn(lambda k, t: rows[:, t, k * P:(k + 1) * P], lambda k: hT[:, k, w * SEQ:(w + 1) * SEQ],
                        KD, NT, m, gain=lambda k: c.mod[:, 0, 16 + k, who:who + 1],
                        shift=lambda k: c.mod[:, 0, k, who:who + 1])
        c.release(slot, PE.last())

    W = I["w_in_attn"][0]
    lhs = lambda k, t: hT[:, k, t * P:(t + 1) * P]

    def z(n0, n1, tiles, dst):
        c.linear_rows(W, n0, n1, lhs, tiles, ready,
                      lambda t, n, w, ps, r: [c.evac(dst(t, n - n0, w), ps, r)])

    o_kv = Q_LORA
    o_pe = o_kv + KV_LORA
    o_qb = o_pe + ROPE_A
    o_kb = o_qb + 1024
    o_g = o_kb + 512
    z(o_kv, o_pe, range(4), lambda t, n, w: ckv[:, t, n:n + w])
    z(o_pe, o_qb, range(4), lambda t, n, w: kpe[:, t, n:n + w])
    z(0, Q_LORA, range(2), lambda t, n, w: cq[:, t, n:n + w])
    z(o_qb, o_kb, range(2), lambda t, n, w: qb[:, t, n:n + w])
    def kv_b(t, n, w, ps, r):
        return [c.evac(kb[:, t, :], ps[:, 0:256], r), c.evac(vb[:, t, :], ps[:, 256:512], r, same=True)]
    c.linear_rows(W, o_kb, o_g, lhs, range(4), ready, kv_b)
    m_z = [V.last(), A.last()]

    junk = qa[:, 0, 0:1024]
    A.wait(m_z)
    V.wait(m_z, m_qn)
    for t in range(NT):
        A.wait(A.done(nc.scalar.activation(junk[:, 0:Q_LORA], cq[:, t, :], ACT.Square, accum_out=c.st[:, 24 + t:25 + t])))
    for t in range(4):
        A.wait(A.done(nc.scalar.activation(junk[:, 0:KV_LORA], ckv[:, t, :], ACT.Square, accum_out=c.st[:, 28 + t:29 + t])))
    m = A.last()
    c.rstd(c.st[:, 0:2], c.st[:, 24:26], m, 1.0 / Q_LORA, (c.st[:, 8:10], c.st[:, 16:18]))
    c.rstd(c.st[:, 2:6], c.st[:, 28:32], m, 1.0 / KV_LORA, (c.st[:, 10:14], c.st[:, 18:22]))
    for t in range(NT):
        V.done(nc.vector.tensor_scalar(cq[:, t, :], cq[:, t, :], c.st[:, t:t + 1], None, ALU.mult))
    for t in range(4):
        V.done(nc.vector.tensor_scalar(ckv[:, t, :], ckv[:, t, :], c.st[:, 2 + t:3 + t], None, ALU.mult))
    m_low = V.last()
    sq = qa[:, 1, 0:1024].rearrange("p (h d) -> p h d", h=8)
    V.wait(m_low)
    for t in range(NT):
        x = qb[:, t, :].rearrange("p (h d) -> p h d", h=8)
        V.wait(V.done(nc.vector.tensor_tensor(sq, x, x, ALU.mult)))
        V.wait(V.done(nc.vector.tensor_reduce(ss[:, 0, t * 8:t * 8 + 8], sq, AX_X, ALU.add)))
    for t in range(4):
        x = kb[:, t, :].rearrange("p (h d) -> p h d", h=2)
        V.wait(V.done(nc.vector.tensor_tensor(sq[:, 0:2, :], x, x, ALU.mult)))
        m = V.done(nc.vector.tensor_reduce(ss[:, 0, 16 + t * 2:18 + t * 2], sq[:, 0:2, :], AX_X, ALU.add))
        V.wait(m)
    c.rstd(ss[:, 1, :], ss[:, 0, :], m, 1.0 / HD, (ss[:, 2, :], ss[:, 0, :]))
    tmp = qa.rearrange("p a b -> p (a b)")
    for t in range(4):
        parts = [(kb, KV_HEADS, 1, 16 + t * 2)] + ([(qb, HEADS, 0, t * 8)] if t < NT else [])
        for x, heads, g, at in parts:
            r = ss[:, 1, at:at + heads]
            xv = x[:, t, :].rearrange("p (h d) -> p h d", h=heads)
            V.wait(V.done(nc.vector.tensor_tensor(xv, xv, r.unsqueeze(2).broadcast_to([P, heads, HD]), ALU.mult)))
            V.wait(V.done(nc.vector.tensor_tensor(xv, xv, qn[:, g, :].unsqueeze(1).broadcast_to([P, heads, HD]), ALU.mult)))
            if t < NT:
                rope_rows(c, xv, c.rope[:, t, 64:128], c.rope[:, t, 128:192], heads, 64, tmp)
    for t in range(NT):
        rope_rows(c, kpe[:, t:t + 1, :], c.rope[:, t, 0:32], c.rope[:, t, 32:64], 1, 32, tmp)
    m_rope = V.last()

    def evac_gate(j, cnt, ps, ready):
        A.wait(ready)
        return [A.done(nc.scalar.activation(gT[:, j:j + cnt, :], ps.rearrange("p (a b) -> p a b", b=SEQ), ACT.Silu))]

    c.linear_cols(W, o_g, o_g + D, lambda k: hT[:, k, 0:SEQ], SEQ, ready, evac_gate)
    c.turn(lambda k, t: cq[:, t, k * P:(k + 1) * P], lambda k: cqT[:, k, :], 6, NT, m_rope,
           gain=lambda k: c.col("q_lora", k))
    c.turn(lambda k, t: ckv[:, t, k * P:(k + 1) * P], lambda k: ckvT[:, k, :], 4, 4, m_rope,
           gain=lambda k: c.col("kv_lora", k))
    c.turn(lambda k, t: qb[:, t, k * P:(k + 1) * P], lambda k: qbT[:, k, :], 8, NT, m_rope)
    c.turn(lambda k, t: kb[:, t, k * P:(k + 1) * P], lambda k: kbT[:, k, :], 2, 4, m_rope)
    m_T = c.turn(lambda k, t: kpe[:, t, :], lambda k: kpeT[0:64, :], 1, 4, m_rope)
    c.barrier()
    kaT = c.at(0, HEADS, 2 * SEQ)
    va = c.at(4 * K1, 4, HEADS * HD)
    qT = c.at(12 * K1, HEADS, SEQ)
    qpeT = c.at(14 * K1, HEADS, SEQ)

    c.linear_rows(I["wq_b"][0], 0, HEADS * 192, lambda k, t: cqT[:, k, t * P:(t + 1) * P], range(NT), m_T,
                  lambda t, n, w, ps, r: [c.evac(qa[:, t, n:n + w], ps, r)], kc=6)
    m_qa = [V.last(), A.last()]
    Wkv = I["wkv_b"][0]
    for half in range(2):
        wt, arrived, slot = c.load(Wkv[:, half * 1024:(half + 1) * 1024].rearrange("(k p) n -> p k n", p=P), 4, 1024)
        wh = wt.rearrange("p k (h d) -> p k h d", h=4)
        PE.wait(arrived)
        for h in range(4):
            i = c.lin.take()
            PE.wait(c.lin.free[i])
            for k in range(4):
                mm = nc.tensor.matmul(c.lin.banks[i][:, :], wh[:, k, h, 0:HD], ckvT[:, k, :], start=(k == 0), stop=(k == 3))
            m = PE.done(mm)
            c.lin.free[i] = [c.evac(kaT[:, half * 4 + h, :], c.lin.banks[i][:, :], m)]
        for t in range(4):
            i = c.lin.take()
            PE.wait(c.lin.free[i])
            for k in range(4):
                mm = nc.tensor.matmul(c.lin.banks[i][:, :].rearrange("p (h d) -> p h d", h=4),
                                      ckvT[:, k, t * P:(t + 1) * P], wh[:, k, :, HD:2 * HD], start=(k == 0), stop=(k == 3))
            m = PE.done(mm)
            c.lin.free[i] = [c.evac(va[:, t, half * 512:(half + 1) * 512], c.lin.banks[i][:, :], m)]
        c.release(slot, m)
    V.wait(m_qa)
    tmp = c.diag[:, :, :].rearrange("p a b -> p (a b)")
    tmp2 = c.at(16 * K1 + 512, 1024)
    for t in range(NT):
        qv = qa[:, t, :].rearrange("p (h d) -> p h d", h=HEADS)[:, :, HD:]
        m = rope_rows(c, qv, c.rope[:, t, 0:32], c.rope[:, t, 32:64], HEADS, 32, tmp2)
    c.turn(lambda k, t: qa[:, t, k * 192:k * 192 + HD], lambda k: qT[:, k, :], 8, NT, m)
    m_q = c.turn(lambda k, t: qa[:, t, k * 192 + HD:(k + 1) * 192], lambda k: qpeT[0:64, k, :], 8, NT, m)
    m_q += [V.last(), A.last()]
    c.barrier()
    prob = c.at(base, 2, NT, 512)
    probT = c.at(base + 2048, 2, 4, SEQ)
    sm = c.sb("softmax_tmp", [P, 16, 8])

    def scores(h):
        out = []
        for t in range(NT):
            i = c.lin.take()
            PE.wait(c.lin.free[i])
            q = slice(t * P, (t + 1) * P)
            bank = c.lin.banks[i]
            if h < HEADS:
                nc.tensor.matmul(bank[:, :], qT[:, h, q], kaT[:, h, :], start=True, stop=False)
                mm = nc.tensor.matmul(bank[:, :], qpeT[0:64, h, q], kpeT[0:64, :], start=False, stop=True)
            else:
                mm = nc.tensor.matmul(bank[:, :], qbT[:, h - HEADS, q], kbT[:, (h - HEADS) // 4, :], start=True, stop=True)
            out.append((i, PE.done(mm)))
        return out

    pT_read = [None, None]
    p_read = [None, None]

    def soft(h, banks):
        A.wait(p_read[h % 2])
        marks = []
        for t, (i, m) in enumerate(banks):
            mp, me = softmax_rows(c, c.lin.banks[i][:, :], m, A_SCALE if h < HEADS else B_SCALE,
                                  prob[:, h % 2, t, :], 512, sm[:, (h % 4) * 2 + t, :])
            c.lin.free[i] = [me]
            marks.append(mp)
        return marks

    def mix(h, m_p):
        for t in range(NT):
            i = c.aux.take()
            PE.wait(c.aux.free[i], m_p[t])
            for k in range(4):
                mm = nc.tensor.transpose(c.aux.banks[i][:, k * P:(k + 1) * P], prob[:, h % 2, t, k * P:(k + 1) * P], c.ident[:, :])
            m = PE.done(mm)
            if t == 0:
                V.wait(pT_read[h % 2])
                A.wait(pT_read[h % 2])
            e = c.evac(probT[:, h % 2, :, t * P:(t + 1) * P], c.aux.banks[i][:, :].rearrange("p (k q) -> p k q", k=4), m)
            c.aux.free[i] = [e]
            PE.wait(e)
        p_read[h % 2] = m
        i = c.aux.take()
        PE.wait(c.aux.free[i])
        for k in range(4):
            v = va[:, k, h * HD:(h + 1) * HD] if h < HEADS else vb[:, k, (h - HEADS) // 4 * HD:((h - HEADS) // 4 + 1) * HD]
            mm = nc.tensor.matmul(c.aux.banks[i][:, 0:SEQ], v, probT[:, h % 2, k, :], start=(k == 0), stop=(k == 3))
        m = PE.done(mm)
        pT_read[h % 2] = m
        V.wait(m)
        c.aux.free[i] = [V.done(nc.vector.tensor_tensor(gT[:, h, :], gT[:, h, :], c.aux.banks[i][:, 0:SEQ], ALU.mult))]

    m_p = soft(0, scores(0))
    for h in range(2 * HEADS):
        nxt = scores(h + 1) if h + 1 < 2 * HEADS else None
        nxt = soft(h + 1, nxt) if nxt else None
        mix(h, m_p)
        m_p = nxt
    c.barrier()
    return gT


def gated_residual(c, W, lhs, lhs_ready, gate_row, H, x, x_ready, kc=8):
    nc, V = c.nc, c.V
    V.wait(x_ready)

    def evac(t, n, w, ps, r):
        V.wait(r)
        u = c.evac_tmp[:, c.tmp_at, :]
        c.tmp_at ^= 1
        m = V.done(nc.vector.tensor_tensor(u, ps, gate_row[:, n:n + w], ALU.mult))
        V.wait(m)
        m2 = V.done(nc.vector.scalar_tensor_tensor(out=H[:, t, n:n + w], in0=x[:, t, n:n + w], scalar=ALPHA,
                                              in1=u, op0=ALU.mult, op1=ALU.add))
        return [m]

    c.linear_rows(W, 0, D, lhs, range(NT), lhs_ready, evac, kc=kc)
    V.wait(V.last())
    return V.last()


def stage_attention_out(c, I, gT):
    nc = c.nc
    H = c.at(0, NT, D)
    gate_row = c.at(4096, D)
    c.evac_tmp = c.sb("evac_tmp", [P, 2, 512])
    c.tmp_at = 0
    m_gate = c.spread_column(c.mod[:, 0, 32:48, 0], gate_row, c.m_mod)
    x, arrived, slot = c.load(I["x"][0].rearrange("(t p) d -> p t d", p=P), NT, D)
    m = gated_residual(c, I["w_out_attn"][0], lambda k, t: gT[:, k, t * P:(t + 1) * P], c.V.last(), gate_row,
                       H, x, [arrived, m_gate])
    c.release(slot, m)
    post_norm(c, H, gate_row, load_gb(c, I, 0), None, m)
    return H


def stage_fourier(c, I, H):
    nc, PE, V, A = c.nc, c.PE, c.V, c.A
    K1 = 1024
    xn = c.at(4 * K1, NT, D)
    hT = c.at(8 * K1, KD, SEQ)
    u = c.at(12 * K1, NT, C_WIDTH)
    yT = c.at(20 * K1, C_WIDTH // P, SEQ)
    dft = c.at(28 * K1, NT, 512)
    ndft = c.at(29 * K1, NT, 256)
    s = DmaSem(c.sem("dft_loaded"))
    s.done(nc.gpsimd.dma_start(dft, I["dft"].rearrange("(t p) n -> p t n", p=P)))
    m_dft = s.done(nc.gpsimd.dma_start(ndft, I["ndft"].rearrange("(t p) n -> p t n", p=P)))
    m = c.layer_norm_rows(lambda t: H[:, t, :], lambda t: xn[:, t, :], V.last())
    m_h = c.turn(lambda k, t: xn[:, t, k * P:(k + 1) * P], lambda k: hT[:, k, :], KD, NT, m,
                 gain=lambda k: c.mod[:, 1, 16 + k, 0:1], shift=lambda k: c.mod[:, 1, k, 0:1])
    W = I["w_in_fourier"][0]
    c.linear_rows(W, 0, C_WIDTH, lambda k, t: hT[:, k, t * P:(t + 1) * P], range(NT), m_h,
                  lambda t, n, w, ps, r: [c.evac(u[:, t, n:n + w], ps, r)])
    m_u = [V.last(), A.last()]

    def evac_gate(j, cnt, ps, ready):
        A.wait(ready)
        return [A.done(nc.scalar.activation(yT[:, j:j + cnt, :], ps.rearrange("p (a b) -> p a b", b=SEQ), ACT.Silu))]

    c.linear_cols(W, C_WIDTH, 2 * C_WIDTH, lambda k: hT[:, k, :], SEQ, m_h, evac_gate)
    V.wait(A.last())
    c.barrier()
    AB = c.at(4 * K1, 2, 2, 512)
    ab_read = [None, None]
    PE.wait(m_dft, m_u)
    for g in range(C_GROUPS):
        par = g % 2
        marks = []
        for ch in range(2):
            i = c.lin.take()
            PE.wait(c.lin.free[i])
            o = g * C_DIM + ch * P
            for t in range(NT):
                mm = nc.tensor.matmul(c.lin.banks[i][:, :], u[:, t, o:o + P], dft[:, t, :], start=(t == 0), stop=(t == NT - 1))
            m = PE.done(mm)
            V.wait(ab_read[par])
            A.wait(ab_read[par])
            e = c.evac(AB[:, par, ch, :], c.lin.banks[i][:, :], m)
            c.lin.free[i] = [e]
            marks.append(e)
        PE.wait(marks)
        i = c.aux.take()
        PE.wait(c.aux.free[i])
        for co in range(2):
            q = slice(co * P, (co + 1) * P)
            for ch in range(2):
                nc.tensor.matmul(c.aux.banks[i][:, co * SEQ:(co + 1) * SEQ], dft[:, ch, q], AB[:, par, ch, 0:SEQ],
                                 start=(ch == 0), stop=False)
            for ch in range(2):
                mm = nc.tensor.matmul(c.aux.banks[i][:, co * SEQ:(co + 1) * SEQ], ndft[:, ch, q],
                                      AB[:, par, ch, SEQ:2 * SEQ], start=False, stop=(ch == 1))
        m = PE.done(mm)
        ab_read[par] = m
        V.wait(m)
        y = yT[:, 2 * g:2 * g + 2, :]
        c.aux.free[i] = [V.done(nc.vector.tensor_tensor(y, y, c.aux.banks[i][:, :].rearrange("p (a b) -> p a b", b=SEQ), ALU.mult))]
    m_y = V.last()
    c.barrier()
    gate_row = c.at(4 * K1, D)
    m_gate = c.spread_column(c.mod[:, 1, 32:48, 0], gate_row, None)
    m = gated_residual(c, I["w_out_fourier"][0], lambda k, t: yT[:, k, t * P:(t + 1) * P], m_y, gate_row, H, H, m_gate)
    post_norm(c, H, gate_row, load_gb(c, I, 1), None, m)
    c.barrier()


def column_sums(c, x, nk, square, ready, tmp):
    nc, PE, G = c.nc, c.PE, c.G
    i = c.aux.take()
    if square:
        G.wait(ready)
        ready = G.done(nc.gpsimd.tensor_tensor(tmp, x, x, ALU.mult))
        x = tmp
    PE.wait(ready, c.aux.free[i])
    for k in range(nk):
        mm = nc.tensor.matmul(c.aux.banks[i][:, 0:SEQ], c.ones[:, :], x[:, k, :], start=(k == 0), stop=(k == nk - 1))
    return i, PE.done(mm)


def stage_mixer(c, I, dr, H):
    nc, PE, V, A, G = c.nc, c.PE, c.V, c.A, c.G
    K1 = 1024
    NC = D_CONV // P
    PAD = TAPS - 1
    uT = c.at(4 * K1, NC, SEQ)
    cpad = c.at(6 * K1, NC, SEQ + PAD)
    convT = c.at(9 * K1, NC, SEQ)
    ysT = c.at(11 * K1, NC, SEQ)
    hn = c.at(13 * K1, NT, D)
    hT = c.at(17 * K1, KD, SEQ)
    aT = c.at(21 * K1, NC, SEQ)
    gT = c.at(23 * K1, NC, SEQ)
    m = c.rms_rows(lambda t: H[:, t, :], lambda t: hn[:, t, :], V.last(), aT.rearrange("p a b -> p (a b)"))
    m_h = c.turn(lambda k, t: hn[:, t, k * P:(k + 1) * P], lambda k: hT[:, k, :], KD, NT, m,
                 gain=lambda k: c.col("mix_g", k))
    m_zero = V.done(nc.vector.memset(cpad[:, :, 0:PAD], 0.0))
    W = I["w_in_2"][0]

    def to(dst):
        return lambda j, cnt, ps, r: [c.evac(dst[:, j:j + cnt, :], ps.rearrange("p (a b) -> p a b", b=SEQ), r)]

    def to_sigmoid(j, cnt, ps, r):
        A.wait(r)
        return [A.done(nc.scalar.activation(gT[:, j:j + cnt, :], ps.rearrange("p (a b) -> p a b", b=SEQ), ACT.Sigmoid))]

    rhs = lambda k: hT[:, k, :]
    c.linear_cols(W, 2 * D_CONV, 3 * D_CONV, rhs, SEQ, m_h, to(uT))
    m_u = [V.last(), A.last()]
    c.linear_cols(W, 0, D_CONV, rhs, SEQ, m_h, to(aT))
    c.linear_cols(W, D_CONV, 2 * D_CONV, rhs, SEQ, m_h, to_sigmoid)
    V.wait(V.last(), A.last())
    m_c = V.done(nc.vector.tensor_tensor(cpad[:, :, PAD:], aT, gT, ALU.mult))
    c.barrier()

    o = 13 * K1
    a, b, t1, t2, t3, t4 = (c.at(o + 2 * K1 * i, S_BATCH, SEQ) for i in range(6))
    pre = c.at(o + 12 * K1, 4, 512)
    tabs, arrived, slot_t = c.load(I["s5_b"].rearrange("(k p) n -> p k n", p=P), 8, 256)
    m_tab = arrived
    C = c.at(o + 4 * K1, 2, S_TILES, 32)
    CK = c.at(27 * K1, 2, S_TILES, 32)
    s = DmaSem(c.sem("s5_c_loaded"))
    m_c_in = s.done(nc.gpsimd.dma_start(C.rearrange("p a b h -> p (a b h)"), I["s5_c"]))
    V.wait(m_c_in)
    kr = c.kap[:, 0, :].unsqueeze(2).broadcast_to([P, S_TILES, 32])
    ki = c.kap[:, 1, :].unsqueeze(2).broadcast_to([P, S_TILES, 32])
    x = c.at(o, 2, S_TILES, 32)
    V.done(nc.vector.tensor_tensor(CK[:, 0], C[:, 0], kr, ALU.mult))
    V.done(nc.vector.tensor_tensor(x[:, 0], C[:, 1], ki, ALU.mult))
    V.done(nc.vector.tensor_tensor(CK[:, 1], C[:, 0], ki, ALU.mult))
    V.wait(V.done(nc.vector.tensor_tensor(x[:, 1], C[:, 1], kr, ALU.mult)))
    V.done(nc.vector.tensor_tensor(CK[:, 0], CK[:, 0], x[:, 0], ALU.subtract))
    V.wait(V.done(nc.vector.tensor_tensor(CK[:, 1], CK[:, 1], x[:, 1], ALU.add)))
    m_ck = V.done(nc.vector.tensor_scalar(CK[:, 1], CK[:, 1], -1.0, None, ALU.mult))
    V.wait(m_ck)

    dg = c.sb("conv_diag", [P, 4, P])
    dg_read = [None] * 4
    PE.wait(m_c, m_zero)

    def conv_tile(k):
        i = c.aux.take()
        PE.wait(c.aux.free[i])
        for tap in range(TAPS):
            q = tap % 4
            A.wait(dg_read[q])
            m = A.done(nc.scalar.activation(dg[:, q, :], c.ident[:, :], ACT.Copy,
                                            scale=c.col("conv_w", k * TAPS + tap)))
            PE.wait(m)
            mm = nc.tensor.matmul(c.aux.banks[i][:, 0:SEQ], dg[:, q, :], cpad[:, k, tap:tap + SEQ],
                                  start=(tap == 0), stop=(tap == TAPS - 1))
            dg_read[q] = PE.done(mm)
        A.wait(dg_read[q])
        c.aux.free[i] = [A.done(nc.scalar.activation(convT[:, k, :], c.aux.banks[i][:, 0:SEQ], ACT.Identity,
                                                     bias=c.col("conv_b", k)))]

    states_read = None
    pool_done = None
    for bt in range(S_TILES // S_BATCH):
        E, m_e, slot_e = c.load(dr["phase"][bt], 2 * S_BATCH, SEQ, after=c.phases_stored)
        V.wait(m_e, states_read, pool_done)
        G.wait(m_e, states_read)
        for jj in range(S_BATCH):
            j = bt * S_BATCH + jj
            r = slice(32 * (j % 4), 32 * (j % 4) + 32)
            i = c.lin.take()
            PE.wait(c.lin.free[i], m_tab, m_u)
            for part in range(2):
                mm = nc.tensor.matmul(c.lin.banks[i][:, part * SEQ:(part + 1) * SEQ],
                                      tabs[r, j // 4, part * P:(part + 1) * P], uT[r, j // 4, :], start=True, stop=True,
                                      skip_group_check=True)
            m = PE.done(mm)
            V.wait(m)
            bank = c.lin.banks[i][:, :].rearrange("p (a b) -> p a b", a=2)
            q = 2 * (jj % 2)
            tc = pre[:, q, :].rearrange("p (a b) -> p a b", a=2)
            ts = pre[:, q + 1, :].rearrange("p (a b) -> p a b", a=2)
            V.done(nc.vector.tensor_tensor(tc, bank, E[:, jj, :].unsqueeze(1).broadcast_to([P, 2, SEQ]), ALU.mult))
            m = V.done(nc.vector.tensor_tensor(ts, bank, E[:, S_BATCH + jj, :].unsqueeze(1).broadcast_to([P, 2, SEQ]), ALU.mult))
            c.lin.free[i] = [m]
            V.wait(m)
            V.done(nc.vector.tensor_tensor(a[:, jj, :], tc[:, 0, :], ts[:, 1, :], ALU.add))
            V.wait(V.done(nc.vector.tensor_tensor(b[:, jj, :], tc[:, 1, :], ts[:, 0, :], ALU.subtract)))
            rho = c.rho[:, j:j + 1].broadcast_to([P, SEQ])
            V.done(nc.vector.tensor_tensor_scan(t1[:, jj, :], rho, a[:, jj, :], 0.0, ALU.mult, ALU.add))
            m = V.done(nc.vector.tensor_tensor_scan(t2[:, jj, :], rho, b[:, jj, :], 0.0, ALU.mult, ALU.add))
        cosv, sinv = E[:, 0:S_BATCH, :], E[:, S_BATCH:, :]
        V.wait(m)
        G.wait(m)
        G.done(nc.gpsimd.tensor_tensor(t3, t1, sinv, ALU.mult))
        G.wait(G.done(nc.gpsimd.tensor_tensor(t4, t2, cosv, ALU.mult)))
        m_im = G.done(nc.gpsimd.tensor_tensor(t3, t3, t4, ALU.add))
        V.done(nc.vector.tensor_tensor(a, t1, cosv, ALU.mult))
        V.wait(V.done(nc.vector.tensor_tensor(b, t2, sinv, ALU.mult)))
        m_re = V.done(nc.vector.tensor_tensor(a, a, b, ALU.subtract))
        c.release(slot_e, m_re, m_im)
        pool_done = m_im
        conv_tile(2 * bt)
        PE.wait(m_ck)
        for cc in range(S_BATCH // 4):
            i = c.aux.take()
            PE.wait(c.aux.free[i], m_re, m_im)
            for q in range(4):
                jj = cc * 4 + q
                j = bt * S_BATCH + jj
                out = c.aux.banks[i][32 * q:32 * q + 32, 0:SEQ]
                nc.tensor.matmul(out, CK[:, 0, j, :], a[:, jj, :], start=True, stop=False)
                mm = nc.tensor.matmul(out, CK[:, 1, j, :], t3[:, jj, :], start=False, stop=True)
            m = PE.done(mm)
            k = bt * 2 + cc
            V.wait(m)
            m = V.done(nc.vector.scalar_tensor_tensor(out=ysT[:, k, :], in0=uT[:, k, :], scalar=c.col("ssm_d", k),
                                                      in1=c.aux.banks[i][:, 0:SEQ], op0=ALU.mult, op1=ALU.add))
            c.aux.free[i] = [m]
        states_read = PE.last()
        conv_tile(2 * bt + 1)
    c.release(slot_t, PE.last())
    c.barrier()

    zT = c.at(o, NC, SEQ)
    sg = c.at(o + 2 * K1, NC, SEQ)
    tmp = c.at(o + 4 * K1, NC, SEQ)
    cen = c.at(o + 6 * K1, NC, SEQ)
    stat = c.at(o + 8 * K1, 6, SEQ)
    tmp2 = c.at(o + 10 * K1, NC, SEQ)
    m_z = A.done(nc.scalar.activation(zT, ysT, ACT.Gelu_apprx_tanh))

    def glu(j, cnt, ps, r):
        A.wait(r)
        return [A.done(nc.scalar.activation(sg[:, j:j + cnt, :], ps.rearrange("p (a b) -> p a b", b=SEQ), ACT.Sigmoid))]

    c.linear_cols(I["ssm_glu_w_2"][0], 0, 1024, lambda k: zT[:, k, :], SEQ, m_z, glu)
    m_sg = A.last()

    def spread(row):
        return row.unsqueeze(1).broadcast_to([P, NC, SEQ])

    i, m = column_sums(c, convT, NC, False, A.last(), None)
    V.wait(m)
    V.wait(V.done(nc.vector.tensor_scalar(stat[:, 0, :], c.aux.banks[i][:, 0:SEQ], 1.0 / D_CONV, None, ALU.mult)))
    c.aux.free[i] = [V.last()]
    m = V.done(nc.vector.tensor_tensor(cen, convT, spread(stat[:, 0, :]), ALU.subtract))
    i, m = column_sums(c, cen, NC, True, m, tmp)
    c.rstd(stat[:, 1, :], c.aux.banks[i][:, 0:SEQ], m, 1.0 / D_CONV, (stat[:, 2, :], stat[:, 3, :]))
    c.aux.free[i] = [V.last()]
    V.wait(V.done(nc.vector.tensor_tensor(cen, cen, spread(stat[:, 1, :]), ALU.mult)))
    A.wait(V.last())
    for k in range(NC):
        m = A.done(nc.scalar.activation(convT[:, k, :], cen[:, k, :], ACT.Silu, bias=c.col("conv_ln_b", k),
                                        scale=c.col("conv_ln_g", k)))
    V.wait(m_sg)
    m_ys = V.done(nc.vector.tensor_tensor(ysT, zT, sg, ALU.mult))
    for x, m_x, name, tt in ((convT, m, "grp_conv", tmp), (ysT, m_ys, "grp_ssm", tmp2)):
        i, m1 = column_sums(c, x, NC, True, m_x, tt)
        c.rstd(stat[:, 1, :], c.aux.banks[i][:, 0:SEQ], m1, 1.0 / D_CONV, (stat[:, 2, :], stat[:, 3, :]))
        c.aux.free[i] = [V.last()]
        for k in range(NC):
            V.done(nc.vector.scalar_tensor_tensor(out=x[:, k, :], in0=x[:, k, :], scalar=c.col(name, k),
                                                  in1=stat[:, 1, :], op0=ALU.mult, op1=ALU.mult))
        V.wait(V.last())
    m = V.last()
    add_product(c, I["w_out_2"][0], lambda k, t: (convT if k < NC else ysT)[:, k % NC, t * P:(t + 1) * P], m, H)


def add_product(c, W, lhs, ready, H):
    nc, V = c.nc, c.V

    def evac(t, n, w, ps, r):
        V.wait(r)
        return [V.done(nc.vector.tensor_tensor(H[:, t, n:n + w], H[:, t, n:n + w], ps, ALU.add))]

    c.linear_rows(W, 0, D, lhs, range(NT), ready, evac)
    V.wait(V.last())
    c.barrier()


def stage_memory(c, I, dr, H):
    nc, PE, V, A = c.nc, c.PE, c.V, c.A
    K1 = 1024
    hn = c.at(4 * K1, NT, D)
    hT = c.at(8 * K1, KD, SEQ)
    qT = c.at(12 * K1, KD, SEQ)
    oT = c.at(16 * K1, KD, SEQ)
    prob = c.at(20 * K1, MEM_HEADS, NT, SEQ)
    probT = c.at(22 * K1, MEM_HEADS, NT, SEQ)
    sm = c.sb("mem_softmax_tmp", [P, MEM_HEADS * NT, 4])
    m = c.rms_rows(lambda t: H[:, t, :], lambda t: hn[:, t, :], V.last(), qT.rearrange("p a b -> p (a b)")[:, 0:D])
    m_h = c.turn(lambda k, t: hn[:, t, k * P:(k + 1) * P], lambda k: hT[:, k, :], KD, NT, m,
                 gain=lambda k: c.col("mem_g", k))
    V.wait(A.last())
    A.wait(A.last())
    c.linear_cols(I["w_q_mem_2"][0], 0, D, lambda k: hT[:, k, :], SEQ, m_h,
                  lambda j, cnt, ps, r: [c.evac(qT[:, j:j + cnt, :], ps.rearrange("p (a b) -> p a b", b=SEQ), r)])
    m_q = [V.last(), A.last()]
    KT, m_k, slot_k = c.load(dr["memk"].rearrange("p a b -> p (a b)"), KD * SEQ, after=c.mem_kv_stored)
    KT = KT.rearrange("p (a b) -> p a b", b=SEQ)
    VV, m_v, slot_v = c.load(dr["memv"].rearrange("p a b -> p (a b)"), NT * D)
    VV = VV.rearrange("p (a b) -> p a b", b=D)
    PE.wait(m_q, m_k)
    KH = MEM_HD // P
    banks = []
    for h in range(MEM_HEADS):
        i = c.lin.take()
        PE.wait(c.lin.free[i])
        for t in range(NT):
            for k in range(KH):
                mm = nc.tensor.matmul(c.lin.banks[i][:, t * SEQ:(t + 1) * SEQ], qT[:, h * KH + k, t * P:(t + 1) * P],
                                      KT[:, h * KH + k, :], start=(k == 0), stop=(k == KH - 1))
        banks.append((i, PE.done(mm)))
    c.release(slot_k, PE.last())
    for h, (i, m) in enumerate(banks):
        marks = []
        for t in range(NT):
            mp, me = softmax_rows(c, c.lin.banks[i][:, t * SEQ:(t + 1) * SEQ], m, MEM_HD ** -0.5,
                                  prob[:, h, t, :], SEQ, sm[:, h * NT + t, :])
            marks.append(me)
        c.lin.free[i] = marks
        i = c.aux.take()
        PE.wait(c.aux.free[i], mp)
        for k in range(NT):
            for t in range(NT):
                mm = nc.tensor.transpose(c.aux.banks[i][:, (k * NT + t) * P:(k * NT + t + 1) * P],
                                         prob[:, h, t, k * P:(k + 1) * P], c.ident[:, :])
        m = PE.done(mm)
        e = c.evac(probT[:, h, :, :], c.aux.banks[i][:, :].rearrange("p (a b) -> p a b", a=NT), m)
        c.aux.free[i] = [e]
        PE.wait(e, m_v)
        for j in range(KH):
            if j % 2 == 0:
                i = c.aux.take()
                PE.wait(c.aux.free[i])
            d = (h * KH + j) * P
            for k in range(NT):
                mm = nc.tensor.matmul(c.aux.banks[i][:, (j % 2) * SEQ:(j % 2 + 1) * SEQ], VV[:, k, d:d + P],
                                      probT[:, h, k, :], start=(k == 0), stop=(k == NT - 1))
            if j % 2:
                m = PE.done(mm)
                c.aux.free[i] = [c.evac(oT[:, h * KH + j - 1:h * KH + j + 1, :],
                                        c.aux.banks[i][:, :].rearrange("p (a b) -> p a b", a=2), m)]
    c.release(slot_v, PE.last())
    add_product(c, I["w_o_mem_2"][0], lambda k, t: oT[:, k, t * P:(t + 1) * P], [V.last(), A.last()], H)


def top16(c, lists, vals, idx, n):
    nc, V = c.nc, c.V
    for q in range(n):
        V.done(nc.vector.max(vals(q)[:, 0:8], lists(q)))
    V.wait(V.last())
    for q in range(n):
        V.done(nc.vector.max_index(idx(q)[:, 0:8], vals(q)[:, 0:8], lists(q)))
    V.wait(V.last())
    for q in range(n):
        V.done(nc.vector.match_replace(lists(q), vals(q)[:, 0:8], lists(q), LOWEST))
    V.wait(V.last())
    for q in range(n):
        V.done(nc.vector.max(vals(q)[:, 8:16], lists(q)))
    V.wait(V.last())
    for q in range(n):
        V.done(nc.vector.max_index(idx(q)[:, 8:16], vals(q)[:, 8:16], lists(q)))
    V.wait(V.last())


def stage_experts(c, I, H, out):
    nc, PE, V, A, G = c.nc, c.PE, c.V, c.A, c.G
    K1 = 1024
    hn = c.at(4 * K1, NT, D)
    hT = c.at(8 * K1, KD, SEQ)
    qT = c.at(12 * K1, E_HEADS, SEQ)
    keys = c.at(14 * K1, E_HEADS, E_KEYS)
    m = c.rms_rows(lambda t: H[:, t, :], lambda t: hn[:, t, :], V.last(), c.at(12 * K1, D))
    A.wait(A.last())
    g_row, arrived, slot = c.load(I["norm_ffn_g_2"][0].partition_broadcast(P), D)
    V.wait(arrived)
    for t in range(NT):
        m = V.done(nc.vector.tensor_tensor(hn[:, t, :], hn[:, t, :], g_row, ALU.mult))
    V.wait(m)
    c.release(slot, m)
    m_h = c.turn(lambda k, t: hn[:, t, k * P:(k + 1) * P], lambda k: hT[:, k, :], KD, NT, m)
    V.wait(A.last())
    s = DmaSem(c.sem("keys_loaded"))
    G.wait(V.last())
    m_keys = s.done(nc.gpsimd.dma_start(keys, I["keysT"]))
    c.linear_cols(I["peer_w_q_2"][0], 0, E_HEADS * 2 * E_HALF, lambda k: hT[:, k, :], SEQ, m_h,
                  lambda j, cnt, ps, r: [c.evac(qT[:, j:j + cnt, :], ps.rearrange("p (a b) -> p a b", b=SEQ), r)])
    PE.wait(m_keys, V.last(), A.last())
    sc = c.at(15 * K1, E_HEADS * 2, E_KEYS)
    cand = c.at(17 * K1, E_HEADS, TOPK, TOPK)
    eq = c.at(19 * K1, E_HEADS, TOPK, TOPK)
    small = c.at(21 * K1, 16, 256)
    v1 = small[:, 0, :].rearrange("p (h s k) -> p h s k", h=8, s=2)
    i1 = small[:, 1, :].bitcast(U32)
    i1f = small[:, 2, :].rearrange("p (h s k) -> p h s k", h=8, s=2)
    top = small[:, 3, 0:E_SLOTS]
    pos = small[:, 4, 0:E_SLOTS].bitcast(U32)
    pi = small[:, 5, 0:E_SLOTS].bitcast(U32)
    pj = small[:, 6, 0:E_SLOTS].bitcast(U32)
    pif = small[:, 7, 0:E_SLOTS].rearrange("p (h k) -> p h k", h=8)
    pjf = small[:, 8, 0:E_SLOTS].rearrange("p (h k) -> p h k", h=8)
    e1 = small[:, 9, 0:E_SLOTS].rearrange("p (h k) -> p h k", h=8)
    e2 = small[:, 10, 0:E_SLOTS].rearrange("p (h k) -> p h k", h=8)
    idxf = small[:, 11, 0:E_SLOTS]
    hsum = small[:, 12, 0:E_HEADS]
    pair = small[:, 12, 128:144]
    g = c.sb("gates", [P, NT, E_SLOTS])
    act = c.sb("acts", [P, NT, E_SLOTS])
    idx = c.sb("experts", [P, NT, E_SLOTS], U32)
    m_idx = []
    for t in range(NT):
        scv = sc.rearrange("p (h s) n -> p h s n", s=2)
        for h0 in range(0, E_HEADS, 4):
            ids = [c.lin.take(), c.lin.take()]
            for sd, i in enumerate(ids):
                PE.wait(c.lin.free[i])
                r = slice(sd * E_HALF, (sd + 1) * E_HALF)
                for h in range(4):
                    mm = nc.tensor.matmul(c.lin.banks[i][:, h * E_KEYS:(h + 1) * E_KEYS],
                                          qT[r, h0 + h, t * P:(t + 1) * P], keys[r, h0 + h, :],
                                          start=True, stop=True, skip_group_check=True)
                m = PE.done(mm)
                V.wait(m)
                c.lin.free[i] = [V.done(nc.vector.tensor_copy(
                    scv[:, h0:h0 + 4, sd, :], c.lin.banks[i][:, :].rearrange("p (a b) -> p a b", a=4)))]
        V.wait(V.last())
        i1q = i1.rearrange("p (q k) -> p q k", k=TOPK)
        v1q = small[:, 0, :].rearrange("p (q k) -> p q k", k=TOPK)
        top16(c, lambda q: sc[:, q, :], lambda q: v1q[:, q, :], lambda q: i1q[:, q, :], 2 * E_HEADS)
        V.done(nc.vector.tensor_copy(small[:, 2, :], i1))
        V.wait(V.done(nc.vector.tensor_tensor(
            cand, v1[:, :, 0, :].unsqueeze(3).broadcast_to([P, E_HEADS, TOPK, TOPK]),
            v1[:, :, 1, :].unsqueeze(2).broadcast_to([P, E_HEADS, TOPK, TOPK]), ALU.add)))
        tv = top.rearrange("p (h k) -> p h k", h=8)
        pv = pos.rearrange("p (h k) -> p h k", h=8)
        top16(c, lambda q: cand[:, q, :, :].rearrange("p a b -> p (a b)"), lambda q: tv[:, q, :],
              lambda q: pv[:, q, :], E_HEADS)
        V.done(nc.vector.tensor_scalar(pi, pos, 4, None, ALU.logical_shift_right))
        V.wait(V.done(nc.vector.tensor_scalar(pj, pos, 15, None, ALU.bitwise_and)))
        V.done(nc.vector.tensor_copy(small[:, 7, 0:E_SLOTS], pi))
        V.wait(V.done(nc.vector.tensor_copy(small[:, 8, 0:E_SLOTS], pj)))
        iot = c.iota[:, :].unsqueeze(1).broadcast_to([P, TOPK, TOPK])
        for f, sd, e in ((pif, 0, e1), (pjf, 1, e2)):
            for h in range(E_HEADS):
                V.done(nc.vector.tensor_tensor(eq[:, h], f[:, h, :].unsqueeze(2).broadcast_to([P, TOPK, TOPK]), iot, ALU.is_equal))
            V.wait(V.last())
            V.wait(V.done(nc.vector.tensor_tensor(
                eq, eq, i1f[:, :, sd, :].unsqueeze(2).broadcast_to([P, E_HEADS, TOPK, TOPK]), ALU.mult)))
            V.wait(V.done(nc.vector.tensor_reduce(e, eq, AX_X, ALU.add)))
        V.wait(V.done(nc.vector.scalar_tensor_tensor(out=idxf, in0=small[:, 9, 0:E_SLOTS], scalar=float(E_KEYS),
                                                     in1=small[:, 10, 0:E_SLOTS], op0=ALU.mult, op1=ALU.add)))
        m = V.done(nc.vector.tensor_copy(idx[:, t, :], idxf))
        m_idx.append(m)
        gt = g[:, t, :].rearrange("p (h k) -> p h k", h=8)
        m = V.done(nc.vector.tensor_tensor(gt, tv, tv[:, :, 0:1].broadcast_to([P, E_HEADS, TOPK]), ALU.subtract))
        A.wait(m)
        m = A.done(nc.scalar.activation(g[:, t, :], g[:, t, :], ACT.Exp))
        V.wait(m)
        V.wait(V.done(nc.vector.tensor_reduce(hsum, gt, AX_X, ALU.add)))
        V.wait(V.done(nc.vector.reciprocal(hsum, hsum)))
        V.wait(V.done(nc.vector.tensor_tensor(gt, gt, hsum.unsqueeze(2).broadcast_to([P, E_HEADS, TOPK]), ALU.mult)))

    c.barrier()
    NG = 2 * RING
    bufs = [c.ring[:, i // 2, (i % 2) * D:(i % 2 + 1) * D] for i in range(NG)]
    gsem = [DmaSem(c.sem(f"gather{i}")) for i in range(NG)]
    read = [None] * NG
    for i in range(RING):
        read[2 * i] = read[2 * i + 1] = c.ring_free[i]
    junk = c.at(8 * K1, D)
    n = 0
    store = DmaSem(c.sem("out_stored"))
    f_row = c.at(12 * K1, D)
    s = DmaSem(c.sem("final_g_loaded"))
    m_f = s.done(nc.sync.dma_start(f_row, I["final_norm_g_2"].partition_broadcast(P))) if c.S.wait(V.last(), A.last(), PE.last()) is None else None
    U, VT = I["peer_u_2"][0], I["peer_v_2"][0]
    for t in range(NT):
        G.wait(m_idx[t])
        for table in (U, VT):
            for k in range(E_SLOTS):
                q = n % NG
                n += 1
                G.wait(read[q])
                m = gsem[q].done(nc.gpsimd.indirect_dma_start(
                    bufs[q], None, table, bass.IndirectOffsetOnAxis(ap=idx[:, t, k:k + 1], axis=0)))
                V.wait(m)
                if table is U:
                    m = V.done(nc.vector.tensor_tensor_reduce(
                        out=junk, in0=bufs[q], in1=hn[:, t, :], scale=1.0, scalar=0.0, op0=ALU.mult, op1=ALU.add,
                        accum_out=act[:, t, k:k + 1]))
                else:
                    m = V.done(nc.vector.scalar_tensor_tensor(
                        out=H[:, t, :], in0=bufs[q], scalar=act[:, t, k:k + 1], in1=H[:, t, :],
                        op0=ALU.mult, op1=ALU.add))
                read[q] = m
                V.wait(m)
            if table is U:
                A.wait(V.last())
                m = A.done(nc.scalar.activation(act[:, t, :], act[:, t, :], ACT.Gelu_apprx_tanh))
                V.wait(m)
                V.wait(V.done(nc.vector.tensor_tensor(act[:, t, :], act[:, t, :], g[:, t, :], ALU.mult)))
    m = c.rms_rows(lambda t: H[:, t, :], lambda t: H[:, t, :], V.last(), junk)
    V.wait(m_f)
    for t in range(NT):
        m = V.done(nc.vector.tensor_tensor(H[:, t, :], H[:, t, :], f_row, ALU.mult))
        c.S.wait(m)
        m = store.done(nc.sync.dma_start(out[0, t * P:(t + 1) * P, :], H[:, t, :]))
    c.S.wait(m)


def program(nc, I, out):
    with ExitStack() as ctx:
        dr = {
            "memk": nc.dram_tensor("mem_keys", (P, KD, SEQ), F32, kind="Internal").ap(),
            "memv": nc.dram_tensor("mem_values", (P, NT, D), F32, kind="Internal").ap(),
            "phase": nc.dram_tensor("phases", (S_TILES // S_BATCH, P, 2 * S_BATCH * SEQ), F32, kind="Internal").ap(),
        }
        dr["phase"] = dr["phase"]
        c = Core(nc, ctx)
        constants(c, I)
        stage_start(c, I, dr)
        c.V.wait(c.mem_kv_stored)
        c.A.wait(c.mem_kv_stored)
        stage_phases(c, I, dr)
        c.barrier()
        gT = stage_attention(c, I)
        H = stage_attention_out(c, I, gT)
        c.barrier()
        stage_fourier(c, I, H)
        stage_mixer(c, I, dr, H)
        stage_memory(c, I, dr, H)
        stage_experts(c, I, H, out)


def _columns(v):
    return np.ascontiguousarray(np.asarray(v).reshape(-1, P).T)


def kernel(**inputs):
    import numpy as _np
    import concourse.bacc as _bacc
    from concourse import mybir as _mybir
    from concourse.bass_utils import run_bass_kernel_spmd as _run

    X = {k: _np.asarray(v) for k, v in inputs.items()}
    f = _np.float32
    pos = _np.arange(SEQ)

    def angles(rot):
        nf = rot // 4
        inv = (f(10000.0) ** (-_np.arange(nf, dtype=f) / f(nf))).astype(f)
        return _np.concatenate([(pos // 64).astype(f)[:, None] * inv, (pos % 64).astype(f)[:, None] * inv], 1)

    aa, ab = angles(ROPE_A), angles(HD)
    rope = _np.concatenate([_np.cos(aa), _np.sin(aa), _np.cos(ab), _np.sin(ab)], 1).astype(f)
    jk = (_np.arange(256)[:, None] * _np.arange(256)[None, :]) % 256 * (2 * _np.pi / 256)
    cb = X["conv_w_2"][0].T.reshape(8, P, TAPS).transpose(1, 0, 2).reshape(P, 8 * TAPS)
    packed = {
        "cvec": _np.concatenate([_columns(X["c"]), _columns(X["c_ctx"])], 1),
        "ada_b0": _columns(X["ada_b"][0]), "ada_b1": _columns(X["ada_b"][1]),
        "q_lora": _columns(X["q_lora_norm"]), "kv_lora": _columns(X["kv_lora_norm"]),
        "mix_g": _columns(X["norm_mix_g_2"]), "conv_b": _columns(X["conv_b_2"]),
        "conv_ln_g": _columns(X["conv_ln_g_2"]), "conv_ln_b": _columns(X["conv_ln_b_2"]),
        "grp_conv": _columns(X["grp_norm_conv_g_2"]), "grp_ssm": _columns(X["grp_norm_ssm_g_2"]),
        "ssm_d": _columns(X["ssm_d_2"]), "mem_g": _columns(X["norm_mem_g_2"]),
        "memn_g": _columns(X["mem_norm_g_2"]), "conv_w": cb,
        "lam_re": _columns(X["ssm_lam_re_2"]), "lam_im": _columns(X["ssm_lam_im_2"]),
        "log_dt": _columns(_np.repeat(X["ssm_log_dt_2"][0], S_STATE)),
    }
    Bd = _np.zeros((S_TILES, 2, S_DIM, 2, 2, S_STATE), f)
    Cd = _np.zeros((2, S_STATE, 2, S_TILES, 2, S_DIM), f)
    for part, s in enumerate(("re", "im")):
        b = X[f"ssm_b_{s}_2"][0].reshape(S_TILES, 2, S_STATE, S_DIM)
        cc = X[f"ssm_c_{s}_2"][0].reshape(S_TILES, 2, S_DIM, S_STATE)
        for gl in range(2):
            Bd[:, gl, :, part, gl, :] = b[:, gl].transpose(0, 2, 1)
            Cd[gl, :, part, :, gl, :] = cc[:, gl].transpose(2, 0, 1)
    arrays = {
        "colpack": _np.concatenate([packed[n] for n in COLS], 1),
        "ident": _np.eye(P, dtype=f), "ones": _np.ones((P, P), f),
        "iota": _np.tile(_np.arange(16, dtype=f), (P, 1)),
        "rope": rope.reshape(NT, P, 192).transpose(1, 0, 2),
        "dft": _np.concatenate([_np.cos(jk), _np.sin(jk)], 1).astype(f) / f(16),
        "ndft": -_np.sin(jk).astype(f) / f(16),
        "s5_b": Bd.reshape(S_TILES * 32, 2 * P),
        "s5_c": Cd.reshape(P, 2 * S_TILES * 32),
        "keysT": X["peer_keys_2"][0].transpose(1, 3, 0, 2).reshape(P, E_HEADS, E_KEYS),
    }
    for name in ("x", "ctx", "ada_w", "ln_g", "ln_b", "w_in_attn", "wq_b", "wkv_b", "q_norm_b", "k_norm_b",
                 "w_out_attn", "w_in_fourier", "w_out_fourier", "mem_2", "w_in_2", "ssm_glu_w_2", "w_out_2",
                 "w_q_mem_2", "w_kv_mem_2", "w_o_mem_2", "norm_ffn_g_2", "peer_w_q_2", "peer_u_2", "peer_v_2",
                 "final_norm_g_2"):
        arrays[name] = X[name]
    nc = _bacc.Bacc("TRN2", target_bir_lowering=False, num_devices=1)
    in_map, I = {}, {}
    for name, a in arrays.items():
        a = _np.ascontiguousarray(a)
        in_map[f"in_{name}"] = a
        I[name] = nc.dram_tensor(f"in_{name}", a.shape, _mybir.dt.from_np(a.dtype), kind="ExternalInput").ap()
    out = nc.dram_tensor("out_0", (1, SEQ, D), F32, kind="ExternalOutput").ap()
    program(nc, I, out)
    r = _run(nc, [in_map], core_ids=[0])
    return r.results[0]["out_0"]
```

```python
from contextlib import ExitStack

import numpy as np
import concourse.bass as bass
from concourse import mybir

F32 = mybir.dt.float32
U32 = mybir.dt.uint32
ACT = mybir.ActivationFunctionType
ALU = mybir.AluOpType
AX_X = mybir.AxisListType.X

P = 128
D = 2048
KD = D // P
SEQ = 256
NT = SEQ // P
EPS = 1e-6
ALPHA = (2.0 * 2) ** 0.25

Q_LORA, KV_LORA, ROPE_A, HEADS, HD = 768, 512, 64, 8, 128
KV_HEADS = 2
A_SCALE = (HD + ROPE_A) ** -0.5
B_SCALE = HD ** -0.5
C_WIDTH, C_GROUPS, C_DIM = 4096, 16, 256

D_CONV, TAPS = 1024, 31
S_GROUPS, S_DIM, S_STATE = 64, 16, 64
S_TILES = S_GROUPS * S_STATE // P
S_BATCH = 4
PH_TILES = 2
MEM_HEADS, MEM_HD = 4, 512
E_HEADS, E_KEYS, E_HALF, TOPK = 8, 128, 64, 16
E_SLOTS = E_HEADS * TOPK

SLOT = 4096
RING = 4
ARENA = 30 * 1024
LOWEST = -3.0e38

COLS = {}
_n = 0
for _name, _w in [("cvec", 32), ("ada_b0", 48), ("ada_b1", 48), ("q_lora", 6), ("kv_lora", 4), ("mix_g", 16),
                  ("conv_b", 8), ("conv_ln_g", 8), ("conv_ln_b", 8), ("grp_conv", 8), ("grp_ssm", 8),
                  ("ssm_d", 8), ("mem_g", 16), ("memn_g", 16), ("conv_w", 8 * TAPS),
                  ("lam_re", S_TILES), ("lam_im", S_TILES), ("log_dt", S_TILES)]:
    COLS[_name] = (_n, _w)
    _n += _w
NCOLS = _n


class Engine:

    def __init__(self, eng, sem):
        self.eng, self.sem, self.count, self.seen = eng, sem, 0, {}

    def wait(self, *marks):
        for m in marks:
            if m is None:
                continue
            if isinstance(m, list):
                self.wait(*m)
                continue
            sem, value = m
            if self.seen.get(sem.name, 0) < value:
                self.eng.wait_ge(sem, value)
                self.seen[sem.name] = value

    def done(self, ins):
        self.count += 1
        ins.then_inc(self.sem, 1)
        return (self.sem, self.count)

    def last(self):
        return (self.sem, self.count) if self.count else None


class DmaSem:

    def __init__(self, sem):
        self.sem, self.count = sem, 0

    def done(self, ins):
        self.count += 16
        ins.then_inc(self.sem, 16)
        return (self.sem, self.count)


class Banks:

    def __init__(self, banks):
        self.banks, self.free, self.at = banks, [None] * len(banks), 0

    def take(self):
        i = self.at
        self.at = (i + 1) % len(self.banks)
        return i


class Core:
    def __init__(self, nc, ctx):
        self.nc, self.ctx = nc, ctx
        self.PE = Engine(nc.tensor, self.sem("pe_done"))
        self.V = Engine(nc.vector, self.sem("dve_done"))
        self.A = Engine(nc.scalar, self.sem("act_done"))
        self.G = Engine(nc.gpsimd, self.sem("pool_done"))
        self.S = Engine(nc.sync, self.sem("sp_done"))
        self.ring = self.sb("ring", [P, RING, SLOT])
        self.ring_sems = [DmaSem(self.sem(f"ring_slot{i}")) for i in range(RING)]
        self.ring_free = [None] * RING
        self.ring_at = 0
        self.ring_held = [False] * RING
        self.arena = self.sb("arena", [P, ARENA])
        self.lin = Banks([self.ps(f"lin{i}") for i in range(4)])
        self.aux = Banks([self.ps(f"aux{i}") for i in range(4)])
        self.flip = 0
        self.background = []
        self.steps = 1
        self.owed = 0.0

    def step(self, n=None):
        if n is None:
            self.owed += self.steps
            n = int(self.owed)
            self.owed -= n
            if not n:
                return
        left = n or -1
        while self.background and left:
            if next(self.background[0], None) is None:
                self.background.pop(0)
            else:
                left -= 1

    def sem(self, name):
        return self.ctx.enter_context(self.nc.semaphore(name))

    def sb(self, name, shape, dt=F32):
        return self.ctx.enter_context(self.nc.sbuf_tensor(name, shape, dt))

    def ps(self, name):
        return self.ctx.enter_context(self.nc.psum_tensor(name, [P, 512], F32))

    def at(self, first, *shape):
        n = 1
        for s in shape:
            n *= s
        assert first + n <= ARENA, (first, shape)
        ap = self.arena[:, first:first + n]
        if len(shape) == 2:
            return ap.rearrange("p (a b) -> p a b", a=shape[0])
        if len(shape) == 3:
            return ap.rearrange("p (a b c) -> p a b c", a=shape[0], b=shape[1])
        return ap

    def barrier(self, pool=False):
        engines = (self.PE, self.V, self.A) + ((self.G,) if pool else ())
        marks = [e.last() for e in engines]
        for e in engines:
            e.wait(marks)

    def load(self, src, *shape, after=None):
        i = self.take_slot()
        n = 1
        for s in shape:
            n *= s
        ap = self.ring[:, i, 0:n]
        if len(shape) == 2:
            ap = ap.rearrange("p (a b) -> p a b", a=shape[0])
        self.S.wait(after)
        return ap, self.ring_sems[i].done(self.nc.sync.dma_start(ap, src)), i

    def take_slot(self):
        while self.ring_held[self.ring_at]:
            self.ring_at = (self.ring_at + 1) % RING
        i = self.ring_at
        self.ring_at = (i + 1) % RING
        self.ring_held[i] = True
        self.S.wait(self.ring_free[i])
        return i

    def release(self, slot, *marks):
        self.ring_free[slot] = list(marks)
        self.ring_held[slot] = False

    def evac(self, dst, src, ready, scale=None, bias=None, same=False):
        if not same:
            self.flip ^= 1
        if self.flip:
            self.V.wait(ready)
            if scale is None:
                return self.V.done(self.nc.vector.tensor_copy(dst, src))
            if bias is None:
                return self.V.done(self.nc.vector.tensor_scalar(dst, src, scale, None, ALU.mult))
            return self.V.done(self.nc.vector.tensor_scalar(dst, src, scale, bias, ALU.mult, ALU.add))
        self.A.wait(ready)
        if scale is None:
            return self.A.done(self.nc.scalar.copy(dst, src))
        if bias is None:
            return self.A.done(self.nc.scalar.activation(dst, src, ACT.Identity, scale=scale))
        return self.A.done(self.nc.scalar.activation(dst, src, ACT.Identity, bias=bias, scale=scale))

    def linear_rows(self, W, n0, n1, lhs, tiles, lhs_ready, evac, kc=8):
        nc, PE = self.nc, self.PE
        K = W.shape[0] // P
        PE.wait(lhs_ready)
        for n in range(n0, n1, 512):
            w = min(512, n1 - n)
            ids = [self.lin.take() for _ in tiles]
            for i in ids:
                PE.wait(self.lin.free[i])
            for c in range(0, K, kc):
                wt, arrived, slot = self.load(
                    W[c * P:(c + kc) * P, n:n + w].rearrange("(k p) n -> p k n", p=P), kc, w)
                PE.wait(arrived)
                for i, t in zip(ids, tiles):
                    for k in range(kc):
                        mm = nc.tensor.matmul(self.lin.banks[i][:, 0:w], lhs(c + k, t), wt[:, k, :],
                                              start=(c + k == 0), stop=(c + k == K - 1))
                    mark = PE.done(mm)
                    if c + kc == K:
                        self.lin.free[i] = evac(t, n, w, self.lin.banks[i][:, 0:w], mark)
                self.release(slot, mark)
                self.step()

    def linear_cols(self, W, n0, n1, rhs, R, rhs_ready, evac, kc=8):
        nc, PE = self.nc, self.PE
        K = W.shape[0] // P
        per = min(4, 512 // R)
        PE.wait(rhs_ready)
        for n in range(n0, n1, 512):
            w = min(512, n1 - n)
            nj = w // P
            ids = [self.lin.take() for _ in range(0, nj, per)]
            for i in ids:
                PE.wait(self.lin.free[i])
            for c in range(0, K, kc):
                wt, arrived, slot = self.load(
                    W[c * P:(c + kc) * P, n:n + w].rearrange("(k p) n -> p k n", p=P), kc, w)
                PE.wait(arrived)
                for j in range(nj):
                    i = ids[j // per]
                    out = self.lin.banks[i][:, (j % per) * R:(j % per + 1) * R]
                    for k in range(kc):
                        mm = nc.tensor.matmul(out, wt[:, k, j * P:(j + 1) * P], rhs(c + k),
                                              start=(c + k == 0 and j % per == 0), stop=(c + k == K - 1),
                                              skip_group_check=True)
                    if j % per == per - 1 or j == nj - 1:
                        mark = PE.done(mm)
                        if c + kc == K:
                            j0 = j - j % per
                            cnt = j - j0 + 1
                            self.lin.free[i] = evac((n - n0) // P + j0, cnt, self.lin.banks[i][:, 0:cnt * R], mark)
                self.release(slot, mark)
                self.step()

    def turn(self, src, dst, nk, nt, ready, gain=None, shift=None):
        nc, PE = self.nc, self.PE
        PE.wait(ready)
        kk = max(1, 4 // nt)
        for k0 in range(0, nk, kk):
            i = self.aux.take()
            PE.wait(self.aux.free[i])
            ks = range(k0, min(nk, k0 + kk))
            for k in ks:
                for t in range(nt):
                    a = src(k, t)
                    f = a.shape[1]
                    mm = nc.tensor.transpose(
                        self.aux.banks[i][0:f, ((k - k0) * nt + t) * P:((k - k0) * nt + t + 1) * P], a, self.ident[:, :])
            mark = PE.done(mm)
            free = []
            for k in ks:
                d = dst(k)
                free.append(self.evac(d, self.aux.banks[i][0:f, (k - k0) * nt * P:(k - k0 + 1) * nt * P], mark,
                                      None if gain is None else gain(k), None if shift is None else shift(k),
                                      same=k > k0))
            self.aux.free[i] = free
        return [self.V.last(), self.A.last()]

    def rstd(self, dst, src, ready, mul, tmp):
        nc, V, A = self.nc, self.V, self.A
        v, s = tmp
        V.wait(ready)
        m = V.done(nc.vector.tensor_scalar(v, src, mul, EPS, ALU.mult, ALU.add))
        A.wait(m)
        m = A.done(nc.scalar.activation(s, v, ACT.Sqrt))
        V.wait(m)
        V.wait(V.done(nc.vector.reciprocal(dst, s)))
        V.wait(V.done(nc.vector.tensor_tensor(s, dst, dst, ALU.mult)))
        V.wait(V.done(nc.vector.tensor_tensor(s, s, v, ALU.mult)))
        V.wait(V.done(nc.vector.tensor_scalar(s, s, -0.5, 1.5, ALU.mult, ALU.add)))
        m = V.done(nc.vector.tensor_tensor(dst, dst, s, ALU.mult))
        V.wait(m)
        return m

    def layer_norm_rows(self, src, dst, ready):
        nc, V = self.nc, self.V
        V.wait(ready)
        for t in range(NT):
            for j in range(4):
                m = V.done(nc.vector.bn_stats(self.bn[:, t, j, :], src(t)[:, j * 512:(j + 1) * 512]))
        V.wait(m)
        for t in range(NT):
            m = V.done(nc.vector.bn_aggr(self.mv[:, t, :], self.bn[:, t, :, :].rearrange("p a b -> p (a b)")))
        self.rstd(self.st[:, 0:NT], self.mv[:, :, 1], m, 1.0, (self.st[:, 8:8 + NT], self.st[:, 16:16 + NT]))
        for t in range(NT):
            m = V.done(nc.vector.tensor_scalar(dst(t), src(t), self.mv[:, t, 0:1], self.st[:, t:t + 1],
                                               ALU.subtract, ALU.mult))
        V.wait(m)
        return m

    def rms_rows(self, src, dst, ready, junk):
        nc, V, A = self.nc, self.V, self.A
        A.wait(ready, V.last())
        for t in range(NT):
            m = A.done(nc.scalar.activation(junk, src(t), ACT.Square, accum_out=self.st[:, 24 + t:25 + t]))
            A.wait(m)
        self.rstd(self.st[:, 0:NT], self.st[:, 24:24 + NT], m, 1.0 / D,
                  (self.st[:, 8:8 + NT], self.st[:, 16:16 + NT]))
        for t in range(NT):
            m = V.done(nc.vector.tensor_scalar(dst(t), src(t), self.st[:, t:t + 1], None, ALU.mult))
        V.wait(m)
        return m

    def spread_column(self, col, dst, ready):
        nc, PE, V = self.nc, self.PE, self.V
        for b in range(4):
            i = self.aux.take()
            V.wait(ready, PE.last())
            for j in range(4):
                m = V.done(nc.vector.tensor_scalar(self.diag[:, j, :], self.ident[:, :],
                                                   col[:, b * 4 + j:b * 4 + j + 1], None, ALU.mult))
            PE.wait(m, self.aux.free[i])
            mm = nc.tensor.matmul(self.aux.banks[i][:, :], self.ones[:, :],
                                  self.diag[:, :, :].rearrange("p a b -> p (a b)"), start=True, stop=True)
            m = PE.done(mm)
            V.wait(m)
            m = V.done(nc.vector.tensor_copy(dst[:, b * 512:(b + 1) * 512], self.aux.banks[i][:, :]))
            self.aux.free[i] = [m]
        return m

    def col(self, name, j=None):
        a, w = COLS[name]
        return self.colpack[:, a:a + w] if j is None else self.colpack[:, a + j:a + j + 1]


def constants(c, I):
    nc = c.nc
    c.ident = c.sb("ident", [P, P])
    c.ones = c.sb("ones", [P, P])
    c.diag = c.sb("diag", [P, 4, P])
    c.colpack = c.sb("colpack_sb", [P, NCOLS])
    c.rope = c.sb("rope_sb", [P, NT, 192])
    c.bn = c.sb("bn", [P, NT, 4, 6])
    c.mv = c.sb("mv", [P, NT, 2])
    c.st = c.sb("st", [P, 64])
    c.iota = c.sb("iota_sb", [P, 16])
    c.macc = c.sb("mod_sums", [P, 2, 512])
    c.cv = c.sb("silu_c", [P, 2, KD])
    c.mod = c.sb("mod", [P, 2, 48, 2])
    s = DmaSem(c.sem("constants"))
    for dst, src in ((c.ident, I["ident"]), (c.colpack, I["colpack"]), (c.iota, I["iota"]), (c.ones, I["ones"]),
                     (c.rope, I["rope"])):
        m = s.done(nc.sync.dma_start(dst[:], src))
    for e in (c.PE, c.V, c.A, c.G):
        e.wait(m)


def softmax_rows(c, psum, ready, scale, prob, n, tmp):
    nc, V, A = c.nc, c.V, c.A
    V.wait(ready)
    V.wait(V.done(nc.vector.tensor_reduce(tmp[:, 0:1], psum, AX_X, ALU.max)))
    m = V.done(nc.vector.tensor_scalar(tmp[:, 1:2], tmp[:, 0:1], -scale, None, ALU.mult))
    A.wait(m)
    m = A.done(nc.scalar.activation(prob, psum, ACT.Exp, bias=tmp[:, 1:2], scale=scale, accum_out=tmp[:, 2:3]))
    V.wait(m)
    V.wait(V.done(nc.vector.reciprocal(tmp[:, 3:4], tmp[:, 2:3])))
    return V.done(nc.vector.tensor_scalar(prob, prob, tmp[:, 3:4], None, ALU.mult)), m


def modulation(c, I, layer, blocks, who):
    nc, PE, V = c.nc, c.PE, c.V
    W = I["ada_w"][layer]
    reduced = None
    for n in blocks:
        for ch in range(2):
            wt, arrived, slot = c.load(
                W[ch * 8 * P:(ch + 1) * 8 * P, n:n + 512].rearrange("(k p) n -> p k n", p=P), 8, 512)
            V.wait(arrived)
            for k in range(8):
                kk = ch * 8 + k
                for w in range(who):
                    acc, cv = c.macc[:, w, :], c.cv[:, w, kk:kk + 1]
                    if kk == 0:
                        V.wait(reduced)
                        V.done(nc.vector.tensor_scalar(acc, wt[:, 0, :], cv, None, ALU.mult))
                    else:
                        V.wait((V.sem, V.count - who + 1))
                        V.done(nc.vector.scalar_tensor_tensor(out=acc, in0=wt[:, k, :], scalar=cv, in1=acc,
                                                              op0=ALU.mult, op1=ALU.add))
            c.release(slot, V.last())
            done = V.last()
            yield True
        i = c.aux.take()
        PE.wait(done, c.aux.free[i])
        for j in range(4):
            for w in range(who):
                mm = nc.tensor.matmul(c.aux.banks[i][:, j * who + w:j * who + w + 1],
                                      c.macc[:, w, j * P:(j + 1) * P], c.ones[:, 0:1], start=True, stop=True)
        reduced = PE.done(mm)
        V.wait(reduced)
        j = n // P
        c.m_mod = V.done(nc.vector.tensor_tensor(
            c.mod[:, layer, j:j + 4, 0:who], c.aux.banks[i][:, 0:4 * who].rearrange("p (a b) -> p a b", b=who),
            c.col("ada_b%d" % layer)[:, j:j + 4].unsqueeze(2).broadcast_to([P, 4, who]), ALU.add))
        if D <= n < 2 * D:
            V.wait(c.m_mod)
            c.m_mod = V.done(nc.vector.tensor_scalar(c.mod[:, layer, j:j + 4, 0:who], c.mod[:, layer, j:j + 4, 0:who],
                                                     1.0, None, ALU.add))
        c.aux.free[i] = [c.m_mod]
        yield True


def attention_input(c, I, name, w):
    hT = c.at(0, KD, 2 * SEQ)
    rows, arrived, slot = c.load(I[name][0].rearrange("(t p) d -> p t d", p=P), NT, D)
    m = c.layer_norm_rows(lambda t: rows[:, t, :], lambda t: rows[:, t, :], arrived)
    yield True
    c.A.wait(c.m_mod)
    for k0 in range(0, KD, 4):
        c.turn(lambda k, t: rows[:, t, (k0 + k) * P:(k0 + k + 1) * P],
               lambda k: hT[:, k0 + k, w * SEQ:(w + 1) * SEQ], 4, NT, m,
               gain=lambda k: c.mod[:, 0, 16 + k0 + k, w:w + 1], shift=lambda k: c.mod[:, 0, k0 + k, w:w + 1])
        yield True
    c.release(slot, c.PE.last())


def stage_start(c, I, dr):
    nc, PE, V, A = c.nc, c.PE, c.V, c.A
    KT = c.at(12 * 1024, KD, SEQ)
    VV = c.at(16 * 1024, NT, D)
    memT = c.at(20 * 1024, KD, SEQ)
    junk = c.at(24 * 1024, D)
    mem, arrived, slot = c.load(I["mem_2"][0].rearrange("(t p) d -> p t d", p=P), NT, D)
    V.wait(A.done(nc.scalar.activation(c.cv[:, :, :], c.col("cvec").rearrange("p (a b) -> p a b", a=2), ACT.Silu)))
    V.wait(arrived)
    m = c.rms_rows(lambda t: mem[:, t, :], lambda t: mem[:, t, :], arrived, junk)
    mT = c.turn(lambda k, t: mem[:, t, k * P:(k + 1) * P], lambda k: memT[:, k, :], KD, NT, m,
                gain=lambda k: c.col("memn_g", k))
    c.release(slot, PE.last())
    inputs = [attention_input(c, I, name, w) for w, name in enumerate(("x", "ctx"))]
    c.background = [modulation(c, I, 0, range(0, 2 * D, 512), 2)] + inputs
    c.steps = 2.2
    Wkv = I["w_kv_mem_2"][0]
    c.linear_cols(Wkv, 0, D, lambda k: memT[:, k, :], SEQ, mT,
                  lambda j, cnt, ps, r: [c.evac(KT[:, j:j + cnt, :], ps.rearrange("p (a b) -> p a b", b=SEQ), r)])
    c.linear_rows(Wkv, D, 2 * D, lambda k, t: memT[:, k, t * P:(t + 1) * P], range(NT), mT,
                  lambda t, n, w, ps, r: [c.evac(VV[:, t, n - D:n - D + w], ps, r)])
    c.step(0)
    c.background = [modulation(c, I, 0, range(2 * D, 3 * D, 512), 1), modulation(c, I, 1, range(0, 3 * D, 512), 1)]
    c.S.wait(V.last(), A.last())
    s = DmaSem(c.sem("mem_kv_stored"))
    s.done(nc.sync.dma_start(dr["memk"], KT))
    c.mem_kv_stored = s.done(nc.sync.dma_start(dr["memv"], VV))
    c.steps = 1


def stage_phases(c, I, dr):
    nc, V, A, G = c.nc, c.V, c.A, c.G
    c.rho = c.sb("rho", [P, S_TILES])
    c.kap = c.sb("kap", [P, 2, S_TILES])
    T = c.sb("phase_tmp", [P, 8, S_TILES])
    dt, x, th, cs, sn, t0, t1, t2 = (T[:, i, :] for i in range(8))
    lr, li = c.col("lam_re"), c.col("lam_im")

    def v(ins):
        m = V.done(ins)
        V.wait(m)
        return m

    vt = nc.vector.tensor_tensor
    vs = nc.vector.tensor_scalar
    A.wait(A.done(nc.scalar.activation(dt, c.col("log_dt"), ACT.Exp)))
    V.wait(A.last())
    v(vt(x, lr, dt, ALU.mult))
    m = v(vt(th, li, dt, ALU.mult))
    A.wait(m)
    m = A.done(nc.scalar.activation(c.rho[:, :], x, ACT.Exp))
    V.wait(m)
    big = 12582912.0
    two_pi = 2 * np.pi
    p1 = 6.28125
    p2 = float(np.float32(np.round((two_pi - p1) * 2 ** 22) / 2 ** 22))
    p3 = float(two_pi - p1 - p2)
    v(vs(t0, th, 1.0 / two_pi, big, ALU.mult, ALU.add))
    v(vs(t0, t0, -big, None, ALU.add))
    for part in (p1, p2, p3):
        v(nc.vector.scalar_tensor_tensor(out=th, in0=t0, scalar=-part, in1=th, op0=ALU.mult, op1=ALU.add))
    lim = 3.1415925
    m = v(vs(th, th, lim, -lim, ALU.min, ALU.max))
    A.wait(m)
    A.done(nc.scalar.activation(sn, th, ACT.Sin))
    m = A.done(nc.scalar.activation(t1, th, ACT.Sin, scale=0.5))
    V.wait(m)
    v(vt(t1, t1, t1, ALU.mult))
    v(vs(cs, t1, -2.0, 1.0, ALU.mult, ALU.add))
    v(vt(t0, c.rho[:, :], cs, ALU.mult))
    v(vs(t0, t0, -1.0, None, ALU.add))
    v(vt(t1, c.rho[:, :], sn, ALU.mult))
    kr, ki = c.kap[:, 0, :], c.kap[:, 1, :]
    v(vt(kr, t0, lr, ALU.mult))
    v(vt(t2, t1, li, ALU.mult))
    v(vt(kr, kr, t2, ALU.add))
    v(vt(ki, t1, lr, ALU.mult))
    v(vt(t2, t0, li, ALU.mult))
    v(vt(ki, ki, t2, ALU.subtract))
    v(vt(t0, lr, lr, ALU.mult))
    v(vt(t1, li, li, ALU.mult))
    v(vt(t0, t0, t1, ALU.add))
    v(nc.vector.reciprocal(t1, t0))
    v(vt(kr, kr, t1, ALU.mult))
    v(vt(ki, ki, t1, ALU.mult))
    c.phases_stored = DmaSem(c.sem("phases_stored"))
    E = c.sb("phase", [P, 2, PH_TILES, SEQ])
    tmp = c.sb("phase_products", [P, 2, PH_TILES, SEQ // 2])
    c.G.wait(V.last(), A.last())
    pt = nc.gpsimd.tensor_tensor
    stored = None

    def g(ins):
        m = G.done(ins)
        G.wait(m)
        return m

    for b in range(S_TILES // PH_TILES):
        lo, hi = b * PH_TILES, (b + 1) * PH_TILES
        G.wait(stored)
        G.done(nc.gpsimd.memset(E[:, 0, :, 0:1], 1.0))
        G.done(nc.gpsimd.memset(E[:, 1, :, 0:1], 0.0))
        G.done(nc.gpsimd.tensor_copy(E[:, 0, :, 1], cs[:, lo:hi]))
        g(nc.gpsimd.tensor_copy(E[:, 1, :, 1], sn[:, lo:hi]))
        n = 2
        cn, sq, tt, uu = t0[:, 0:PH_TILES], t0[:, 8:8 + PH_TILES], t1[:, 0:PH_TILES], t1[:, 8:8 + PH_TILES]
        while n < SEQ:
            a, d = E[:, 0, :, n - 1], E[:, 1, :, n - 1]
            G.done(pt(tt, a, cs[:, lo:hi], ALU.mult))
            g(pt(uu, d, sn[:, lo:hi], ALU.mult))
            g(pt(cn, tt, uu, ALU.subtract))
            G.done(pt(tt, a, sn[:, lo:hi], ALU.mult))
            g(pt(uu, d, cs[:, lo:hi], ALU.mult))
            g(pt(sq, tt, uu, ALU.add))
            C = cn.unsqueeze(2).broadcast_to([P, PH_TILES, n])
            S = sq.unsqueeze(2).broadcast_to([P, PH_TILES, n])
            e0, e1 = E[:, 0, :, 0:n], E[:, 1, :, 0:n]
            x0, x1 = tmp[:, 0, :, 0:n], tmp[:, 1, :, 0:n]
            G.done(pt(x0, e0, C, ALU.mult))
            g(pt(x1, e1, S, ALU.mult))
            g(pt(E[:, 0, :, n:2 * n], x0, x1, ALU.subtract))
            G.done(pt(x0, e0, S, ALU.mult))
            g(pt(x1, e1, C, ALU.mult))
            g(pt(E[:, 1, :, n:2 * n], x0, x1, ALU.add))
            n *= 2
        dst = dr["phase"][lo // S_BATCH].rearrange("p (e a x) -> p e a x", e=2, a=S_BATCH)
        stored = c.phases_stored.done(nc.gpsimd.dma_start(dst[:, :, lo % S_BATCH:lo % S_BATCH + PH_TILES, :], E[:]))
    c.phases_stored = stored


def rope_rows(c, x, cos, sin, heads, half, tmp):
    nc, V = c.nc, c.V
    xe = x.rearrange("p h (f two) -> p h f two", two=2)
    x1, x2 = xe[:, :, :, 0], xe[:, :, :, 1]
    C = cos.unsqueeze(1).broadcast_to([P, heads, half])
    S = sin.unsqueeze(1).broadcast_to([P, heads, half])
    n = heads * half
    t = [tmp[:, i * n:(i + 1) * n].rearrange("p (h f) -> p h f", h=heads) for i in range(4)]
    V.done(nc.vector.tensor_tensor(t[0], x1, C, ALU.mult))
    V.done(nc.vector.tensor_tensor(t[1], x2, S, ALU.mult))
    V.done(nc.vector.tensor_tensor(t[2], x1, S, ALU.mult))
    V.wait(V.done(nc.vector.tensor_tensor(t[3], x2, C, ALU.mult)))
    V.done(nc.vector.tensor_tensor(x1, t[0], t[1], ALU.subtract))
    m = V.done(nc.vector.tensor_tensor(x2, t[2], t[3], ALU.add))
    V.wait(m)
    return m


def post_norm(c, H, gate_row, g_slot, m_g, base_ready):
    nc, V = c.nc, c.V
    m = c.layer_norm_rows(lambda t: H[:, t, :], lambda t: H[:, t, :], base_ready)
    gb, arrived, slot = g_slot
    V.wait(arrived, m)
    for t in range(NT):
        V.done(nc.vector.tensor_tensor(H[:, t, :], H[:, t, :], gb[:, 0:D], ALU.mult))
    V.wait(V.last())
    for t in range(NT):
        V.done(nc.vector.tensor_tensor(H[:, t, :], H[:, t, :], gb[:, D:2 * D], ALU.add))
    V.wait(V.last())
    c.release(slot, V.last())
    return V.last()


def load_gb(c, I, layer):
    i = c.take_slot()
    s = c.ring_sems[i]
    s.done(c.nc.sync.dma_start(c.ring[:, i, 0:D], I["ln_g"][layer].partition_broadcast(P)))
    m = s.done(c.nc.sync.dma_start(c.ring[:, i, D:2 * D], I["ln_b"][layer].partition_broadcast(P)))
    return c.ring[:, i, :], m, i


def stage_attention(c, I):
    nc, PE, V, A = c.nc, c.PE, c.V, c.A
    K1 = 1024
    hT = c.at(0, KD, 2 * SEQ)
    gT = c.at(8 * K1, KD, SEQ)
    cq = c.at(12 * K1, NT, Q_LORA)
    qb = c.at(12 * K1 + 1536, NT, 1024)
    kb = c.at(12 * K1 + 3584, 4, 256)
    ckv = c.at(12 * K1 + 4608, 4, KV_LORA)
    vb = c.at(12 * K1 + 6656, 4, 256)
    kpe = c.at(12 * K1 + 7680, 4, ROPE_A)
    base = 20 * K1
    cqT = c.at(base, 6, SEQ)
    qa = c.at(base + 1536, NT, HEADS * 192)
    ckvT = c.at(base + 4608, 4, 2 * SEQ)
    qbT = c.at(base + 6656, HEADS, SEQ)
    kbT = c.at(base + 8704, KV_HEADS, 2 * SEQ)
    kpeT = c.at(base + 9728, 2 * SEQ)
    qn = c.sb("qk_norm", [P, 2, HD])
    ss = c.sb("head_ss", [P, 3, 24])

    s = DmaSem(c.sem("qk_norm_loaded"))
    s.done(nc.scalar.dma_start(qn[:, 0, :], I["q_norm_b"][0].partition_broadcast(P)))
    m_qn = s.done(nc.scalar.dma_start(qn[:, 1, :], I["k_norm_b"][0].partition_broadcast(P)))

    ready = [V.last(), A.last()]
    V.wait(c.mem_kv_stored)
    A.wait(c.mem_kv_stored)
    W = I["w_in_attn"][0]
    lhs = lambda k, t: hT[:, k, t * P:(t + 1) * P]

    def z(n0, n1, tiles, dst):
        c.linear_rows(W, n0, n1, lhs, tiles, ready,
                      lambda t, n, w, ps, r: [c.evac(dst(t, n - n0, w), ps, r)])

    o_kv = Q_LORA
    o_pe = o_kv + KV_LORA
    o_qb = o_pe + ROPE_A
    o_kb = o_qb + 1024
    o_g = o_kb + 512
    z(o_kv, o_pe, range(4), lambda t, n, w: ckv[:, t, n:n + w])
    z(o_pe, o_qb, range(4), lambda t, n, w: kpe[:, t, n:n + w])
    z(0, Q_LORA, range(2), lambda t, n, w: cq[:, t, n:n + w])
    z(o_qb, o_kb, range(2), lambda t, n, w: qb[:, t, n:n + w])
    def kv_b(t, n, w, ps, r):
        return [c.evac(kb[:, t, :], ps[:, 0:256], r), c.evac(vb[:, t, :], ps[:, 256:512], r, same=True)]
    c.linear_rows(W, o_kb, o_g, lhs, range(4), ready, kv_b)
    m_z = [V.last(), A.last()]

    junk = qa[:, 0, 0:1024]
    A.wait(m_z)
    V.wait(m_z, m_qn)
    for t in range(NT):
        A.wait(A.done(nc.scalar.activation(junk[:, 0:Q_LORA], cq[:, t, :], ACT.Square, accum_out=c.st[:, 24 + t:25 + t])))
    for t in range(4):
        A.wait(A.done(nc.scalar.activation(junk[:, 0:KV_LORA], ckv[:, t, :], ACT.Square, accum_out=c.st[:, 28 + t:29 + t])))
    m = A.last()
    c.rstd(c.st[:, 0:2], c.st[:, 24:26], m, 1.0 / Q_LORA, (c.st[:, 8:10], c.st[:, 16:18]))
    c.rstd(c.st[:, 2:6], c.st[:, 28:32], m, 1.0 / KV_LORA, (c.st[:, 10:14], c.st[:, 18:22]))
    for t in range(NT):
        V.done(nc.vector.tensor_scalar(cq[:, t, :], cq[:, t, :], c.st[:, t:t + 1], None, ALU.mult))
    for t in range(4):
        V.done(nc.vector.tensor_scalar(ckv[:, t, :], ckv[:, t, :], c.st[:, 2 + t:3 + t], None, ALU.mult))
    m_low = V.last()
    sq = qa[:, 1, 0:1024].rearrange("p (h d) -> p h d", h=8)
    V.wait(m_low)
    for t in range(NT):
        x = qb[:, t, :].rearrange("p (h d) -> p h d", h=8)
        V.wait(V.done(nc.vector.tensor_tensor(sq, x, x, ALU.mult)))
        V.wait(V.done(nc.vector.tensor_reduce(ss[:, 0, t * 8:t * 8 + 8], sq, AX_X, ALU.add)))
    for t in range(4):
        x = kb[:, t, :].rearrange("p (h d) -> p h d", h=2)
        V.wait(V.done(nc.vector.tensor_tensor(sq[:, 0:2, :], x, x, ALU.mult)))
        m = V.done(nc.vector.tensor_reduce(ss[:, 0, 16 + t * 2:18 + t * 2], sq[:, 0:2, :], AX_X, ALU.add))
        V.wait(m)
    c.rstd(ss[:, 1, :], ss[:, 0, :], m, 1.0 / HD, (ss[:, 2, :], ss[:, 0, :]))
    tmp = qa.rearrange("p a b -> p (a b)")
    for t in range(4):
        parts = [(kb, KV_HEADS, 1, 16 + t * 2)] + ([(qb, HEADS, 0, t * 8)] if t < NT else [])
        for x, heads, g, at in parts:
            r = ss[:, 1, at:at + heads]
            xv = x[:, t, :].rearrange("p (h d) -> p h d", h=heads)
            V.wait(V.done(nc.vector.tensor_tensor(xv, xv, r.unsqueeze(2).broadcast_to([P, heads, HD]), ALU.mult)))
            V.wait(V.done(nc.vector.tensor_tensor(xv, xv, qn[:, g, :].unsqueeze(1).broadcast_to([P, heads, HD]), ALU.mult)))
            if t < NT:
                rope_rows(c, xv, c.rope[:, t, 64:128], c.rope[:, t, 128:192], heads, 64, tmp)
    for t in range(NT):
        rope_rows(c, kpe[:, t:t + 1, :], c.rope[:, t, 0:32], c.rope[:, t, 32:64], 1, 32, tmp)
    m_rope = V.last()

    def evac_gate(j, cnt, ps, ready):
        A.wait(ready)
        return [A.done(nc.scalar.activation(gT[:, j:j + cnt, :], ps.rearrange("p (a b) -> p a b", b=SEQ), ACT.Silu))]

    def gate(n0, n1):
        c.linear_cols(W, o_g + n0, o_g + n1, lambda k: hT[:, k, 0:SEQ], SEQ, ready,
                      lambda j, cnt, ps, r: evac_gate(n0 // P + j, cnt, ps, r))

    gate(0, 1024)
    c.turn(lambda k, t: cq[:, t, k * P:(k + 1) * P], lambda k: cqT[:, k, :], 6, NT, m_rope,
           gain=lambda k: c.col("q_lora", k))
    c.turn(lambda k, t: ckv[:, t, k * P:(k + 1) * P], lambda k: ckvT[:, k, :], 4, 4, m_rope,
           gain=lambda k: c.col("kv_lora", k))
    gate(1024, 1536)
    c.turn(lambda k, t: qb[:, t, k * P:(k + 1) * P], lambda k: qbT[:, k, :], 8, NT, m_rope)
    c.turn(lambda k, t: kb[:, t, k * P:(k + 1) * P], lambda k: kbT[:, k, :], 2, 4, m_rope)
    m_T = c.turn(lambda k, t: kpe[:, t, :], lambda k: kpeT[0:64, :], 1, 4, m_rope)
    gate(1536, D)
    c.barrier()
    kaT = c.at(0, HEADS, 2 * SEQ)
    va = c.at(4 * K1, 4, HEADS * HD)
    qT = c.at(12 * K1, HEADS, SEQ)
    qpeT = c.at(14 * K1, HEADS, SEQ)

    c.linear_rows(I["wq_b"][0], 0, HEADS * 192, lambda k, t: cqT[:, k, t * P:(t + 1) * P], range(NT), m_T,
                  lambda t, n, w, ps, r: [c.evac(qa[:, t, n:n + w], ps, r)], kc=6)
    m_qa = [V.last(), A.last()]
    Wkv = I["wkv_b"][0]
    for half in range(2):
        wt, arrived, slot = c.load(Wkv[:, half * 1024:(half + 1) * 1024].rearrange("(k p) n -> p k n", p=P), 4, 1024)
        wh = wt.rearrange("p k (h d) -> p k h d", h=4)
        PE.wait(arrived)
        for h in range(4):
            i = c.lin.take()
            PE.wait(c.lin.free[i])
            for k in range(4):
                mm = nc.tensor.matmul(c.lin.banks[i][:, :], wh[:, k, h, 0:HD], ckvT[:, k, :], start=(k == 0), stop=(k == 3))
            m = PE.done(mm)
            c.lin.free[i] = [c.evac(kaT[:, half * 4 + h, :], c.lin.banks[i][:, :], m)]
        for t in range(4):
            i = c.lin.take()
            PE.wait(c.lin.free[i])
            for k in range(4):
                mm = nc.tensor.matmul(c.lin.banks[i][:, :].rearrange("p (h d) -> p h d", h=4),
                                      ckvT[:, k, t * P:(t + 1) * P], wh[:, k, :, HD:2 * HD], start=(k == 0), stop=(k == 3))
            m = PE.done(mm)
            c.lin.free[i] = [c.evac(va[:, t, half * 512:(half + 1) * 512], c.lin.banks[i][:, :], m)]
        c.release(slot, m)
    V.wait(m_qa)
    tmp = c.diag[:, :, :].rearrange("p a b -> p (a b)")
    tmp2 = c.at(16 * K1 + 512, 1024)
    for t in range(NT):
        qv = qa[:, t, :].rearrange("p (h d) -> p h d", h=HEADS)[:, :, HD:]
        m = rope_rows(c, qv, c.rope[:, t, 0:32], c.rope[:, t, 32:64], HEADS, 32, tmp2)
    c.turn(lambda k, t: qa[:, t, k * 192:k * 192 + HD], lambda k: qT[:, k, :], 8, NT, m)
    m_q = c.turn(lambda k, t: qa[:, t, k * 192 + HD:(k + 1) * 192], lambda k: qpeT[0:64, k, :], 8, NT, m)
    m_q += [V.last(), A.last()]
    c.barrier()
    prob = c.at(base, 3, NT, 512)
    probT = c.at(base + 3072, 2, 4, SEQ)
    sm = c.sb("softmax_tmp", [P, 3, NT, 4])
    probT_read = [None] * 2
    prob_read = [None] * 3
    exps = {}

    def scores(h):
        A.wait(prob_read[h % 3])
        scale = A_SCALE if h < HEADS else B_SCALE
        banks = []
        for t in range(NT):
            i = c.lin.take()
            PE.wait(c.lin.free[i])
            q = slice(t * P, (t + 1) * P)
            bank = c.lin.banks[i]
            if h < HEADS:
                nc.tensor.matmul(bank[:, :], qT[:, h, q], kaT[:, h, :], start=True, stop=False)
                mm = nc.tensor.matmul(bank[:, :], qpeT[0:64, h, q], kpeT[0:64, :], start=False, stop=True)
            else:
                mm = nc.tensor.matmul(bank[:, :], qbT[:, h - HEADS, q], kbT[:, (h - HEADS) // 4, :], start=True, stop=True)
            banks.append((i, PE.done(mm)))
        marks = []
        for t, (i, m) in enumerate(banks):
            tmp = sm[:, h % 3, t, :]
            V.wait(m)
            marks.append(V.done(nc.vector.tensor_reduce(tmp[:, 0:1], c.lin.banks[i][:, :], AX_X, ALU.max)))
        for t, (i, _) in enumerate(banks):
            tmp = sm[:, h % 3, t, :]
            V.wait(marks[t])
            A.wait(V.done(nc.vector.tensor_scalar(tmp[:, 1:2], tmp[:, 0:1], -scale, None, ALU.mult)))
            exps[h, t] = A.done(nc.scalar.activation(prob[:, h % 3, t, :], c.lin.banks[i][:, :], ACT.Exp,
                                                     bias=tmp[:, 1:2], scale=scale, accum_out=tmp[:, 2:3]))
            c.lin.free[i] = [exps[h, t]]

    def normalise(h):
        marks = []
        for t in range(NT):
            tmp = sm[:, h % 3, t, :]
            V.wait(exps[h, t])
            marks.append(V.done(nc.vector.reciprocal(tmp[:, 3:4], tmp[:, 2:3])))
        for t in range(NT):
            V.wait(marks[t])
            marks[t] = V.done(nc.vector.tensor_scalar(prob[:, h % 3, t, :], prob[:, h % 3, t, :],
                                                      sm[:, h % 3, t, 3:4], None, ALU.mult))
        return marks

    def turn_probs(h, m_p):
        out = []
        for t in range(NT):
            i = c.aux.take()
            PE.wait(c.aux.free[i], m_p[t])
            for k in range(4):
                mm = nc.tensor.transpose(c.aux.banks[i][:, k * P:(k + 1) * P], prob[:, h % 3, t, k * P:(k + 1) * P], c.ident[:, :])
            m = PE.done(mm)
            V.wait(probT_read[h % 2])
            A.wait(probT_read[h % 2])
            e = c.evac(probT[:, h % 2, :, t * P:(t + 1) * P], c.aux.banks[i][:, :].rearrange("p (k q) -> p k q", k=4), m)
            c.aux.free[i] = [e]
            out.append(e)
        prob_read[h % 3] = m
        return out

    def mix(h, m_t):
        i = c.aux.take()
        PE.wait(c.aux.free[i], m_t)
        for k in range(4):
            v = va[:, k, h * HD:(h + 1) * HD] if h < HEADS else vb[:, k, (h - HEADS) // 4 * HD:((h - HEADS) // 4 + 1) * HD]
            mm = nc.tensor.matmul(c.aux.banks[i][:, 0:SEQ], v, probT[:, h % 2, k, :], start=(k == 0), stop=(k == 3))
        m = PE.done(mm)
        probT_read[h % 2] = m
        V.wait(m)
        c.aux.free[i] = [V.done(nc.vector.tensor_tensor(gT[:, h, :], gT[:, h, :], c.aux.banks[i][:, 0:SEQ], ALU.mult))]

    scores(0)
    scores(1)
    m_p = normalise(0)
    for h in range(2 * HEADS):
        m_t = turn_probs(h, m_p)
        if h + 1 < 2 * HEADS:
            m_p = normalise(h + 1)
        if h + 2 < 2 * HEADS:
            scores(h + 2)
        mix(h, m_t)
        c.step(1)
    c.barrier()
    return gT


def gated_residual(c, W, lhs, lhs_ready, gate_row, H, x, x_ready, kc=8):
    nc, V = c.nc, c.V
    V.wait(x_ready)
    products = c.at(6 * 1024, 2, 512)
    turn = [0]

    def evac(t, n, w, ps, r):
        V.wait(r)
        u = products[:, turn[0], :]
        turn[0] ^= 1
        m = V.done(nc.vector.tensor_tensor(u, ps, gate_row[:, n:n + w], ALU.mult))
        V.wait(m)
        m2 = V.done(nc.vector.scalar_tensor_tensor(out=H[:, t, n:n + w], in0=x[:, t, n:n + w], scalar=ALPHA,
                                              in1=u, op0=ALU.mult, op1=ALU.add))
        return [m]

    c.linear_rows(W, 0, D, lhs, range(NT), lhs_ready, evac, kc=kc)
    V.wait(V.last())
    return V.last()


def stage_attention_out(c, I, gT):
    nc = c.nc
    H = c.at(0, NT, D)
    gate_row = c.at(4096, D)
    m_gate = c.spread_column(c.mod[:, 0, 32:48, 0], gate_row, c.m_mod)
    x, arrived, slot = c.load(I["x"][0].rearrange("(t p) d -> p t d", p=P), NT, D)
    m = gated_residual(c, I["w_out_attn"][0], lambda k, t: gT[:, k, t * P:(t + 1) * P], c.V.last(), gate_row,
                       H, x, [arrived, m_gate])
    c.release(slot, m)
    post_norm(c, H, gate_row, load_gb(c, I, 0), None, m)
    return H


def stage_fourier(c, I, H):
    nc, PE, V, A = c.nc, c.PE, c.V, c.A
    K1 = 1024
    xn = c.at(4 * K1, NT, D)
    hT = c.at(8 * K1, KD, SEQ)
    u = c.at(12 * K1, NT, C_WIDTH)
    yT = c.at(20 * K1, C_WIDTH // P, SEQ)
    dft = c.at(28 * K1, NT, 512)
    ndft = c.at(29 * K1, NT, 256)
    s = DmaSem(c.sem("dft_loaded"))
    s.done(nc.scalar.dma_start(dft, I["dft"].rearrange("(t p) n -> p t n", p=P)))
    m_dft = s.done(nc.scalar.dma_start(ndft, I["ndft"].rearrange("(t p) n -> p t n", p=P)))
    m = c.layer_norm_rows(lambda t: H[:, t, :], lambda t: xn[:, t, :], V.last())
    m_h = c.turn(lambda k, t: xn[:, t, k * P:(k + 1) * P], lambda k: hT[:, k, :], KD, NT, m,
                 gain=lambda k: c.mod[:, 1, 16 + k, 0:1], shift=lambda k: c.mod[:, 1, k, 0:1])
    W = I["w_in_fourier"][0]
    c.linear_rows(W, 0, C_WIDTH, lambda k, t: hT[:, k, t * P:(t + 1) * P], range(NT), m_h,
                  lambda t, n, w, ps, r: [c.evac(u[:, t, n:n + w], ps, r)])
    m_u = [V.last(), A.last()]

    def evac_gate(j, cnt, ps, ready):
        A.wait(ready)
        return [A.done(nc.scalar.activation(yT[:, j:j + cnt, :], ps.rearrange("p (a b) -> p a b", b=SEQ), ACT.Silu))]

    c.linear_cols(W, C_WIDTH, 2 * C_WIDTH, lambda k: hT[:, k, :], SEQ, m_h, evac_gate)
    V.wait(A.last())
    c.barrier()
    AB = c.at(4 * K1, 2, 2, 512)
    ab_read = [None, None]
    PE.wait(m_dft, m_u)
    for g in range(C_GROUPS):
        par = g % 2
        marks = []
        for ch in range(2):
            i = c.lin.take()
            PE.wait(c.lin.free[i])
            o = g * C_DIM + ch * P
            for t in range(NT):
                mm = nc.tensor.matmul(c.lin.banks[i][:, :], u[:, t, o:o + P], dft[:, t, :], start=(t == 0), stop=(t == NT - 1))
            m = PE.done(mm)
            V.wait(ab_read[par])
            A.wait(ab_read[par])
            e = c.evac(AB[:, par, ch, :], c.lin.banks[i][:, :], m)
            c.lin.free[i] = [e]
            marks.append(e)
        PE.wait(marks)
        i = c.aux.take()
        PE.wait(c.aux.free[i])
        for co in range(2):
            q = slice(co * P, (co + 1) * P)
            for ch in range(2):
                nc.tensor.matmul(c.aux.banks[i][:, co * SEQ:(co + 1) * SEQ], dft[:, ch, q], AB[:, par, ch, 0:SEQ],
                                 start=(ch == 0), stop=False)
            for ch in range(2):
                mm = nc.tensor.matmul(c.aux.banks[i][:, co * SEQ:(co + 1) * SEQ], ndft[:, ch, q],
                                      AB[:, par, ch, SEQ:2 * SEQ], start=False, stop=(ch == 1))
        m = PE.done(mm)
        ab_read[par] = m
        V.wait(m)
        y = yT[:, 2 * g:2 * g + 2, :]
        c.aux.free[i] = [V.done(nc.vector.tensor_tensor(y, y, c.aux.banks[i][:, :].rearrange("p (a b) -> p a b", b=SEQ), ALU.mult))]
    m_y = V.last()
    c.barrier()
    gate_row = c.at(4 * K1, D)
    m_gate = c.spread_column(c.mod[:, 1, 32:48, 0], gate_row, None)
    m = gated_residual(c, I["w_out_fourier"][0], lambda k, t: yT[:, k, t * P:(t + 1) * P], m_y, gate_row, H, H, m_gate)
    post_norm(c, H, gate_row, load_gb(c, I, 1), None, m)
    c.barrier()


def column_sums(c, x, nk, square, ready, tmp):
    nc, PE, G = c.nc, c.PE, c.G
    i = c.aux.take()
    if square:
        G.wait(ready)
        ready = G.done(nc.gpsimd.tensor_tensor(tmp, x, x, ALU.mult))
        x = tmp
    PE.wait(ready, c.aux.free[i])
    for k in range(nk):
        mm = nc.tensor.matmul(c.aux.banks[i][:, 0:SEQ], c.ones[:, :], x[:, k, :], start=(k == 0), stop=(k == nk - 1))
    return i, PE.done(mm)


def stage_mixer(c, I, dr, H):
    nc, PE, V, A, G = c.nc, c.PE, c.V, c.A, c.G
    K1 = 1024
    NC = D_CONV // P
    PAD = TAPS - 1
    uT = c.at(4 * K1, NC, SEQ)
    cpad = c.at(6 * K1, NC, SEQ + PAD)
    convT = c.at(9 * K1, NC, SEQ)
    ysT = c.at(11 * K1, NC, SEQ)
    hn = c.at(13 * K1, NT, D)
    hT = c.at(17 * K1, KD, SEQ)
    aT = c.at(21 * K1, NC, SEQ)
    gT = c.at(23 * K1, NC, SEQ)
    m = c.rms_rows(lambda t: H[:, t, :], lambda t: hn[:, t, :], V.last(), aT.rearrange("p a b -> p (a b)"))
    m_h = c.turn(lambda k, t: hn[:, t, k * P:(k + 1) * P], lambda k: hT[:, k, :], KD, NT, m,
                 gain=lambda k: c.col("mix_g", k))
    m_zero = V.done(nc.vector.memset(cpad[:, :, 0:PAD], 0.0))
    W = I["w_in_2"][0]

    def to(dst):
        return lambda j, cnt, ps, r: [c.evac(dst[:, j:j + cnt, :], ps.rearrange("p (a b) -> p a b", b=SEQ), r)]

    def to_sigmoid(j, cnt, ps, r):
        A.wait(r)
        return [A.done(nc.scalar.activation(gT[:, j:j + cnt, :], ps.rearrange("p (a b) -> p a b", b=SEQ), ACT.Sigmoid))]

    rhs = lambda k: hT[:, k, :]
    c.linear_cols(W, 2 * D_CONV, 3 * D_CONV, rhs, SEQ, m_h, to(uT))
    m_u = [V.last(), A.last()]
    c.linear_cols(W, 0, D_CONV, rhs, SEQ, m_h, to(aT))
    c.linear_cols(W, D_CONV, 2 * D_CONV, rhs, SEQ, m_h, to_sigmoid)
    V.wait(V.last(), A.last())
    m_c = V.done(nc.vector.tensor_tensor(cpad[:, :, PAD:], aT, gT, ALU.mult))
    c.barrier(pool=True)

    o = 13 * K1
    bufs = [[c.at(o + K1 * (6 * par + i), S_BATCH, SEQ) for i in range(6)] for par in range(2)]
    pre = c.at(o + 12 * K1, 4, 512)
    tabs, arrived, slot_t = c.load(I["s5_b"].rearrange("(k p) n -> p k n", p=P), 8, 256)
    m_tab = arrived
    C = c.at(o + 4 * K1, 2, S_TILES, 32)
    CK = c.at(27 * K1, 2, S_TILES, 32)
    s = DmaSem(c.sem("s5_c_loaded"))
    m_c_in = s.done(nc.scalar.dma_start(C.rearrange("p a b h -> p (a b h)"), I["s5_c"]))
    V.wait(m_c_in)
    kr = c.kap[:, 0, :].unsqueeze(2).broadcast_to([P, S_TILES, 32])
    ki = c.kap[:, 1, :].unsqueeze(2).broadcast_to([P, S_TILES, 32])
    x = c.at(o, 2, S_TILES, 32)
    V.done(nc.vector.tensor_tensor(CK[:, 0], C[:, 0], kr, ALU.mult))
    V.done(nc.vector.tensor_tensor(x[:, 0], C[:, 1], ki, ALU.mult))
    V.done(nc.vector.tensor_tensor(CK[:, 1], C[:, 0], ki, ALU.mult))
    V.wait(V.done(nc.vector.tensor_tensor(x[:, 1], C[:, 1], kr, ALU.mult)))
    V.done(nc.vector.tensor_tensor(CK[:, 0], CK[:, 0], x[:, 0], ALU.subtract))
    V.wait(V.done(nc.vector.tensor_tensor(CK[:, 1], CK[:, 1], x[:, 1], ALU.add)))
    m_ck = V.done(nc.vector.tensor_scalar(CK[:, 1], CK[:, 1], -1.0, None, ALU.mult))
    V.wait(m_ck)

    dg = c.diag
    dg_read = [None] * 4
    PE.wait(m_c, m_zero)

    def conv_tile(k):
        i = c.aux.take()
        PE.wait(c.aux.free[i])
        for tap in range(TAPS):
            q = tap % 4
            A.wait(dg_read[q])
            m = A.done(nc.scalar.activation(dg[:, q, :], c.ident[:, :], ACT.Copy,
                                            scale=c.col("conv_w", k * TAPS + tap)))
            PE.wait(m)
            mm = nc.tensor.matmul(c.aux.banks[i][:, 0:SEQ], dg[:, q, :], cpad[:, k, tap:tap + SEQ],
                                  start=(tap == 0), stop=(tap == TAPS - 1))
            dg_read[q] = PE.done(mm)
        A.wait(dg_read[q])
        c.aux.free[i] = [A.done(nc.scalar.activation(convT[:, k, :], c.aux.banks[i][:, 0:SEQ], ACT.Identity,
                                                     bias=c.col("conv_b", k)))]

    inputs = {}

    def state_inputs(k):
        PE.wait(m_tab, m_u)
        for jj in range(S_BATCH):
            r = slice(32 * jj, 32 * jj + 32)
            i = c.lin.take()
            PE.wait(c.lin.free[i])
            for part in range(2):
                mm = nc.tensor.matmul(c.lin.banks[i][:, part * SEQ:(part + 1) * SEQ],
                                      tabs[r, k, part * P:(part + 1) * P], uT[r, k, :], start=True, stop=True,
                                      skip_group_check=True)
            inputs[k, jj] = (i, PE.done(mm))

    states_read = [None, None]
    state_inputs(0)
    for k in range(NC):
        a, b, t1, t2, t3, t4 = bufs[k % 2]
        E, m_e, slot_e = c.load(dr["phase"][k], 2 * S_BATCH, SEQ, after=c.phases_stored)
        V.wait(m_e, states_read[k % 2])
        G.wait(m_e, states_read[k % 2])
        for jj in range(S_BATCH):
            i, m = inputs[k, jj]
            V.wait(m)
            bank = c.lin.banks[i][:, :].rearrange("p (a b) -> p a b", a=2)
            q = 2 * (jj % 2)
            tc = pre[:, q, :].rearrange("p (a b) -> p a b", a=2)
            ts = pre[:, q + 1, :].rearrange("p (a b) -> p a b", a=2)
            V.done(nc.vector.tensor_tensor(tc, bank, E[:, jj, :].unsqueeze(1).broadcast_to([P, 2, SEQ]), ALU.mult))
            m = V.done(nc.vector.tensor_tensor(ts, bank, E[:, S_BATCH + jj, :].unsqueeze(1).broadcast_to([P, 2, SEQ]), ALU.mult))
            c.lin.free[i] = [m]
            V.wait(m)
            V.done(nc.vector.tensor_tensor(a[:, jj, :], tc[:, 0, :], ts[:, 1, :], ALU.add))
            m = V.done(nc.vector.tensor_tensor(b[:, jj, :], tc[:, 1, :], ts[:, 0, :], ALU.subtract))
        V.wait(m)
        for jj in range(S_BATCH):
            j = k * S_BATCH + jj
            rho = c.rho[:, j:j + 1].broadcast_to([P, SEQ])
            V.done(nc.vector.tensor_tensor_scan(t1[:, jj, :], rho, a[:, jj, :], 0.0, ALU.mult, ALU.add))
            m = V.done(nc.vector.tensor_tensor_scan(t2[:, jj, :], rho, b[:, jj, :], 0.0, ALU.mult, ALU.add))
        cosv, sinv = E[:, 0:S_BATCH, :], E[:, S_BATCH:, :]
        V.wait(m)
        G.wait(m)
        G.done(nc.gpsimd.tensor_tensor(t3, t1, sinv, ALU.mult))
        G.wait(G.done(nc.gpsimd.tensor_tensor(t4, t2, cosv, ALU.mult)))
        m_im = G.done(nc.gpsimd.tensor_tensor(t3, t3, t4, ALU.add))
        V.done(nc.vector.tensor_tensor(a, t1, cosv, ALU.mult))
        V.wait(V.done(nc.vector.tensor_tensor(b, t2, sinv, ALU.mult)))
        m_re = V.done(nc.vector.tensor_tensor(a, a, b, ALU.subtract))
        c.release(slot_e, m_re, m_im)
        conv_tile(k)
        if k + 1 < NC:
            state_inputs(k + 1)
        i = c.aux.take()
        PE.wait(c.aux.free[i], m_ck, m_re, m_im)
        for jj in range(S_BATCH):
            j = k * S_BATCH + jj
            out = c.aux.banks[i][32 * jj:32 * jj + 32, 0:SEQ]
            nc.tensor.matmul(out, CK[:, 0, j, :], a[:, jj, :], start=True, stop=False)
            mm = nc.tensor.matmul(out, CK[:, 1, j, :], t3[:, jj, :], start=False, stop=True)
        m = PE.done(mm)
        states_read[k % 2] = m
        V.wait(m)
        m = V.done(nc.vector.scalar_tensor_tensor(out=ysT[:, k, :], in0=uT[:, k, :], scalar=c.col("ssm_d", k),
                                                  in1=c.aux.banks[i][:, 0:SEQ], op0=ALU.mult, op1=ALU.add))
        c.aux.free[i] = [m]
    c.release(slot_t, PE.last())
    c.barrier(pool=True)

    zT = c.at(o, NC, SEQ)
    sg = c.at(o + 2 * K1, NC, SEQ)
    tmp = c.at(o + 4 * K1, NC, SEQ)
    cen = c.at(o + 6 * K1, NC, SEQ)
    stat = c.at(o + 8 * K1, 6, SEQ)
    tmp2 = c.at(o + 10 * K1, NC, SEQ)
    m_z = A.done(nc.scalar.activation(zT, ysT, ACT.Gelu_apprx_tanh))

    def glu(j, cnt, ps, r):
        A.wait(r)
        return [A.done(nc.scalar.activation(sg[:, j:j + cnt, :], ps.rearrange("p (a b) -> p a b", b=SEQ), ACT.Sigmoid))]

    c.linear_cols(I["ssm_glu_w_2"][0], 0, 1024, lambda k: zT[:, k, :], SEQ, m_z, glu)
    m_sg = A.last()

    def spread(row):
        return row.unsqueeze(1).broadcast_to([P, NC, SEQ])

    i, m = column_sums(c, convT, NC, False, A.last(), None)
    V.wait(m)
    V.wait(V.done(nc.vector.tensor_scalar(stat[:, 0, :], c.aux.banks[i][:, 0:SEQ], 1.0 / D_CONV, None, ALU.mult)))
    c.aux.free[i] = [V.last()]
    m = V.done(nc.vector.tensor_tensor(cen, convT, spread(stat[:, 0, :]), ALU.subtract))
    i, m = column_sums(c, cen, NC, True, m, tmp)
    c.rstd(stat[:, 1, :], c.aux.banks[i][:, 0:SEQ], m, 1.0 / D_CONV, (stat[:, 2, :], stat[:, 3, :]))
    c.aux.free[i] = [V.last()]
    V.wait(V.done(nc.vector.tensor_tensor(cen, cen, spread(stat[:, 1, :]), ALU.mult)))
    A.wait(V.last())
    for k in range(NC):
        m = A.done(nc.scalar.activation(convT[:, k, :], cen[:, k, :], ACT.Silu, bias=c.col("conv_ln_b", k),
                                        scale=c.col("conv_ln_g", k)))
    V.wait(m_sg)
    m_ys = V.done(nc.vector.tensor_tensor(ysT, zT, sg, ALU.mult))
    for x, m_x, name, tt in ((convT, m, "grp_conv", tmp), (ysT, m_ys, "grp_ssm", tmp2)):
        i, m1 = column_sums(c, x, NC, True, m_x, tt)
        c.rstd(stat[:, 1, :], c.aux.banks[i][:, 0:SEQ], m1, 1.0 / D_CONV, (stat[:, 2, :], stat[:, 3, :]))
        c.aux.free[i] = [V.last()]
        for k in range(NC):
            V.done(nc.vector.scalar_tensor_tensor(out=x[:, k, :], in0=x[:, k, :], scalar=c.col(name, k),
                                                  in1=stat[:, 1, :], op0=ALU.mult, op1=ALU.mult))
        V.wait(V.last())
    m = V.last()
    add_product(c, I["w_out_2"][0], lambda k, t: (convT if k < NC else ysT)[:, k % NC, t * P:(t + 1) * P], m, H)


def add_product(c, W, lhs, ready, H):
    nc, V = c.nc, c.V

    def evac(t, n, w, ps, r):
        V.wait(r)
        return [V.done(nc.vector.tensor_tensor(H[:, t, n:n + w], H[:, t, n:n + w], ps, ALU.add))]

    c.linear_rows(W, 0, D, lhs, range(NT), ready, evac)
    V.wait(V.last())
    c.barrier(pool=True)


def stage_memory(c, I, dr, H):
    nc, PE, V, A = c.nc, c.PE, c.V, c.A
    K1 = 1024
    hn = c.at(4 * K1, NT, D)
    hT = c.at(8 * K1, KD, SEQ)
    qT = c.at(12 * K1, KD, SEQ)
    oT = c.at(16 * K1, KD, SEQ)
    prob = c.at(20 * K1, MEM_HEADS, NT, SEQ)
    probT = c.at(22 * K1, MEM_HEADS, NT, SEQ)
    sm = c.sb("mem_softmax_tmp", [P, MEM_HEADS * NT, 4])
    m = c.rms_rows(lambda t: H[:, t, :], lambda t: hn[:, t, :], V.last(), qT.rearrange("p a b -> p (a b)")[:, 0:D])
    m_h = c.turn(lambda k, t: hn[:, t, k * P:(k + 1) * P], lambda k: hT[:, k, :], KD, NT, m,
                 gain=lambda k: c.col("mem_g", k))
    V.wait(A.last())
    A.wait(A.last())
    c.linear_cols(I["w_q_mem_2"][0], 0, D, lambda k: hT[:, k, :], SEQ, m_h,
                  lambda j, cnt, ps, r: [c.evac(qT[:, j:j + cnt, :], ps.rearrange("p (a b) -> p a b", b=SEQ), r)])
    m_q = [V.last(), A.last()]
    KT, m_k, slot_k = c.load(dr["memk"].rearrange("p a b -> p (a b)"), KD * SEQ, after=c.mem_kv_stored)
    KT = KT.rearrange("p (a b) -> p a b", b=SEQ)
    VV, m_v, slot_v = c.load(dr["memv"].rearrange("p a b -> p (a b)"), NT * D)
    VV = VV.rearrange("p (a b) -> p a b", b=D)
    PE.wait(m_q, m_k)
    KH = MEM_HD // P
    banks = []
    for h in range(MEM_HEADS):
        i = c.lin.take()
        PE.wait(c.lin.free[i])
        for t in range(NT):
            for k in range(KH):
                mm = nc.tensor.matmul(c.lin.banks[i][:, t * SEQ:(t + 1) * SEQ], qT[:, h * KH + k, t * P:(t + 1) * P],
                                      KT[:, h * KH + k, :], start=(k == 0), stop=(k == KH - 1))
        banks.append((i, PE.done(mm)))
    c.release(slot_k, PE.last())
    for h, (i, m) in enumerate(banks):
        marks = []
        for t in range(NT):
            mp, me = softmax_rows(c, c.lin.banks[i][:, t * SEQ:(t + 1) * SEQ], m, MEM_HD ** -0.5,
                                  prob[:, h, t, :], SEQ, sm[:, h * NT + t, :])
            marks.append(me)
        c.lin.free[i] = marks
        i = c.aux.take()
        PE.wait(c.aux.free[i], mp)
        for k in range(NT):
            for t in range(NT):
                mm = nc.tensor.transpose(c.aux.banks[i][:, (k * NT + t) * P:(k * NT + t + 1) * P],
                                         prob[:, h, t, k * P:(k + 1) * P], c.ident[:, :])
        m = PE.done(mm)
        e = c.evac(probT[:, h, :, :], c.aux.banks[i][:, :].rearrange("p (a b) -> p a b", a=NT), m)
        c.aux.free[i] = [e]
        PE.wait(e, m_v)
        for j in range(KH):
            if j % 2 == 0:
                i = c.aux.take()
                PE.wait(c.aux.free[i])
            d = (h * KH + j) * P
            for k in range(NT):
                mm = nc.tensor.matmul(c.aux.banks[i][:, (j % 2) * SEQ:(j % 2 + 1) * SEQ], VV[:, k, d:d + P],
                                      probT[:, h, k, :], start=(k == 0), stop=(k == NT - 1))
            if j % 2:
                m = PE.done(mm)
                c.aux.free[i] = [c.evac(oT[:, h * KH + j - 1:h * KH + j + 1, :],
                                        c.aux.banks[i][:, :].rearrange("p (a b) -> p a b", a=2), m)]
    c.release(slot_v, PE.last())
    add_product(c, I["w_o_mem_2"][0], lambda k, t: oT[:, k, t * P:(t + 1) * P], [V.last(), A.last()], H)


def top16(c, lists, vals, idx, n):
    nc, V = c.nc, c.V
    passes = (
        lambda q: nc.vector.max(vals(q)[:, 0:8], lists(q)),
        lambda q: nc.vector.max_index(idx(q)[:, 0:8], vals(q)[:, 0:8], lists(q)),
        lambda q: nc.vector.match_replace(lists(q), vals(q)[:, 0:8], lists(q), LOWEST),
        lambda q: nc.vector.max(vals(q)[:, 8:16], lists(q)),
        lambda q: nc.vector.max_index(idx(q)[:, 8:16], vals(q)[:, 8:16], lists(q)),
    )
    for one in passes:
        V.wait(V.last())
        for q in range(n):
            V.done(one(q))
            if q % 4 == 3:
                yield True
    V.wait(V.last())


def stage_experts(c, I, H, out):
    nc, PE, V, A, G = c.nc, c.PE, c.V, c.A, c.G
    K1 = 1024
    hn = c.at(4 * K1, NT, D)
    hT = c.at(8 * K1, KD, SEQ)
    qT = c.at(12 * K1, E_HEADS, SEQ)
    keys = c.at(14 * K1, E_HEADS, E_KEYS)
    m = c.rms_rows(lambda t: H[:, t, :], lambda t: hn[:, t, :], V.last(), c.at(12 * K1, D))
    A.wait(A.last())
    g_row, arrived, slot = c.load(I["norm_ffn_g_2"][0].partition_broadcast(P), D)
    V.wait(arrived)
    for t in range(NT):
        m = V.done(nc.vector.tensor_tensor(hn[:, t, :], hn[:, t, :], g_row, ALU.mult))
    V.wait(m)
    c.release(slot, m)
    m_h = c.turn(lambda k, t: hn[:, t, k * P:(k + 1) * P], lambda k: hT[:, k, :], KD, NT, m)
    V.wait(A.last())
    s = DmaSem(c.sem("keys_loaded"))
    A.wait(V.last())
    m_keys = s.done(nc.scalar.dma_start(keys, I["keysT"]))
    c.linear_cols(I["peer_w_q_2"][0], 0, E_HEADS * 2 * E_HALF, lambda k: hT[:, k, :], SEQ, m_h,
                  lambda j, cnt, ps, r: [c.evac(qT[:, j:j + cnt, :], ps.rearrange("p (a b) -> p a b", b=SEQ), r)])
    PE.wait(m_keys, V.last(), A.last())
    sc = c.at(15 * K1, E_HEADS * 2, E_KEYS)
    cand = c.at(17 * K1, E_HEADS, TOPK, TOPK)
    eq = c.at(19 * K1, E_HEADS, TOPK, TOPK)
    small = c.at(21 * K1, 16, 256)
    v1 = small[:, 0, :].rearrange("p (h s k) -> p h s k", h=8, s=2)
    i1 = small[:, 1, :].bitcast(U32)
    i1f = small[:, 2, :].rearrange("p (h s k) -> p h s k", h=8, s=2)
    top = small[:, 3, 0:E_SLOTS]
    pos = small[:, 4, 0:E_SLOTS].bitcast(U32)
    pi = small[:, 5, 0:E_SLOTS].bitcast(U32)
    pj = small[:, 6, 0:E_SLOTS].bitcast(U32)
    pif = small[:, 7, 0:E_SLOTS].rearrange("p (h k) -> p h k", h=8)
    pjf = small[:, 8, 0:E_SLOTS].rearrange("p (h k) -> p h k", h=8)
    e1 = small[:, 9, 0:E_SLOTS].rearrange("p (h k) -> p h k", h=8)
    e2 = small[:, 10, 0:E_SLOTS].rearrange("p (h k) -> p h k", h=8)
    idxf = small[:, 11, 0:E_SLOTS]
    hsum = small[:, 12, 0:E_HEADS]
    pair = small[:, 12, 128:144]
    g = c.at(25 * K1, NT, E_SLOTS)
    act = c.at(25 * K1 + 256, NT, E_SLOTS)
    idx = c.at(25 * K1 + 512, NT, E_SLOTS).bitcast(U32)
    m_idx = [None] * NT

    def choose(t):
        scv = sc.rearrange("p (h s) n -> p h s n", s=2)
        for h0 in range(0, E_HEADS, 4):
            ids = [c.lin.take(), c.lin.take()]
            for sd, i in enumerate(ids):
                PE.wait(c.lin.free[i])
                r = slice(sd * E_HALF, (sd + 1) * E_HALF)
                for h in range(4):
                    mm = nc.tensor.matmul(c.lin.banks[i][:, h * E_KEYS:(h + 1) * E_KEYS],
                                          qT[r, h0 + h, t * P:(t + 1) * P], keys[r, h0 + h, :],
                                          start=True, stop=True, skip_group_check=True)
                m = PE.done(mm)
                V.wait(m)
                c.lin.free[i] = [V.done(nc.vector.tensor_copy(
                    scv[:, h0:h0 + 4, sd, :], c.lin.banks[i][:, :].rearrange("p (a b) -> p a b", a=4)))]
        V.wait(V.last())
        yield True
        i1q = i1.rearrange("p (q k) -> p q k", k=TOPK)
        v1q = small[:, 0, :].rearrange("p (q k) -> p q k", k=TOPK)
        yield from top16(c, lambda q: sc[:, q, :], lambda q: v1q[:, q, :], lambda q: i1q[:, q, :], 2 * E_HEADS)
        V.done(nc.vector.tensor_copy(small[:, 2, :], i1))
        V.wait(V.done(nc.vector.tensor_tensor(
            cand, v1[:, :, 0, :].unsqueeze(3).broadcast_to([P, E_HEADS, TOPK, TOPK]),
            v1[:, :, 1, :].unsqueeze(2).broadcast_to([P, E_HEADS, TOPK, TOPK]), ALU.add)))
        tv = top.rearrange("p (h k) -> p h k", h=8)
        pv = pos.rearrange("p (h k) -> p h k", h=8)
        yield from top16(c, lambda q: cand[:, q, :, :].rearrange("p a b -> p (a b)"), lambda q: tv[:, q, :],
              lambda q: pv[:, q, :], E_HEADS)
        V.done(nc.vector.tensor_scalar(pi, pos, 4, None, ALU.logical_shift_right))
        V.wait(V.done(nc.vector.tensor_scalar(pj, pos, 15, None, ALU.bitwise_and)))
        V.done(nc.vector.tensor_copy(small[:, 7, 0:E_SLOTS], pi))
        V.wait(V.done(nc.vector.tensor_copy(small[:, 8, 0:E_SLOTS], pj)))
        iot = c.iota[:, :].unsqueeze(1).broadcast_to([P, TOPK, TOPK])
        for f, sd, e in ((pif, 0, e1), (pjf, 1, e2)):
            for h in range(E_HEADS):
                V.done(nc.vector.tensor_tensor(eq[:, h], f[:, h, :].unsqueeze(2).broadcast_to([P, TOPK, TOPK]), iot, ALU.is_equal))
            V.wait(V.last())
            V.wait(V.done(nc.vector.tensor_tensor(
                eq, eq, i1f[:, :, sd, :].unsqueeze(2).broadcast_to([P, E_HEADS, TOPK, TOPK]), ALU.mult)))
            V.wait(V.done(nc.vector.tensor_reduce(e, eq, AX_X, ALU.add)))
            yield True
        V.wait(V.done(nc.vector.scalar_tensor_tensor(out=idxf, in0=small[:, 9, 0:E_SLOTS], scalar=float(E_KEYS),
                                                     in1=small[:, 10, 0:E_SLOTS], op0=ALU.mult, op1=ALU.add)))
        m = V.done(nc.vector.tensor_copy(idx[:, t, :], idxf))
        m_idx[t] = m
        yield True
        gt = g[:, t, :].rearrange("p (h k) -> p h k", h=8)
        m = V.done(nc.vector.tensor_tensor(gt, tv, tv[:, :, 0:1].broadcast_to([P, E_HEADS, TOPK]), ALU.subtract))
        A.wait(m)
        m = A.done(nc.scalar.activation(g[:, t, :], g[:, t, :], ACT.Exp))
        V.wait(m)
        V.wait(V.done(nc.vector.tensor_reduce(hsum, gt, AX_X, ALU.add)))
        V.wait(V.done(nc.vector.reciprocal(hsum, hsum)))
        V.wait(V.done(nc.vector.tensor_tensor(gt, gt, hsum.unsqueeze(2).broadcast_to([P, E_HEADS, TOPK]), ALU.mult)))

    for _ in choose(0):
        pass
    later = choose(1)

    c.barrier(pool=True)
    NG = 2 * RING
    bufs = [c.ring[:, i // 2, (i % 2) * D:(i % 2 + 1) * D] for i in range(NG)]
    gsem = [DmaSem(c.sem(f"gather{i}")) for i in range(NG)]
    read = [None] * NG
    for i in range(RING):
        read[2 * i] = read[2 * i + 1] = c.ring_free[i]
    junk = c.at(8 * K1, D)
    n = 0
    store = DmaSem(c.sem("out_stored"))
    f_row = c.at(10 * K1, D)
    s = DmaSem(c.sem("final_g_loaded"))
    c.S.wait(V.last(), A.last(), PE.last())
    m_f = s.done(nc.sync.dma_start(f_row, I["final_norm_g_2"].partition_broadcast(P)))
    U, VT = I["peer_u_2"][0], I["peer_v_2"][0]
    for t in range(NT):
        G.wait(m_idx[t])
        for table in (U, VT):
            for k in range(E_SLOTS):
                q = n % NG
                n += 1
                G.wait(read[q])
                m = gsem[q].done(nc.gpsimd.indirect_dma_start(
                    bufs[q], None, table, bass.IndirectOffsetOnAxis(ap=idx[:, t, k:k + 1], axis=0)))
                V.wait(m)
                if table is U:
                    m = V.done(nc.vector.tensor_tensor_reduce(
                        out=bufs[q], in0=bufs[q], in1=hn[:, t, :], scale=1.0, scalar=0.0, op0=ALU.mult, op1=ALU.add,
                        accum_out=act[:, t, k:k + 1]))
                else:
                    V.wait(V.last())
                    m = V.done(nc.vector.scalar_tensor_tensor(
                        out=H[:, t, :], in0=bufs[q], scalar=act[:, t, k:k + 1], in1=H[:, t, :],
                        op0=ALU.mult, op1=ALU.add))
                read[q] = m
                next(later, None)
            if table is U:
                for _ in later:
                    pass
                A.wait(V.last())
                m = A.done(nc.scalar.activation(act[:, t, :], act[:, t, :], ACT.Gelu_apprx_tanh))
                V.wait(m)
                V.wait(V.done(nc.vector.tensor_tensor(act[:, t, :], act[:, t, :], g[:, t, :], ALU.mult)))
    m = c.rms_rows(lambda t: H[:, t, :], lambda t: H[:, t, :], V.last(), junk)
    V.wait(m_f)
    for t in range(NT):
        m = V.done(nc.vector.tensor_tensor(H[:, t, :], H[:, t, :], f_row, ALU.mult))
        c.S.wait(m)
        m = store.done(nc.sync.dma_start(out[0, t * P:(t + 1) * P, :], H[:, t, :]))
    c.S.wait(m)


def program(nc, I, out):
    with ExitStack() as ctx:
        dr = {
            "memk": nc.dram_tensor("mem_keys", (P, KD, SEQ), F32, kind="Internal").ap(),
            "memv": nc.dram_tensor("mem_values", (P, NT, D), F32, kind="Internal").ap(),
            "phase": nc.dram_tensor("phases", (S_TILES // S_BATCH, P, 2 * S_BATCH * SEQ), F32, kind="Internal").ap(),
        }
        c = Core(nc, ctx)
        constants(c, I)
        stage_phases(c, I, dr)
        stage_start(c, I, dr)
        gT = stage_attention(c, I)
        H = stage_attention_out(c, I, gT)
        c.step(0)
        c.barrier()
        stage_fourier(c, I, H)
        stage_mixer(c, I, dr, H)
        stage_memory(c, I, dr, H)
        stage_experts(c, I, H, out)


def _columns(v):
    return np.ascontiguousarray(np.asarray(v).reshape(-1, P).T)


def kernel(**inputs):
    import numpy as _np
    import concourse.bacc as _bacc
    from concourse import mybir as _mybir
    from concourse.bass_utils import run_bass_kernel_spmd as _run

    X = {k: _np.asarray(v) for k, v in inputs.items()}
    f = _np.float32
    pos = _np.arange(SEQ)

    def angles(rot):
        nf = rot // 4
        inv = (f(10000.0) ** (-_np.arange(nf, dtype=f) / f(nf))).astype(f)
        return _np.concatenate([(pos // 64).astype(f)[:, None] * inv, (pos % 64).astype(f)[:, None] * inv], 1)

    aa, ab = angles(ROPE_A), angles(HD)
    rope = _np.concatenate([_np.cos(aa), _np.sin(aa), _np.cos(ab), _np.sin(ab)], 1).astype(f)
    jk = (_np.arange(256)[:, None] * _np.arange(256)[None, :]) % 256 * (2 * _np.pi / 256)
    cb = X["conv_w_2"][0].T.reshape(8, P, TAPS).transpose(1, 0, 2).reshape(P, 8 * TAPS)
    packed = {
        "cvec": _np.concatenate([_columns(X["c"]), _columns(X["c_ctx"])], 1),
        "ada_b0": _columns(X["ada_b"][0]), "ada_b1": _columns(X["ada_b"][1]),
        "q_lora": _columns(X["q_lora_norm"]), "kv_lora": _columns(X["kv_lora_norm"]),
        "mix_g": _columns(X["norm_mix_g_2"]), "conv_b": _columns(X["conv_b_2"]),
        "conv_ln_g": _columns(X["conv_ln_g_2"]), "conv_ln_b": _columns(X["conv_ln_b_2"]),
        "grp_conv": _columns(X["grp_norm_conv_g_2"]), "grp_ssm": _columns(X["grp_norm_ssm_g_2"]),
        "ssm_d": _columns(X["ssm_d_2"]), "mem_g": _columns(X["norm_mem_g_2"]),
        "memn_g": _columns(X["mem_norm_g_2"]), "conv_w": cb,
        "lam_re": _columns(X["ssm_lam_re_2"]), "lam_im": _columns(X["ssm_lam_im_2"]),
        "log_dt": _columns(_np.repeat(X["ssm_log_dt_2"][0], S_STATE)),
    }
    Bd = _np.zeros((S_TILES, 2, S_DIM, 2, 2, S_STATE), f)
    Cd = _np.zeros((2, S_STATE, 2, S_TILES, 2, S_DIM), f)
    for part, s in enumerate(("re", "im")):
        b = X[f"ssm_b_{s}_2"][0].reshape(S_TILES, 2, S_STATE, S_DIM)
        cc = X[f"ssm_c_{s}_2"][0].reshape(S_TILES, 2, S_DIM, S_STATE)
        for gl in range(2):
            Bd[:, gl, :, part, gl, :] = b[:, gl].transpose(0, 2, 1)
            Cd[gl, :, part, :, gl, :] = cc[:, gl].transpose(2, 0, 1)
    arrays = {
        "colpack": _np.concatenate([packed[n] for n in COLS], 1),
        "ident": _np.eye(P, dtype=f), "ones": _np.ones((P, P), f),
        "iota": _np.tile(_np.arange(16, dtype=f), (P, 1)),
        "rope": rope.reshape(NT, P, 192).transpose(1, 0, 2),
        "dft": _np.concatenate([_np.cos(jk), _np.sin(jk)], 1).astype(f) / f(16),
        "ndft": -_np.sin(jk).astype(f) / f(16),
        "s5_b": Bd.reshape(S_TILES * 32, 2 * P),
        "s5_c": Cd.reshape(P, 2 * S_TILES * 32),
        "keysT": X["peer_keys_2"][0].transpose(1, 3, 0, 2).reshape(P, E_HEADS, E_KEYS),
    }
    for name in ("x", "ctx", "ada_w", "ln_g", "ln_b", "w_in_attn", "wq_b", "wkv_b", "q_norm_b", "k_norm_b",
                 "w_out_attn", "w_in_fourier", "w_out_fourier", "mem_2", "w_in_2", "ssm_glu_w_2", "w_out_2",
                 "w_q_mem_2", "w_kv_mem_2", "w_o_mem_2", "norm_ffn_g_2", "peer_w_q_2", "peer_u_2", "peer_v_2",
                 "final_norm_g_2"):
        arrays[name] = X[name]
    nc = _bacc.Bacc("TRN2", target_bir_lowering=False, num_devices=1)
    in_map, I = {}, {}
    for name, a in arrays.items():
        a = _np.ascontiguousarray(a)
        in_map[f"in_{name}"] = a
        I[name] = nc.dram_tensor(f"in_{name}", a.shape, _mybir.dt.from_np(a.dtype), kind="ExternalInput").ap()
    out = nc.dram_tensor("out_0", (1, SEQ, D), F32, kind="ExternalOutput").ap()
    program(nc, I, out)
    r = _run(nc, [in_map], core_ids=[0])
    return r.results[0]["out_0"]
```

```python
from contextlib import ExitStack

import numpy as np
import concourse.bass as bass
from concourse import mybir

F32 = mybir.dt.float32
F32R = mybir.dt.float32r
U32 = mybir.dt.uint32
ACT = mybir.ActivationFunctionType
ALU = mybir.AluOpType
AX_X = mybir.AxisListType.X

P = 128
D = 2048
KD = D // P
SEQ = 256
NT = SEQ // P
EPS = 1e-6
ALPHA = (2.0 * 2) ** 0.25

Q_LORA, KV_LORA, ROPE_A, HEADS, HD = 768, 512, 64, 8, 128
KV_HEADS = 2
A_SCALE = (HD + ROPE_A) ** -0.5
B_SCALE = HD ** -0.5
C_WIDTH, C_GROUPS, C_DIM = 4096, 16, 256

D_CONV, TAPS = 1024, 31
S_GROUPS, S_DIM, S_STATE = 64, 16, 64
S_TILES = S_GROUPS * S_STATE // P
S_BATCH = 4
PH_TILES = 2
MEM_HEADS, MEM_HD = 4, 512
E_HEADS, E_KEYS, E_HALF, TOPK = 8, 128, 64, 16
E_SLOTS = E_HEADS * TOPK

SLOT = 4096
RING = 4
ARENA = 30 * 1024
PARTS_K = 1
PARTS_BUFS = SLOT // (2 * 512 * PARTS_K)
LOWEST = -3.0e38

COLS = {}
_n = 0
for _name, _w in [("cvec", 32), ("ada_b0", 48), ("ada_b1", 48), ("q_lora", 6), ("kv_lora", 4), ("mix_g", 16),
                  ("conv_b", 8), ("conv_ln_g", 8), ("conv_ln_b", 8), ("grp_conv", 8), ("grp_ssm", 8),
                  ("ssm_d", 8), ("mem_g", 16), ("memn_g", 16), ("conv_w", 8 * TAPS),
                  ("lam_re", S_TILES), ("lam_im", S_TILES), ("log_dt", S_TILES)]:
    COLS[_name] = (_n, _w)
    _n += _w
NCOLS = _n


class Engine:

    def __init__(self, eng, sem):
        self.eng, self.sem, self.count, self.seen = eng, sem, 0, {}

    def wait(self, *marks):
        for m in marks:
            if m is None:
                continue
            if isinstance(m, list):
                self.wait(*m)
                continue
            sem, value = m
            if self.seen.get(sem.name, 0) < value:
                self.eng.wait_ge(sem, value)
                self.seen[sem.name] = value

    def done(self, ins):
        self.count += 1
        ins.then_inc(self.sem, 1)
        return (self.sem, self.count)

    def last(self):
        return (self.sem, self.count) if self.count else None


class DmaSem:

    def __init__(self, sem):
        self.sem, self.count = sem, 0

    def done(self, ins):
        self.count += 16
        ins.then_inc(self.sem, 16)
        return (self.sem, self.count)


class Banks:

    def __init__(self, banks):
        self.banks, self.free, self.at = banks, [None] * len(banks), 0

    def take(self):
        i = self.at
        self.at = (i + 1) % len(self.banks)
        return i


class Chunks:

    def __init__(self, chunks):
        self.chunks, self.marks = chunks, []
        self.upto(0)

    def upto(self, i):
        while len(self.marks) <= i:
            mark = next(self.chunks, None)
            if mark is None:
                break
            self.marks.append(mark)
        return self.marks[min(i, len(self.marks) - 1)]


class Core:
    def __init__(self, nc, ctx):
        self.nc, self.ctx = nc, ctx
        self.PE = Engine(nc.tensor, self.sem("pe_done"))
        self.V = Engine(nc.vector, self.sem("dve_done"))
        self.A = Engine(nc.scalar, self.sem("act_done"))
        self.G = Engine(nc.gpsimd, self.sem("pool_done"))
        self.S = Engine(nc.sync, self.sem("sp_done"))
        base = (nc.sbuf_base + 31) // 32 * 32
        self.ring = self.sb("ring", [P, RING, SLOT])
        self.ring_sems = [DmaSem(self.sem(f"ring_slot{i}")) for i in range(RING)]
        self.ring_free = [None] * RING
        self.ring_at = 0
        self.ring_held = [False] * RING
        self.arena = self.sb("arena", [P, ARENA])
        assert nc.sbuf_base - base == 4 * (RING * SLOT + ARENA)
        self.base = base
        self.w_parts = nc.alloc_sbuf_tensor_at("weight_parts", [P, PARTS_BUFS, 2, 512 * PARTS_K], F32R,
                                               offset=base + 4 * (RING - 1) * SLOT)
        self.w_parts_read = [None] * PARTS_BUFS
        self.w_parts_at = 0
        self.r_views = 0
        self.lin = Banks([self.ps(f"lin{i}") for i in range(4)])
        self.aux = Banks([self.ps(f"aux{i}") for i in range(4)])
        self.flip = 0
        self.background = []
        self.steps = 1
        self.owed = 0.0

    def step(self, n=None):
        if n is None:
            self.owed += self.steps
            n = int(self.owed)
            self.owed -= n
            if not n:
                return
        left = n or -1
        while self.background and left:
            if next(self.background[0], None) is None:
                self.background.pop(0)
            else:
                left -= 1

    def sem(self, name):
        return self.ctx.enter_context(self.nc.semaphore(name))

    def sb(self, name, shape, dt=F32):
        return self.ctx.enter_context(self.nc.sbuf_tensor(name, shape, dt))

    def ps(self, name):
        return self.ctx.enter_context(self.nc.psum_tensor(name, [P, 512], F32))

    def at(self, first, *shape):
        n = 1
        for s in shape:
            n *= s
        assert first + n <= ARENA, (first, shape)
        ap = self.arena[:, first:first + n]
        if len(shape) == 2:
            return ap.rearrange("p (a b) -> p a b", a=shape[0])
        if len(shape) == 3:
            return ap.rearrange("p (a b c) -> p a b c", a=shape[0], b=shape[1])
        return ap

    def at_r(self, first, n):
        self.r_views += 1
        t = self.nc.alloc_sbuf_tensor_at(f"parts{self.r_views}", [P, n], F32R,
                                         offset=self.base + 4 * (RING * SLOT + first))
        return t[:, :]

    def keep_slot_for_parts(self):
        i = RING - 1
        assert not self.ring_held[i]
        self.ring_held[i] = True
        self.w_parts_read = [self.ring_free[i]] * PARTS_BUFS

    def give_slot_back(self):
        self.release(RING - 1, *self.w_parts_read)

    def barrier(self, pool=False):
        engines = (self.PE, self.V, self.A) + ((self.G,) if pool else ())
        marks = [e.last() for e in engines]
        for e in engines:
            e.wait(marks)

    def load(self, src, *shape, after=None):
        i = self.take_slot()
        n = 1
        for s in shape:
            n *= s
        ap = self.ring[:, i, 0:n]
        if len(shape) == 2:
            ap = ap.rearrange("p (a b) -> p a b", a=shape[0])
        self.S.wait(after)
        return ap, self.ring_sems[i].done(self.nc.sync.dma_start(ap, src)), i

    def take_slot(self):
        while self.ring_held[self.ring_at]:
            self.ring_at = (self.ring_at + 1) % RING
        i = self.ring_at
        self.ring_at = (i + 1) % RING
        self.ring_held[i] = True
        self.S.wait(self.ring_free[i])
        return i

    def release(self, slot, *marks):
        self.ring_free[slot] = list(marks)
        self.ring_held[slot] = False

    def evac(self, dst, src, ready, scale=None, bias=None, same=False):
        if not same:
            self.flip ^= 1
        if self.flip:
            self.V.wait(ready)
            if scale is None:
                return self.V.done(self.nc.vector.tensor_copy(dst, src))
            if bias is None:
                return self.V.done(self.nc.vector.tensor_scalar(dst, src, scale, None, ALU.mult))
            return self.V.done(self.nc.vector.tensor_scalar(dst, src, scale, bias, ALU.mult, ALU.add))
        self.A.wait(ready)
        if scale is None:
            return self.A.done(self.nc.scalar.copy(dst, src))
        if bias is None:
            return self.A.done(self.nc.scalar.activation(dst, src, ACT.Identity, scale=scale))
        return self.A.done(self.nc.scalar.activation(dst, src, ACT.Identity, bias=bias, scale=scale))

    def linear_rows(self, W, n0, n1, lhs, tiles, lhs_ready, evac, kc=8):
        nc, PE = self.nc, self.PE
        K = W.shape[0] // P
        PE.wait(lhs_ready)
        for n in range(n0, n1, 512):
            w = min(512, n1 - n)
            ids = [self.lin.take() for _ in tiles]
            for i in ids:
                PE.wait(self.lin.free[i])
            for c in range(0, K, kc):
                wt, arrived, slot = self.load(
                    W[c * P:(c + kc) * P, n:n + w].rearrange("(k p) n -> p k n", p=P), kc, w)
                PE.wait(arrived)
                for i, t in zip(ids, tiles):
                    for k in range(kc):
                        mm = nc.tensor.matmul(self.lin.banks[i][:, 0:w], lhs(c + k, t), wt[:, k, :],
                                              start=(c + k == 0), stop=(c + k == K - 1))
                    mark = PE.done(mm)
                    if c + kc == K:
                        self.lin.free[i] = evac(t, n, w, self.lin.banks[i][:, 0:w], mark)
                self.release(slot, mark)
                self.step()

    def linear_cols(self, W, n0, n1, rhs, R, rhs_ready, evac, kc=8):
        nc, PE = self.nc, self.PE
        K = W.shape[0] // P
        per = min(4, 512 // R)
        PE.wait(rhs_ready)
        for n in range(n0, n1, 512):
            w = min(512, n1 - n)
            nj = w // P
            ids = [self.lin.take() for _ in range(0, nj, per)]
            for i in ids:
                PE.wait(self.lin.free[i])
            for c in range(0, K, kc):
                wt, arrived, slot = self.load(
                    W[c * P:(c + kc) * P, n:n + w].rearrange("(k p) n -> p k n", p=P), kc, w)
                PE.wait(arrived)
                for j in range(nj):
                    i = ids[j // per]
                    out = self.lin.banks[i][:, (j % per) * R:(j % per + 1) * R]
                    for k in range(kc):
                        mm = nc.tensor.matmul(out, wt[:, k, j * P:(j + 1) * P], rhs(c + k),
                                              start=(c + k == 0 and j % per == 0), stop=(c + k == K - 1),
                                              skip_group_check=True)
                    if j % per == per - 1 or j == nj - 1:
                        mark = PE.done(mm)
                        if c + kc == K:
                            j0 = j - j % per
                            cnt = j - j0 + 1
                            self.lin.free[i] = evac((n - n0) // P + j0, cnt, self.lin.banks[i][:, 0:cnt * R], mark)
                self.release(slot, mark)
                self.step()

    def turn(self, src, dst, nk, nt, ready, gain=None, shift=None):
        nc, PE = self.nc, self.PE
        PE.wait(ready)
        kk = max(1, 4 // nt)
        for k0 in range(0, nk, kk):
            i = self.aux.take()
            PE.wait(self.aux.free[i])
            ks = range(k0, min(nk, k0 + kk))
            for k in ks:
                for t in range(nt):
                    a = src(k, t)
                    f = a.shape[1]
                    mm = nc.tensor.transpose(
                        self.aux.banks[i][0:f, ((k - k0) * nt + t) * P:((k - k0) * nt + t + 1) * P], a, self.ident[:, :])
            mark = PE.done(mm)
            free = []
            for k in ks:
                d = dst(k)
                free.append(self.evac(d, self.aux.banks[i][0:f, (k - k0) * nt * P:(k - k0 + 1) * nt * P], mark,
                                      None if gain is None else gain(k), None if shift is None else shift(k),
                                      same=k > k0))
            self.aux.free[i] = free
        return [self.V.last(), self.A.last()]

    def parts(self, x, hi, lo, ready):
        return Chunks(self.make_parts(x, hi, lo, ready))

    def turn_parts(self, src, x, hi, lo, ready, gain=None, shift=None):
        return Chunks(self.make_turned_parts(src, x, hi, lo, ready, gain, shift))

    def make_parts(self, x, hi, lo, ready):
        nc, V, A = self.nc, self.V, self.A
        A.wait(ready)
        for o in range(0, x.shape[1], 1024):
            s = slice(o, o + 1024)
            m = A.done(nc.scalar.copy(hi[:, s], x[:, s]))
            V.wait(m)
            yield V.done(nc.vector.tensor_tensor(lo[:, s], x[:, s], hi[:, s].bitcast(F32), ALU.subtract))

    def make_turned_parts(self, src, x, hi, lo, ready, gain, shift):
        for k0 in range(0, KD, 4):
            m = self.turn(lambda k, t: src(k0 + k, t), lambda k: x[:, (k0 + k) * SEQ:(k0 + k + 1) * SEQ], 4, NT, ready[k0 // 4],
                          None if gain is None else lambda k: gain(k0 + k),
                          None if shift is None else lambda k: shift(k0 + k))
            s = slice(k0 * SEQ, (k0 + 4) * SEQ)
            yield from self.make_parts(x[:, s], hi[:, s], lo[:, s], m)

    def weight_parts(self, W, n0, n1, kc):
        nc, V, A = self.nc, self.V, self.A
        for n in range(n0, n1, 512):
            w = min(512, n1 - n)
            for c in range(0, W.shape[0] // P, kc):
                wt, arrived, slot = self.load(
                    W[c * P:(c + kc) * P, n:n + w].rearrange("(k p) n -> p k n", p=P), kc, w)
                for g in range(0, kc, PARTS_K):
                    q = self.w_parts_at
                    self.w_parts_at = (q + 1) % PARTS_BUFS
                    hi, lo = (self.w_parts[:, q, h, 0:PARTS_K * w].rearrange("p (k n) -> p k n", n=w) for h in range(2))
                    A.wait(arrived, self.w_parts_read[q])
                    m = A.done(nc.scalar.copy(hi, wt[:, g:g + PARTS_K, :]))
                    V.wait(m)
                    m = V.done(nc.vector.tensor_tensor(lo, wt[:, g:g + PARTS_K, :], hi.bitcast(F32), ALU.subtract))
                    if g + PARTS_K == kc:
                        self.release(slot, m)
                        self.step()
                    yield n, w, c + g, hi, lo, m, q

    def ahead(self, items):
        made = []
        for item in items:
            made.append(item)
            if len(made) == PARTS_BUFS:
                yield made.pop(0)
        yield from made

    def split_rows(self, W, n0, n1, lhs, x_chunks, evac, kc=8):
        nc, PE = self.nc, self.PE
        K = W.shape[0] // P
        for n, w, k0, hi, lo, m, q in self.ahead(self.weight_parts(W, n0, n1, kc)):
            if k0 == 0:
                ids = [self.lin.take() for _ in range(NT)]
                for i in ids:
                    PE.wait(self.lin.free[i])
            PE.wait(m, x_chunks.upto(k0 // 4))
            x_chunks.upto(k0 // 4 + 1)
            for t, i in enumerate(ids):
                for k in range(PARTS_K):
                    for a, b in ((0, hi), (0, lo), (1, hi)):
                        mm = nc.tensor.matmul(self.lin.banks[i][:, 0:w], lhs(a, k0 + k, t), b[:, k, :],
                                              start=(k0 + k == 0 and a == 0 and b is hi),
                                              stop=(k0 + k == K - 1 and a == 1))
                mark = PE.done(mm)
                if k0 + PARTS_K == K:
                    self.lin.free[i] = evac(t, n, w, self.lin.banks[i][:, 0:w], mark)
            self.w_parts_read[q] = mark

    def split_cols(self, W, n0, n1, rhs, x_chunks, evac, kc=8):
        nc, PE = self.nc, self.PE
        K = W.shape[0] // P
        for n, w, k0, hi, lo, m, q in self.ahead(self.weight_parts(W, n0, n1, kc)):
            nj = w // P
            if k0 == 0:
                ids = [self.lin.take() for _ in range(0, nj, 2)]
                for i in ids:
                    PE.wait(self.lin.free[i])
            PE.wait(m, x_chunks.upto(k0 // 4))
            x_chunks.upto(k0 // 4 + 1)
            for j in range(nj):
                i = ids[j // 2]
                out = self.lin.banks[i][:, (j % 2) * SEQ:(j % 2 + 1) * SEQ]
                for k in range(PARTS_K):
                    for a, b in ((hi, 0), (hi, 1), (lo, 0)):
                        mm = nc.tensor.matmul(out, a[:, k, j * P:(j + 1) * P], rhs(b, k0 + k),
                                              start=(k0 + k == 0 and j % 2 == 0 and a is hi and b == 0),
                                              stop=(k0 + k == K - 1 and a is lo), skip_group_check=True)
                if j % 2 or j == nj - 1:
                    mark = PE.done(mm)
                    if k0 + PARTS_K == K:
                        j0 = j - j % 2
                        cnt = j - j0 + 1
                        self.lin.free[i] = evac((n - n0) // P + j0, cnt, self.lin.banks[i][:, 0:cnt * SEQ], mark)
            self.w_parts_read[q] = mark

    def rstd(self, dst, src, ready, mul, tmp):
        nc, V, A = self.nc, self.V, self.A
        v, s = tmp
        V.wait(ready)
        m = V.done(nc.vector.tensor_scalar(v, src, mul, EPS, ALU.mult, ALU.add))
        A.wait(m)
        m = A.done(nc.scalar.activation(s, v, ACT.Sqrt))
        V.wait(m)
        V.wait(V.done(nc.vector.reciprocal(dst, s)))
        V.wait(V.done(nc.vector.tensor_tensor(s, dst, dst, ALU.mult)))
        V.wait(V.done(nc.vector.tensor_tensor(s, s, v, ALU.mult)))
        V.wait(V.done(nc.vector.tensor_scalar(s, s, -0.5, 1.5, ALU.mult, ALU.add)))
        m = V.done(nc.vector.tensor_tensor(dst, dst, s, ALU.mult))
        V.wait(m)
        return m

    def row_moments(self):
        nc, V = self.nc, self.V
        V.wait(V.last())
        for t in range(NT):
            m = V.done(nc.vector.bn_aggr(self.mv[:, t, :], self.bn[:, t, :, :].rearrange("p a b -> p (a b)")))
        self.rstd(self.st[:, 0:NT], self.mv[:, :, 1], m, 1.0, (self.st[:, 8:8 + NT], self.st[:, 16:16 + NT]))

    def layer_norm_rows(self, src, dst, ready):
        nc, V = self.nc, self.V
        V.wait(ready)
        for t in range(NT):
            for j in range(4):
                m = V.done(nc.vector.bn_stats(self.bn[:, t, j, :], src(t)[:, j * 512:(j + 1) * 512]))
        self.row_moments()
        t = NT - 1
        m = V.done(nc.vector.scalar_tensor_tensor(out=self.st[:, 40:41], in0=self.mv[:, t, 0:1], scalar=-1.0,
                                                  in1=self.st[:, t:t + 1], op0=ALU.mult, op1=ALU.mult))
        self.A.wait(m)
        return self.apply_blocks(
            lambda t, s: nc.vector.tensor_scalar(dst(t)[:, s], src(t)[:, s], self.mv[:, t, 0:1], self.st[:, t:t + 1],
                                                 ALU.subtract, ALU.mult),
            lambda t, s: nc.scalar.activation(dst(t)[:, s], src(t)[:, s], ACT.Identity, bias=self.st[:, 40:41],
                                              scale=self.st[:, t:t + 1]))

    def apply_blocks(self, on_vector, on_scalar):
        marks = []
        for n in range(0, D, 512):
            s = slice(n, n + 512)
            marks.append([self.V.done(on_vector(0, s)), self.A.done(on_scalar(NT - 1, s))])
        return marks

    def squares(self, t, n, x, ready):
        self.A.wait(ready, self.A.last())
        return self.A.done(self.nc.scalar.activation(self.junk[:, :], x, ACT.Square,
                                                     accum_out=self.sq[:, t, n // 512:n // 512 + 1]))

    def rms_rows(self, src, dst, ready, known=False, tiles=range(NT)):
        nc, V, A = self.nc, self.V, self.A
        if not known:
            for t in tiles:
                for n in range(0, D, 512):
                    self.squares(t, n, src(t)[:, n:n + 512], ready)
        V.wait(A.last())
        t0, t1 = tiles[0], tiles[-1] + 1
        m = V.done(nc.vector.tensor_reduce(self.st[:, 24 + t0:24 + t1], self.sq[:, t0:t1, :], AX_X, ALU.add))
        self.rstd(self.st[:, t0:t1], self.st[:, 24 + t0:24 + t1], m, 1.0 / D,
                  (self.st[:, 8:8 + t1 - t0], self.st[:, 16:16 + t1 - t0]))
        if dst is None:
            return None
        A.wait(V.last())
        return self.apply_blocks(
            lambda t, s: nc.vector.tensor_scalar(dst(t)[:, s], src(t)[:, s], self.st[:, t:t + 1], None, ALU.mult),
            lambda t, s: nc.scalar.activation(dst(t)[:, s], src(t)[:, s], ACT.Identity, scale=self.st[:, t:t + 1]))

    def spread_column(self, col, dst, ready):
        nc, PE, V = self.nc, self.PE, self.V
        read = None
        for b in range(4):
            V.wait(ready, read)
            for j in range(4):
                m = V.done(nc.vector.tensor_scalar(self.diag[:, j, :], self.ident[:, :],
                                                   col[:, b * 4 + j:b * 4 + j + 1], None, ALU.mult))
            yield True
            i = self.aux.take()
            PE.wait(m, self.aux.free[i])
            mm = nc.tensor.matmul(self.aux.banks[i][:, :], self.ones[:, :],
                                  self.diag[:, :, :].rearrange("p a b -> p (a b)"), start=True, stop=True)
            read = PE.done(mm)
            V.wait(read)
            self.m_spread = V.done(nc.vector.tensor_copy(dst[:, b * 512:(b + 1) * 512], self.aux.banks[i][:, :]))
            self.aux.free[i] = [self.m_spread]
            yield True

    def col(self, name, j=None):
        a, w = COLS[name]
        return self.colpack[:, a:a + w] if j is None else self.colpack[:, a + j:a + j + 1]


def constants(c, I):
    nc = c.nc
    c.ident = c.sb("ident", [P, P])
    c.ones = c.sb("ones", [P, P])
    c.diag = c.sb("diag", [P, 4, P])
    c.colpack = c.sb("colpack_sb", [P, NCOLS])
    c.rope = c.sb("rope_sb", [P, NT, 192])
    c.bn = c.sb("bn", [P, NT, 4, 6])
    c.mv = c.sb("mv", [P, NT, 2])
    c.st = c.sb("st", [P, 64])
    c.sq = c.sb("square_sums", [P, NT, 4])
    c.junk = c.sb("squares_out", [P, 512])
    c.iota = c.sb("iota_sb", [P, 16])
    c.macc = c.sb("mod_sums", [P, 2, 512])
    c.cv = c.sb("silu_c", [P, 2, KD])
    c.mod = c.sb("mod", [P, 2, 48, 2])
    s = DmaSem(c.sem("constants"))
    for dst, src in ((c.ident, I["ident"]), (c.colpack, I["colpack"]), (c.iota, I["iota"]), (c.ones, I["ones"]),
                     (c.rope, I["rope"])):
        m = s.done(nc.sync.dma_start(dst[:], src))
    for e in (c.PE, c.V, c.A, c.G):
        e.wait(m)


def softmax_rows(c, psum, ready, scale, prob, n, tmp):
    nc, V, A = c.nc, c.V, c.A
    V.wait(ready)
    V.wait(V.done(nc.vector.tensor_reduce(tmp[:, 0:1], psum, AX_X, ALU.max)))
    m = V.done(nc.vector.tensor_scalar(tmp[:, 1:2], tmp[:, 0:1], -scale, None, ALU.mult))
    A.wait(m)
    m = A.done(nc.scalar.activation(prob, psum, ACT.Exp, bias=tmp[:, 1:2], scale=scale, accum_out=tmp[:, 2:3]))
    V.wait(m)
    V.wait(V.done(nc.vector.reciprocal(tmp[:, 3:4], tmp[:, 2:3])))
    return V.done(nc.vector.tensor_scalar(prob, prob, tmp[:, 3:4], None, ALU.mult)), m


def modulation(c, I, layer, blocks, who):
    nc, PE, V = c.nc, c.PE, c.V
    W = I["ada_w"][layer]
    reduced = None
    for n in blocks:
        for ch in range(2):
            wt, arrived, slot = c.load(
                W[ch * 8 * P:(ch + 1) * 8 * P, n:n + 512].rearrange("(k p) n -> p k n", p=P), 8, 512)
            V.wait(arrived)
            for k in range(8):
                if k == 4:
                    yield True
                kk = ch * 8 + k
                for w in range(who):
                    acc, cv = c.macc[:, w, :], c.cv[:, w, kk:kk + 1]
                    if kk == 0:
                        V.wait(reduced)
                        V.done(nc.vector.tensor_scalar(acc, wt[:, 0, :], cv, None, ALU.mult))
                    else:
                        V.wait((V.sem, V.count - who + 1))
                        V.done(nc.vector.scalar_tensor_tensor(out=acc, in0=wt[:, k, :], scalar=cv, in1=acc,
                                                              op0=ALU.mult, op1=ALU.add))
            c.release(slot, V.last())
            done = V.last()
            yield True
        i = c.aux.take()
        PE.wait(done, c.aux.free[i])
        for j in range(4):
            for w in range(who):
                mm = nc.tensor.matmul(c.aux.banks[i][:, j * who + w:j * who + w + 1],
                                      c.macc[:, w, j * P:(j + 1) * P], c.ones[:, 0:1], start=True, stop=True)
        reduced = PE.done(mm)
        V.wait(reduced)
        j = n // P
        c.m_mod = V.done(nc.vector.tensor_tensor(
            c.mod[:, layer, j:j + 4, 0:who], c.aux.banks[i][:, 0:4 * who].rearrange("p (a b) -> p a b", b=who),
            c.col("ada_b%d" % layer)[:, j:j + 4].unsqueeze(2).broadcast_to([P, 4, who]), ALU.add))
        if D <= n < 2 * D:
            V.wait(c.m_mod)
            c.m_mod = V.done(nc.vector.tensor_scalar(c.mod[:, layer, j:j + 4, 0:who], c.mod[:, layer, j:j + 4, 0:who],
                                                     1.0, None, ALU.add))
        c.aux.free[i] = [c.m_mod]
        yield True


def attention_input(c, I, name, w):
    hT = c.at(0, KD, 2 * SEQ)
    rows, arrived, slot = c.load(I[name][0].rearrange("(t p) d -> p t d", p=P), NT, D)
    m = c.layer_norm_rows(lambda t: rows[:, t, :], lambda t: rows[:, t, :], arrived)
    yield True
    c.A.wait(c.m_mod)
    for k0 in range(0, KD, 4):
        c.turn(lambda k, t: rows[:, t, (k0 + k) * P:(k0 + k + 1) * P],
               lambda k: hT[:, k0 + k, w * SEQ:(w + 1) * SEQ], 4, NT, m[k0 // 4],
               gain=lambda k: c.mod[:, 0, 16 + k0 + k, w:w + 1], shift=lambda k: c.mod[:, 0, k0 + k, w:w + 1])
        yield True
    c.release(slot, c.PE.last())


def stage_start(c, I, dr):
    nc, PE, V, A = c.nc, c.PE, c.V, c.A
    KT = c.at(12 * 1024, KD, SEQ)
    VV = c.at(16 * 1024, NT, D)
    memT = c.at(20 * 1024, KD, SEQ)
    mem, arrived, slot = c.load(I["mem_2"][0].rearrange("(t p) d -> p t d", p=P), NT, D)
    V.wait(A.done(nc.scalar.activation(c.cv[:, :, :], c.col("cvec").rearrange("p (a b) -> p a b", a=2), ACT.Silu)))
    V.wait(arrived)
    m = c.rms_rows(lambda t: mem[:, t, :], lambda t: mem[:, t, :], arrived)
    mT = c.turn(lambda k, t: mem[:, t, k * P:(k + 1) * P], lambda k: memT[:, k, :], KD, NT, m,
                gain=lambda k: c.col("memn_g", k))
    c.release(slot, PE.last())
    inputs = [attention_input(c, I, name, w) for w, name in enumerate(("x", "ctx"))]
    c.background = [modulation(c, I, 0, range(0, 2 * D, 512), 2)] + inputs
    c.steps = 3.2
    Wkv = I["w_kv_mem_2"][0]
    c.linear_cols(Wkv, 0, D, lambda k: memT[:, k, :], SEQ, mT,
                  lambda j, cnt, ps, r: [c.evac(KT[:, j:j + cnt, :], ps.rearrange("p (a b) -> p a b", b=SEQ), r)])
    s = DmaSem(c.sem("mem_kv_stored"))
    A.wait(V.last(), A.last())
    s.done(nc.scalar.dma_start(dr["memk"], KT))
    c.linear_rows(Wkv, D, 2 * D, lambda k, t: memT[:, k, t * P:(t + 1) * P], range(NT), mT,
                  lambda t, n, w, ps, r: [c.evac(VV[:, t, n - D:n - D + w], ps, r)])
    c.step(0)
    c.background = [modulation(c, I, 0, range(2 * D, 3 * D, 512), 1), modulation(c, I, 1, range(0, 3 * D, 512), 1)]
    A.wait(V.last(), A.last())
    c.mem_kv_stored = s.done(nc.scalar.dma_start(dr["memv"], VV))
    c.steps = 2


def stage_phases(c, I, dr):
    nc, V, A, G = c.nc, c.V, c.A, c.G
    c.rho = c.sb("rho", [P, S_TILES])
    c.kap = c.sb("kap", [P, 2, S_TILES])
    T = c.sb("phase_tmp", [P, 8, S_TILES])
    dt, x, th, cs, sn, t0, t1, t2 = (T[:, i, :] for i in range(8))
    lr, li = c.col("lam_re"), c.col("lam_im")

    def v(ins):
        m = V.done(ins)
        V.wait(m)
        return m

    vt = nc.vector.tensor_tensor
    vs = nc.vector.tensor_scalar
    A.wait(A.done(nc.scalar.activation(dt, c.col("log_dt"), ACT.Exp)))
    V.wait(A.last())
    v(vt(x, lr, dt, ALU.mult))
    m = v(vt(th, li, dt, ALU.mult))
    A.wait(m)
    m = A.done(nc.scalar.activation(c.rho[:, :], x, ACT.Exp))
    V.wait(m)
    big = 12582912.0
    two_pi = 2 * np.pi
    p1 = 6.28125
    p2 = float(np.float32(np.round((two_pi - p1) * 2 ** 22) / 2 ** 22))
    p3 = float(two_pi - p1 - p2)
    v(vs(t0, th, 1.0 / two_pi, big, ALU.mult, ALU.add))
    v(vs(t0, t0, -big, None, ALU.add))
    for part in (p1, p2, p3):
        v(nc.vector.scalar_tensor_tensor(out=th, in0=t0, scalar=-part, in1=th, op0=ALU.mult, op1=ALU.add))
    lim = 3.1415925
    m = v(vs(th, th, lim, -lim, ALU.min, ALU.max))
    A.wait(m)
    A.done(nc.scalar.activation(sn, th, ACT.Sin))
    m = A.done(nc.scalar.activation(t1, th, ACT.Sin, scale=0.5))
    V.wait(m)
    v(vt(t1, t1, t1, ALU.mult))
    v(vs(cs, t1, -2.0, 1.0, ALU.mult, ALU.add))
    v(vt(t0, c.rho[:, :], cs, ALU.mult))
    v(vs(t0, t0, -1.0, None, ALU.add))
    v(vt(t1, c.rho[:, :], sn, ALU.mult))
    kr, ki = c.kap[:, 0, :], c.kap[:, 1, :]
    v(vt(kr, t0, lr, ALU.mult))
    v(vt(t2, t1, li, ALU.mult))
    v(vt(kr, kr, t2, ALU.add))
    v(vt(ki, t1, lr, ALU.mult))
    v(vt(t2, t0, li, ALU.mult))
    v(vt(ki, ki, t2, ALU.subtract))
    v(vt(t0, lr, lr, ALU.mult))
    v(vt(t1, li, li, ALU.mult))
    v(vt(t0, t0, t1, ALU.add))
    v(nc.vector.reciprocal(t1, t0))
    v(vt(kr, kr, t1, ALU.mult))
    v(vt(ki, ki, t1, ALU.mult))
    c.phases_stored = DmaSem(c.sem("phases_stored"))
    E = c.sb("phase", [P, 2, PH_TILES, SEQ])
    tmp = c.sb("phase_products", [P, 2, PH_TILES, SEQ // 2])
    c.G.wait(V.last(), A.last())
    pt = nc.gpsimd.tensor_tensor
    stored = None

    def g(ins):
        m = G.done(ins)
        G.wait(m)
        return m

    for b in range(S_TILES // PH_TILES):
        lo, hi = b * PH_TILES, (b + 1) * PH_TILES
        G.wait(stored)
        G.done(nc.gpsimd.memset(E[:, 0, :, 0:1], 1.0))
        G.done(nc.gpsimd.memset(E[:, 1, :, 0:1], 0.0))
        G.done(nc.gpsimd.tensor_copy(E[:, 0, :, 1], cs[:, lo:hi]))
        g(nc.gpsimd.tensor_copy(E[:, 1, :, 1], sn[:, lo:hi]))
        n = 2
        cn, sq, tt, uu = t0[:, 0:PH_TILES], t0[:, 8:8 + PH_TILES], t1[:, 0:PH_TILES], t1[:, 8:8 + PH_TILES]
        while n < SEQ:
            a, d = E[:, 0, :, n - 1], E[:, 1, :, n - 1]
            G.done(pt(tt, a, cs[:, lo:hi], ALU.mult))
            g(pt(uu, d, sn[:, lo:hi], ALU.mult))
            g(pt(cn, tt, uu, ALU.subtract))
            G.done(pt(tt, a, sn[:, lo:hi], ALU.mult))
            g(pt(uu, d, cs[:, lo:hi], ALU.mult))
            g(pt(sq, tt, uu, ALU.add))
            C = cn.unsqueeze(2).broadcast_to([P, PH_TILES, n])
            S = sq.unsqueeze(2).broadcast_to([P, PH_TILES, n])
            e0, e1 = E[:, 0, :, 0:n], E[:, 1, :, 0:n]
            x0, x1 = tmp[:, 0, :, 0:n], tmp[:, 1, :, 0:n]
            G.done(pt(x0, e0, C, ALU.mult))
            g(pt(x1, e1, S, ALU.mult))
            g(pt(E[:, 0, :, n:2 * n], x0, x1, ALU.subtract))
            G.done(pt(x0, e0, S, ALU.mult))
            g(pt(x1, e1, C, ALU.mult))
            g(pt(E[:, 1, :, n:2 * n], x0, x1, ALU.add))
            n *= 2
        dst = dr["phase"][lo // S_BATCH].rearrange("p (e a x) -> p e a x", e=2, a=S_BATCH)
        stored = c.phases_stored.done(nc.gpsimd.dma_start(dst[:, :, lo % S_BATCH:lo % S_BATCH + PH_TILES, :], E[:]))
    c.phases_stored = stored


def rope_rows(c, x, cos, sin, heads, half, tmp):
    nc, V = c.nc, c.V
    xe = x.rearrange("p h (f two) -> p h f two", two=2)
    x1, x2 = xe[:, :, :, 0], xe[:, :, :, 1]
    C = cos.unsqueeze(1).broadcast_to([P, heads, half])
    S = sin.unsqueeze(1).broadcast_to([P, heads, half])
    n = heads * half
    t = [tmp[:, i * n:(i + 1) * n].rearrange("p (h f) -> p h f", h=heads) for i in range(4)]
    V.done(nc.vector.tensor_tensor(t[0], x1, C, ALU.mult))
    V.done(nc.vector.tensor_tensor(t[1], x2, S, ALU.mult))
    V.done(nc.vector.tensor_tensor(t[2], x1, S, ALU.mult))
    V.wait(V.done(nc.vector.tensor_tensor(t[3], x2, C, ALU.mult)))
    V.done(nc.vector.tensor_tensor(x1, t[0], t[1], ALU.subtract))
    m = V.done(nc.vector.tensor_tensor(x2, t[2], t[3], ALU.add))
    V.wait(m)
    return m


def post_norm(c, H, g_slot):
    nc, V = c.nc, c.V
    c.row_moments()
    gb, arrived, slot = g_slot
    V.wait(arrived)
    for t in range(NT):
        V.done(nc.vector.scalar_tensor_tensor(out=H[:, t, :], in0=H[:, t, :], scalar=c.mv[:, t, 0:1], in1=gb[:, 0:D],
                                              op0=ALU.subtract, op1=ALU.mult))
    V.wait(V.last())
    for t in range(NT):
        V.done(nc.vector.scalar_tensor_tensor(out=H[:, t, :], in0=H[:, t, :], scalar=c.st[:, t:t + 1],
                                              in1=gb[:, D:2 * D], op0=ALU.mult, op1=ALU.add))
    V.wait(V.last())
    c.release(slot, V.last())
    return V.last()


def load_gb(c, I, layer):
    i = c.take_slot()
    s = c.ring_sems[i]
    s.done(c.nc.sync.dma_start(c.ring[:, i, 0:D], I["ln_g"][layer].partition_broadcast(P)))
    m = s.done(c.nc.sync.dma_start(c.ring[:, i, D:2 * D], I["ln_b"][layer].partition_broadcast(P)))
    return c.ring[:, i, :], m, i


def stage_attention(c, I):
    nc, PE, V, A = c.nc, c.PE, c.V, c.A
    K1 = 1024
    hT = c.at(0, KD, 2 * SEQ)
    gT = c.at(8 * K1, KD, SEQ)
    cq = c.at(12 * K1, NT, Q_LORA)
    qb = c.at(12 * K1 + 1536, NT, 1024)
    kb = c.at(12 * K1 + 3584, 4, 256)
    ckv = c.at(12 * K1 + 4608, 4, KV_LORA)
    vb = c.at(12 * K1 + 6656, 4, 256)
    kpe = c.at(12 * K1 + 7680, 4, ROPE_A)
    base = 20 * K1
    cqT = c.at(base, 6, SEQ)
    qa = c.at(base + 1536, NT, HEADS * 192)
    ckvT = c.at(base + 4608, 4, 2 * SEQ)
    qbT = c.at(base + 6656, HEADS, SEQ)
    kbT = c.at(base + 8704, KV_HEADS, 2 * SEQ)
    kpeT = c.at(base + 9728, 2 * SEQ)
    qn = c.sb("qk_norm", [P, 2, HD])
    ss = c.sb("head_ss", [P, 3, 24])

    s = DmaSem(c.sem("qk_norm_loaded"))
    s.done(nc.scalar.dma_start(qn[:, 0, :], I["q_norm_b"][0].partition_broadcast(P)))
    m_qn = s.done(nc.scalar.dma_start(qn[:, 1, :], I["k_norm_b"][0].partition_broadcast(P)))

    ready = [V.last(), A.last()]
    V.wait(c.mem_kv_stored)
    A.wait(c.mem_kv_stored)
    W = I["w_in_attn"][0]
    lhs = lambda k, t: hT[:, k, t * P:(t + 1) * P]

    def z(n0, n1, tiles, dst):
        c.steps = len(tiles)
        c.linear_rows(W, n0, n1, lhs, tiles, ready,
                      lambda t, n, w, ps, r: [c.evac(dst(t, n - n0, w), ps, r)])

    o_kv = Q_LORA
    o_pe = o_kv + KV_LORA
    o_qb = o_pe + ROPE_A
    o_kb = o_qb + 1024
    o_g = o_kb + 512
    z(o_kv, o_pe, range(4), lambda t, n, w: ckv[:, t, n:n + w])
    z(o_pe, o_qb, range(4), lambda t, n, w: kpe[:, t, n:n + w])
    z(0, Q_LORA, range(2), lambda t, n, w: cq[:, t, n:n + w])
    z(o_qb, o_kb, range(2), lambda t, n, w: qb[:, t, n:n + w])
    def kv_b(t, n, w, ps, r):
        return [c.evac(kb[:, t, :], ps[:, 0:256], r), c.evac(vb[:, t, :], ps[:, 256:512], r, same=True)]
    c.steps = 4
    c.linear_rows(W, o_kb, o_g, lhs, range(4), ready, kv_b)
    m_z = [V.last(), A.last()]

    junk = qa[:, 0, 0:1024]
    A.wait(m_z)
    V.wait(m_z, m_qn)
    for t in range(NT):
        A.wait(A.done(nc.scalar.activation(junk[:, 0:Q_LORA], cq[:, t, :], ACT.Square, accum_out=c.st[:, 24 + t:25 + t])))
    for t in range(4):
        A.wait(A.done(nc.scalar.activation(junk[:, 0:KV_LORA], ckv[:, t, :], ACT.Square, accum_out=c.st[:, 28 + t:29 + t])))
    m = A.last()
    c.rstd(c.st[:, 0:2], c.st[:, 24:26], m, 1.0 / Q_LORA, (c.st[:, 8:10], c.st[:, 16:18]))
    c.rstd(c.st[:, 2:6], c.st[:, 28:32], m, 1.0 / KV_LORA, (c.st[:, 10:14], c.st[:, 18:22]))
    for t in range(NT):
        V.done(nc.vector.tensor_scalar(cq[:, t, :], cq[:, t, :], c.st[:, t:t + 1], None, ALU.mult))
    for t in range(4):
        V.done(nc.vector.tensor_scalar(ckv[:, t, :], ckv[:, t, :], c.st[:, 2 + t:3 + t], None, ALU.mult))
    m_low = V.last()
    sq = qa[:, 1, 0:1024].rearrange("p (h d) -> p h d", h=8)
    V.wait(m_low)
    for t in range(NT):
        x = qb[:, t, :].rearrange("p (h d) -> p h d", h=8)
        V.wait(V.done(nc.vector.tensor_tensor(sq, x, x, ALU.mult)))
        V.wait(V.done(nc.vector.tensor_reduce(ss[:, 0, t * 8:t * 8 + 8], sq, AX_X, ALU.add)))
    for t in range(4):
        x = kb[:, t, :].rearrange("p (h d) -> p h d", h=2)
        V.wait(V.done(nc.vector.tensor_tensor(sq[:, 0:2, :], x, x, ALU.mult)))
        m = V.done(nc.vector.tensor_reduce(ss[:, 0, 16 + t * 2:18 + t * 2], sq[:, 0:2, :], AX_X, ALU.add))
        V.wait(m)
    c.rstd(ss[:, 1, :], ss[:, 0, :], m, 1.0 / HD, (ss[:, 2, :], ss[:, 0, :]))
    tmp = qa.rearrange("p a b -> p (a b)")
    for t in range(4):
        parts = [(kb, KV_HEADS, 1, 16 + t * 2)] + ([(qb, HEADS, 0, t * 8)] if t < NT else [])
        for x, heads, g, at in parts:
            r = ss[:, 1, at:at + heads]
            xv = x[:, t, :].rearrange("p (h d) -> p h d", h=heads)
            V.wait(V.done(nc.vector.tensor_tensor(xv, xv, r.unsqueeze(2).broadcast_to([P, heads, HD]), ALU.mult)))
            V.wait(V.done(nc.vector.tensor_tensor(xv, xv, qn[:, g, :].unsqueeze(1).broadcast_to([P, heads, HD]), ALU.mult)))
            if t < NT:
                rope_rows(c, xv, c.rope[:, t, 64:128], c.rope[:, t, 128:192], heads, 64, tmp)
    for t in range(NT):
        rope_rows(c, kpe[:, t:t + 1, :], c.rope[:, t, 0:32], c.rope[:, t, 32:64], 1, 32, tmp)
    m_rope = V.last()

    def evac_gate(j, cnt, ps, ready):
        A.wait(ready)
        return [A.done(nc.scalar.activation(gT[:, j:j + cnt, :], ps.rearrange("p (a b) -> p a b", b=SEQ), ACT.Silu))]

    def gate(n0, n1):
        c.linear_cols(W, o_g + n0, o_g + n1, lambda k: hT[:, k, 0:SEQ], SEQ, ready,
                      lambda j, cnt, ps, r: evac_gate(n0 // P + j, cnt, ps, r))

    c.steps = 0
    gate(0, 1536)
    c.steps = 3
    c.turn(lambda k, t: cq[:, t, k * P:(k + 1) * P], lambda k: cqT[:, k, :], 6, NT, m_rope,
           gain=lambda k: c.col("q_lora", k))
    c.turn(lambda k, t: ckv[:, t, k * P:(k + 1) * P], lambda k: ckvT[:, k, :], 4, 4, m_rope,
           gain=lambda k: c.col("kv_lora", k))
    c.turn(lambda k, t: qb[:, t, k * P:(k + 1) * P], lambda k: qbT[:, k, :], 8, NT, m_rope)
    c.turn(lambda k, t: kb[:, t, k * P:(k + 1) * P], lambda k: kbT[:, k, :], 2, 4, m_rope)
    m_T = c.turn(lambda k, t: kpe[:, t, :], lambda k: kpeT[0:64, :], 1, 4, m_rope)
    gate(1536, D)
    c.barrier()
    kaT = c.at(0, HEADS, 2 * SEQ)
    va = c.at(4 * K1, 4, HEADS * HD)
    qT = c.at(12 * K1, HEADS, SEQ)
    qpeT = c.at(14 * K1, HEADS, SEQ)

    c.linear_rows(I["wq_b"][0], 0, HEADS * 192, lambda k, t: cqT[:, k, t * P:(t + 1) * P], range(NT), m_T,
                  lambda t, n, w, ps, r: [c.evac(qa[:, t, n:n + w], ps, r)], kc=6)
    m_qa = [V.last(), A.last()]
    Wkv = I["wkv_b"][0]
    for half in range(2):
        wt, arrived, slot = c.load(Wkv[:, half * 1024:(half + 1) * 1024].rearrange("(k p) n -> p k n", p=P), 4, 1024)
        wh = wt.rearrange("p k (h d) -> p k h d", h=4)
        PE.wait(arrived)
        for h in range(4):
            i = c.lin.take()
            PE.wait(c.lin.free[i])
            for k in range(4):
                mm = nc.tensor.matmul(c.lin.banks[i][:, :], wh[:, k, h, 0:HD], ckvT[:, k, :], start=(k == 0), stop=(k == 3))
            m = PE.done(mm)
            c.lin.free[i] = [c.evac(kaT[:, half * 4 + h, :], c.lin.banks[i][:, :], m)]
        for t in range(4):
            i = c.lin.take()
            PE.wait(c.lin.free[i])
            for k in range(4):
                mm = nc.tensor.matmul(c.lin.banks[i][:, :].rearrange("p (h d) -> p h d", h=4),
                                      ckvT[:, k, t * P:(t + 1) * P], wh[:, k, :, HD:2 * HD], start=(k == 0), stop=(k == 3))
            m = PE.done(mm)
            c.lin.free[i] = [c.evac(va[:, t, half * 512:(half + 1) * 512], c.lin.banks[i][:, :], m)]
        c.release(slot, m)
    V.wait(m_qa)
    tmp = c.diag[:, :, :].rearrange("p a b -> p (a b)")
    tmp2 = c.at(16 * K1 + 512, 1024)
    for t in range(NT):
        qv = qa[:, t, :].rearrange("p (h d) -> p h d", h=HEADS)[:, :, HD:]
        m = rope_rows(c, qv, c.rope[:, t, 0:32], c.rope[:, t, 32:64], HEADS, 32, tmp2)
    c.turn(lambda k, t: qa[:, t, k * 192:k * 192 + HD], lambda k: qT[:, k, :], 8, NT, m)
    m_q = c.turn(lambda k, t: qa[:, t, k * 192 + HD:(k + 1) * 192], lambda k: qpeT[0:64, k, :], 8, NT, m)
    m_q += [V.last(), A.last()]
    c.barrier()
    prob = c.at(base, 3, NT, 512)
    probT = c.at(base + 3072, 2, 4, SEQ)
    sm = c.sb("softmax_tmp", [P, 3, NT, 4])
    probT_read = [None] * 2
    prob_read = [None] * 3
    exps = {}

    def scores(h):
        A.wait(prob_read[h % 3])
        scale = A_SCALE if h < HEADS else B_SCALE
        banks = []
        for t in range(NT):
            i = c.lin.take()
            PE.wait(c.lin.free[i])
            q = slice(t * P, (t + 1) * P)
            bank = c.lin.banks[i]
            if h < HEADS:
                nc.tensor.matmul(bank[:, :], qT[:, h, q], kaT[:, h, :], start=True, stop=False)
                mm = nc.tensor.matmul(bank[:, :], qpeT[0:64, h, q], kpeT[0:64, :], start=False, stop=True)
            else:
                mm = nc.tensor.matmul(bank[:, :], qbT[:, h - HEADS, q], kbT[:, (h - HEADS) // 4, :], start=True, stop=True)
            banks.append((i, PE.done(mm)))
        marks = []
        for t, (i, m) in enumerate(banks):
            tmp = sm[:, h % 3, t, :]
            V.wait(m)
            marks.append(V.done(nc.vector.tensor_reduce(tmp[:, 0:1], c.lin.banks[i][:, :], AX_X, ALU.max)))
        for t, (i, _) in enumerate(banks):
            tmp = sm[:, h % 3, t, :]
            V.wait(marks[t])
            A.wait(V.done(nc.vector.tensor_scalar(tmp[:, 1:2], tmp[:, 0:1], -scale, None, ALU.mult)))
            exps[h, t] = A.done(nc.scalar.activation(prob[:, h % 3, t, :], c.lin.banks[i][:, :], ACT.Exp,
                                                     bias=tmp[:, 1:2], scale=scale, accum_out=tmp[:, 2:3]))
            c.lin.free[i] = [exps[h, t]]

    def normalise(h):
        marks = []
        for t in range(NT):
            tmp = sm[:, h % 3, t, :]
            V.wait(exps[h, t])
            marks.append(V.done(nc.vector.reciprocal(tmp[:, 3:4], tmp[:, 2:3])))
        for t in range(NT):
            V.wait(marks[t])
            marks[t] = V.done(nc.vector.tensor_scalar(prob[:, h % 3, t, :], prob[:, h % 3, t, :],
                                                      sm[:, h % 3, t, 3:4], None, ALU.mult))
        return marks

    def turn_probs(h, m_p):
        out = []
        for t in range(NT):
            i = c.aux.take()
            PE.wait(c.aux.free[i], m_p[t])
            for k in range(4):
                mm = nc.tensor.transpose(c.aux.banks[i][:, k * P:(k + 1) * P], prob[:, h % 3, t, k * P:(k + 1) * P], c.ident[:, :])
            m = PE.done(mm)
            V.wait(probT_read[h % 2])
            A.wait(probT_read[h % 2])
            e = c.evac(probT[:, h % 2, :, t * P:(t + 1) * P], c.aux.banks[i][:, :].rearrange("p (k q) -> p k q", k=4), m)
            c.aux.free[i] = [e]
            out.append(e)
        prob_read[h % 3] = m
        return out

    def mix(h, m_t):
        i = c.aux.take()
        PE.wait(c.aux.free[i], m_t)
        for k in range(4):
            v = va[:, k, h * HD:(h + 1) * HD] if h < HEADS else vb[:, k, (h - HEADS) // 4 * HD:((h - HEADS) // 4 + 1) * HD]
            mm = nc.tensor.matmul(c.aux.banks[i][:, 0:SEQ], v, probT[:, h % 2, k, :], start=(k == 0), stop=(k == 3))
        m = PE.done(mm)
        probT_read[h % 2] = m
        V.wait(m)
        c.aux.free[i] = [V.done(nc.vector.tensor_tensor(gT[:, h, :], gT[:, h, :], c.aux.banks[i][:, 0:SEQ], ALU.mult))]

    assert len(c.background) <= 1
    c.V.wait(c.PE.last())
    c.background.insert(0, c.spread_column(c.mod[:, 0, 32:48, 0], c.at(16 * K1 + 512, D), c.m_mod))
    scores(0)
    scores(1)
    m_p = normalise(0)
    for h in range(2 * HEADS):
        m_t = turn_probs(h, m_p)
        if h + 1 < 2 * HEADS:
            m_p = normalise(h + 1)
        if h + 2 < 2 * HEADS:
            scores(h + 2)
        c.step(1)
        mix(h, m_t)
        c.step(1)
    c.barrier()
    return gT


def gated_residual(c, W, yT, hi, lo, y_ready, gate_row, H, x, x_ready):
    nc, V = c.nc, c.V
    m_y = c.parts(yT, hi, lo, y_ready)
    pair = (hi, lo)
    V.wait(x_ready)
    products = c.at(6 * 1024, 2, 512)
    turn = [0]

    def evac(t, n, w, ps, r):
        V.wait(r)
        u = products[:, turn[0], :]
        turn[0] ^= 1
        m = V.done(nc.vector.tensor_tensor(u, ps, gate_row[:, n:n + w], ALU.mult))
        V.wait(m)
        V.wait(V.done(nc.vector.scalar_tensor_tensor(out=H[:, t, n:n + w], in0=x[:, t, n:n + w], scalar=ALPHA,
                                                     in1=u, op0=ALU.mult, op1=ALU.add)))
        V.done(nc.vector.bn_stats(c.bn[:, t, n // 512, :], H[:, t, n:n + w]))
        return [m]

    c.split_rows(W, 0, D, lambda a, k, t: pair[a][:, k * SEQ + t * P:k * SEQ + (t + 1) * P], m_y, evac)
    V.wait(V.last())
    return V.last()


def stage_attention_out(c, I, gT):
    nc = c.nc
    H = c.at(0, NT, D)
    gate_row = c.at(16 * 1024 + 512, D)
    K1 = 1024
    x = c.at(20 * K1, NT, D)
    s = DmaSem(c.sem("x_loaded_again"))
    c.G.wait(c.V.last(), c.A.last(), c.PE.last())
    arrived = s.done(nc.gpsimd.dma_start(x, I["x"][0].rearrange("(t p) d -> p t d", p=P)))
    c.keep_slot_for_parts()
    m = gated_residual(c, I["w_out_attn"][0], c.at(8 * K1, KD * SEQ), c.at_r(12 * K1, KD * SEQ),
                       c.at_r(8 * K1, KD * SEQ), [c.V.last(), c.PE.last()], gate_row, H, x, [arrived, c.m_spread])
    c.give_slot_back()
    post_norm(c, H, load_gb(c, I, 0))
    return H


def stage_fourier(c, I, H):
    nc, PE, V, A = c.nc, c.PE, c.V, c.A
    K1 = 1024
    hr = [c.at_r(4 * K1, KD * SEQ), c.at_r(8 * K1, KD * SEQ)]
    u = c.at(12 * K1, NT, C_WIDTH)
    xn = c.at(12 * K1, NT, D)
    hT = c.at(20 * K1, KD * SEQ)
    yT = c.at(20 * K1, C_WIDTH // P, SEQ)
    dft = c.at(28 * K1, NT, 512)
    ndft = c.at(29 * K1, NT, 256)
    s = DmaSem(c.sem("dft_loaded"))
    s.done(nc.scalar.dma_start(dft, I["dft"].rearrange("(t p) n -> p t n", p=P)))
    m_dft = s.done(nc.scalar.dma_start(ndft, I["ndft"].rearrange("(t p) n -> p t n", p=P)))
    m = c.layer_norm_rows(lambda t: H[:, t, :], lambda t: xn[:, t, :], V.last())
    c.keep_slot_for_parts()
    m_h = c.turn_parts(lambda k, t: xn[:, t, k * P:(k + 1) * P], hT, hr[0], hr[1], m,
                       gain=lambda k: c.mod[:, 1, 16 + k, 0:1], shift=lambda k: c.mod[:, 1, k, 0:1])
    W = I["w_in_fourier"][0]
    c.split_rows(W, 0, C_WIDTH, lambda a, k, t: hr[a][:, k * SEQ + t * P:k * SEQ + (t + 1) * P], m_h,
                 lambda t, n, w, ps, r: [c.evac(u[:, t, n:n + w], ps, r)])
    m_u = [V.last(), A.last()]

    def evac_gate(j, cnt, ps, ready):
        A.wait(ready)
        return [A.done(nc.scalar.activation(yT[:, j:j + cnt, :], ps.rearrange("p (a b) -> p a b", b=SEQ), ACT.Silu))]

    A.wait(V.last())
    c.split_cols(W, C_WIDTH, 2 * C_WIDTH, lambda a, k: hr[a][:, k * SEQ:(k + 1) * SEQ], m_h, evac_gate)
    V.wait(A.last())
    c.barrier()
    AB = c.at(4 * K1, 2, 2, 512)
    ab_read = [None, None]
    PE.wait(m_dft, m_u)
    gate_row = c.at(8 * K1, D)
    c.background = [c.spread_column(c.mod[:, 1, 32:48, 0], gate_row, None)]
    for g in range(C_GROUPS):
        par = g % 2
        marks = []
        for ch in range(2):
            i = c.lin.take()
            PE.wait(c.lin.free[i])
            o = g * C_DIM + ch * P
            for t in range(NT):
                mm = nc.tensor.matmul(c.lin.banks[i][:, :], u[:, t, o:o + P], dft[:, t, :], start=(t == 0), stop=(t == NT - 1))
            m = PE.done(mm)
            V.wait(ab_read[par])
            A.wait(ab_read[par])
            e = c.evac(AB[:, par, ch, :], c.lin.banks[i][:, :], m)
            c.lin.free[i] = [e]
            marks.append(e)
        PE.wait(marks)
        i = c.aux.take()
        PE.wait(c.aux.free[i])
        for co in range(2):
            q = slice(co * P, (co + 1) * P)
            for ch in range(2):
                nc.tensor.matmul(c.aux.banks[i][:, co * SEQ:(co + 1) * SEQ], dft[:, ch, q], AB[:, par, ch, 0:SEQ],
                                 start=(ch == 0), stop=False)
            for ch in range(2):
                mm = nc.tensor.matmul(c.aux.banks[i][:, co * SEQ:(co + 1) * SEQ], ndft[:, ch, q],
                                      AB[:, par, ch, SEQ:2 * SEQ], start=False, stop=(ch == 1))
        m = PE.done(mm)
        ab_read[par] = m
        V.wait(m)
        y = yT[:, 2 * g:2 * g + 2, :]
        c.aux.free[i] = [V.done(nc.vector.tensor_tensor(y, y, c.aux.banks[i][:, :].rearrange("p (a b) -> p a b", b=SEQ), ALU.mult))]
        c.step(1)
    m_y = V.last()
    c.step(0)
    c.barrier()
    y_lo = c.at_r(20 * K1, C_WIDTH // P * SEQ)
    m = gated_residual(c, I["w_out_fourier"][0], c.at(20 * K1, C_WIDTH // P * SEQ), c.at_r(12 * K1, C_WIDTH // P * SEQ),
                       y_lo, m_y, gate_row, H, H, c.m_spread)
    post_norm(c, H, load_gb(c, I, 1))
    c.barrier()


def column_sums(c, x, nk, square, ready, tmp):
    nc, PE, G = c.nc, c.PE, c.G
    i = c.aux.take()
    if square:
        G.wait(ready)
        ready = G.done(nc.gpsimd.tensor_tensor(tmp, x, x, ALU.mult))
        x = tmp
    PE.wait(ready, c.aux.free[i])
    for k in range(nk):
        mm = nc.tensor.matmul(c.aux.banks[i][:, 0:SEQ], c.ones[:, :], x[:, k, :], start=(k == 0), stop=(k == nk - 1))
    return i, PE.done(mm)


def stage_mixer(c, I, dr, H):
    nc, PE, V, A, G = c.nc, c.PE, c.V, c.A, c.G
    K1 = 1024
    NC = D_CONV // P
    PAD = TAPS - 1
    uT = c.at(4 * K1, NC, SEQ)
    cpad = c.at(6 * K1, NC, SEQ + PAD)
    convT = c.at(9 * K1, NC, SEQ)
    ysT = c.at(11 * K1, NC, SEQ)
    hn = c.at(13 * K1, NT, D)
    aT = c.at(21 * K1, NC, SEQ)
    gT = c.at(23 * K1, NC, SEQ)
    m = c.rms_rows(lambda t: H[:, t, :], lambda t: hn[:, t, :], V.last())
    hr = [c.at_r(9 * K1, KD * SEQ), c.at_r(25 * K1, KD * SEQ)]
    m_h = c.turn_parts(lambda k, t: hn[:, t, k * P:(k + 1) * P], c.at(17 * K1, KD * SEQ), hr[0], hr[1], m,
                       gain=lambda k: c.col("mix_g", k))
    m_zero = V.done(nc.vector.memset(cpad[:, :, 0:PAD], 0.0))
    W = I["w_in_2"][0]

    def to(dst):
        return lambda j, cnt, ps, r: [c.evac(dst[:, j:j + cnt, :], ps.rearrange("p (a b) -> p a b", b=SEQ), r)]

    def to_sigmoid(j, cnt, ps, r):
        A.wait(r)
        return [A.done(nc.scalar.activation(gT[:, j:j + cnt, :], ps.rearrange("p (a b) -> p a b", b=SEQ), ACT.Sigmoid))]

    rhs = lambda a, k: hr[a][:, k * SEQ:(k + 1) * SEQ]
    c.split_cols(W, 2 * D_CONV, 3 * D_CONV, rhs, m_h, to(uT))
    m_u = [V.last(), A.last()]
    c.split_cols(W, 0, D_CONV, rhs, m_h, to(aT))
    c.split_cols(W, D_CONV, 2 * D_CONV, rhs, m_h, to_sigmoid)
    V.wait(V.last(), A.last())
    m_c = V.done(nc.vector.tensor_tensor(cpad[:, :, PAD:], aT, gT, ALU.mult))
    c.barrier(pool=True)

    o = 13 * K1
    bufs = [[c.at(o + K1 * (6 * par + i), S_BATCH, SEQ) for i in range(6)] for par in range(2)]
    pre = c.at(o + 12 * K1, 4, 512)
    tabs, arrived, slot_t = c.load(I["s5_b"].rearrange("(k p) n -> p k n", p=P), 8, 256)
    m_tab = arrived
    C = c.at(o + 4 * K1, 2, S_TILES, 32)
    CK = c.at(27 * K1, 2, S_TILES, 32)
    s = DmaSem(c.sem("s5_c_loaded"))
    m_c_in = s.done(nc.scalar.dma_start(C.rearrange("p a b h -> p (a b h)"), I["s5_c"]))
    V.wait(m_c_in)
    kr = c.kap[:, 0, :].unsqueeze(2).broadcast_to([P, S_TILES, 32])
    ki = c.kap[:, 1, :].unsqueeze(2).broadcast_to([P, S_TILES, 32])
    x = c.at(o, 2, S_TILES, 32)
    V.done(nc.vector.tensor_tensor(CK[:, 0], C[:, 0], kr, ALU.mult))
    V.done(nc.vector.tensor_tensor(x[:, 0], C[:, 1], ki, ALU.mult))
    V.done(nc.vector.tensor_tensor(CK[:, 1], C[:, 0], ki, ALU.mult))
    V.wait(V.done(nc.vector.tensor_tensor(x[:, 1], C[:, 1], kr, ALU.mult)))
    V.done(nc.vector.tensor_tensor(CK[:, 0], CK[:, 0], x[:, 0], ALU.subtract))
    V.wait(V.done(nc.vector.tensor_tensor(CK[:, 1], CK[:, 1], x[:, 1], ALU.add)))
    m_ck = V.done(nc.vector.tensor_scalar(CK[:, 1], CK[:, 1], -1.0, None, ALU.mult))
    V.wait(m_ck)

    dg = c.diag
    dg_read = [None] * 4
    PE.wait(m_c, m_zero)

    def conv_tile(k):
        i = c.aux.take()
        PE.wait(c.aux.free[i])
        for tap in range(TAPS):
            q = tap % 4
            A.wait(dg_read[q])
            m = A.done(nc.scalar.activation(dg[:, q, :], c.ident[:, :], ACT.Copy,
                                            scale=c.col("conv_w", k * TAPS + tap)))
            PE.wait(m)
            mm = nc.tensor.matmul(c.aux.banks[i][:, 0:SEQ], dg[:, q, :], cpad[:, k, tap:tap + SEQ],
                                  start=(tap == 0), stop=(tap == TAPS - 1))
            dg_read[q] = PE.done(mm)
        A.wait(dg_read[q])
        c.aux.free[i] = [A.done(nc.scalar.activation(convT[:, k, :], c.aux.banks[i][:, 0:SEQ], ACT.Identity,
                                                     bias=c.col("conv_b", k)))]

    inputs = {}

    def state_inputs(k):
        PE.wait(m_tab, m_u)
        for jj in range(S_BATCH):
            r = slice(32 * jj, 32 * jj + 32)
            i = c.lin.take()
            PE.wait(c.lin.free[i])
            for part in range(2):
                mm = nc.tensor.matmul(c.lin.banks[i][:, part * SEQ:(part + 1) * SEQ],
                                      tabs[r, k, part * P:(part + 1) * P], uT[r, k, :], start=True, stop=True,
                                      skip_group_check=True)
            inputs[k, jj] = (i, PE.done(mm))

    states_read = [None, None]
    state_inputs(0)
    for k in range(NC):
        a, b, t1, t2, t3, t4 = bufs[k % 2]
        E, m_e, slot_e = c.load(dr["phase"][k], 2 * S_BATCH, SEQ, after=c.phases_stored)
        V.wait(m_e, states_read[k % 2])
        G.wait(m_e, states_read[k % 2])
        for jj in range(S_BATCH):
            i, m = inputs[k, jj]
            V.wait(m)
            bank = c.lin.banks[i][:, :].rearrange("p (a b) -> p a b", a=2)
            q = 2 * (jj % 2)
            tc = pre[:, q, :].rearrange("p (a b) -> p a b", a=2)
            ts = pre[:, q + 1, :].rearrange("p (a b) -> p a b", a=2)
            V.done(nc.vector.tensor_tensor(tc, bank, E[:, jj, :].unsqueeze(1).broadcast_to([P, 2, SEQ]), ALU.mult))
            m = V.done(nc.vector.tensor_tensor(ts, bank, E[:, S_BATCH + jj, :].unsqueeze(1).broadcast_to([P, 2, SEQ]), ALU.mult))
            c.lin.free[i] = [m]
            V.wait(m)
            V.done(nc.vector.tensor_tensor(a[:, jj, :], tc[:, 0, :], ts[:, 1, :], ALU.add))
            m = V.done(nc.vector.tensor_tensor(b[:, jj, :], tc[:, 1, :], ts[:, 0, :], ALU.subtract))
        V.wait(m)
        for jj in range(S_BATCH):
            j = k * S_BATCH + jj
            rho = c.rho[:, j:j + 1].broadcast_to([P, SEQ])
            V.done(nc.vector.tensor_tensor_scan(t1[:, jj, :], rho, a[:, jj, :], 0.0, ALU.mult, ALU.add))
            m = V.done(nc.vector.tensor_tensor_scan(t2[:, jj, :], rho, b[:, jj, :], 0.0, ALU.mult, ALU.add))
        cosv, sinv = E[:, 0:S_BATCH, :], E[:, S_BATCH:, :]
        V.wait(m)
        G.wait(m)
        G.done(nc.gpsimd.tensor_tensor(t3, t1, sinv, ALU.mult))
        G.wait(G.done(nc.gpsimd.tensor_tensor(t4, t2, cosv, ALU.mult)))
        m_im = G.done(nc.gpsimd.tensor_tensor(t3, t3, t4, ALU.add))
        V.done(nc.vector.tensor_tensor(a, t1, cosv, ALU.mult))
        V.wait(V.done(nc.vector.tensor_tensor(b, t2, sinv, ALU.mult)))
        m_re = V.done(nc.vector.tensor_tensor(a, a, b, ALU.subtract))
        c.release(slot_e, m_re, m_im)
        conv_tile(k)
        if k + 1 < NC:
            state_inputs(k + 1)
        i = c.aux.take()
        PE.wait(c.aux.free[i], m_ck, m_re, m_im)
        for jj in range(S_BATCH):
            j = k * S_BATCH + jj
            out = c.aux.banks[i][32 * jj:32 * jj + 32, 0:SEQ]
            nc.tensor.matmul(out, CK[:, 0, j, :], a[:, jj, :], start=True, stop=False)
            mm = nc.tensor.matmul(out, CK[:, 1, j, :], t3[:, jj, :], start=False, stop=True)
        m = PE.done(mm)
        states_read[k % 2] = m
        V.wait(m)
        m = V.done(nc.vector.scalar_tensor_tensor(out=ysT[:, k, :], in0=uT[:, k, :], scalar=c.col("ssm_d", k),
                                                  in1=c.aux.banks[i][:, 0:SEQ], op0=ALU.mult, op1=ALU.add))
        c.aux.free[i] = [m]
    c.release(slot_t, PE.last())
    c.barrier(pool=True)

    zT = c.at(o, NC, SEQ)
    sg = c.at(o + 2 * K1, NC, SEQ)
    tmp = c.at(o + 4 * K1, NC, SEQ)
    cen = c.at(o + 6 * K1, NC, SEQ)
    stat = c.at(o + 8 * K1, 6, SEQ)
    tmp2 = c.at(o + 10 * K1, NC, SEQ)
    m_z = A.done(nc.scalar.activation(zT, ysT, ACT.Gelu_apprx_tanh))

    def glu(j, cnt, ps, r):
        A.wait(r)
        return [A.done(nc.scalar.activation(sg[:, j:j + cnt, :], ps.rearrange("p (a b) -> p a b", b=SEQ), ACT.Sigmoid))]

    zr = [c.at_r(25 * K1, NC * SEQ), c.at_r(27 * K1, NC * SEQ)]
    c.split_cols(I["ssm_glu_w_2"][0], 0, D_CONV, lambda a, k: zr[a][:, k * SEQ:(k + 1) * SEQ],
                 c.parts(c.at(o, NC * SEQ), zr[0], zr[1], m_z), glu)
    m_sg = A.last()

    def spread(row):
        return row.unsqueeze(1).broadcast_to([P, NC, SEQ])

    i, m = column_sums(c, convT, NC, False, A.last(), None)
    V.wait(m)
    V.wait(V.done(nc.vector.tensor_scalar(stat[:, 0, :], c.aux.banks[i][:, 0:SEQ], 1.0 / D_CONV, None, ALU.mult)))
    c.aux.free[i] = [V.last()]
    m = V.done(nc.vector.tensor_tensor(cen, convT, spread(stat[:, 0, :]), ALU.subtract))
    i, m = column_sums(c, cen, NC, True, m, tmp)
    c.rstd(stat[:, 1, :], c.aux.banks[i][:, 0:SEQ], m, 1.0 / D_CONV, (stat[:, 2, :], stat[:, 3, :]))
    c.aux.free[i] = [V.last()]
    V.wait(V.done(nc.vector.tensor_tensor(cen, cen, spread(stat[:, 1, :]), ALU.mult)))
    A.wait(V.last())
    for k in range(NC):
        m = A.done(nc.scalar.activation(convT[:, k, :], cen[:, k, :], ACT.Silu, bias=c.col("conv_ln_b", k),
                                        scale=c.col("conv_ln_g", k)))
    V.wait(m_sg)
    m_ys = V.done(nc.vector.tensor_tensor(ysT, zT, sg, ALU.mult))
    for x, m_x, name, tt in ((convT, m, "grp_conv", tmp), (ysT, m_ys, "grp_ssm", tmp2)):
        i, m1 = column_sums(c, x, NC, True, m_x, tt)
        c.rstd(stat[:, 1, :], c.aux.banks[i][:, 0:SEQ], m1, 1.0 / D_CONV, (stat[:, 2, :], stat[:, 3, :]))
        c.aux.free[i] = [V.last()]
        for k in range(NC):
            V.done(nc.vector.scalar_tensor_tensor(out=x[:, k, :], in0=x[:, k, :], scalar=c.col(name, k),
                                                  in1=stat[:, 1, :], op0=ALU.mult, op1=ALU.mult))
        V.wait(V.last())
    add_product(c, I["w_out_2"][0], c.at(9 * K1, KD * SEQ), c.at_r(25 * K1, KD * SEQ), c.at_r(9 * K1, KD * SEQ),
                [V.last(), PE.last()], H)


def add_product(c, W, yT, hi, lo, ready, H):
    nc, V = c.nc, c.V
    m_y = c.parts(yT, hi, lo, ready)
    pair = (hi, lo)

    def evac(t, n, w, ps, r):
        V.wait(r)
        m = V.done(nc.vector.tensor_tensor(H[:, t, n:n + w], H[:, t, n:n + w], ps, ALU.add))
        c.squares(t, n, H[:, t, n:n + w], m)
        return [m]

    c.split_rows(W, 0, D, lambda a, k, t: pair[a][:, k * SEQ + t * P:k * SEQ + (t + 1) * P], m_y, evac)
    V.wait(V.last())
    c.barrier(pool=True)


def stage_memory(c, I, dr, H):
    nc, PE, V, A = c.nc, c.PE, c.V, c.A
    K1 = 1024
    hn = c.at(4 * K1, NT, D)
    qT = c.at(12 * K1, KD, SEQ)
    oT = c.at(16 * K1, KD, SEQ)
    prob = c.at(20 * K1, MEM_HEADS, NT, SEQ)
    probT = c.at(22 * K1, MEM_HEADS, NT, SEQ)
    sm = c.sb("mem_softmax_tmp", [P, MEM_HEADS * NT, 4])
    m = c.rms_rows(lambda t: H[:, t, :], lambda t: hn[:, t, :], None, known=True)
    hr = [c.at_r(16 * K1, KD * SEQ), c.at_r(24 * K1, KD * SEQ)]
    m_h = c.turn_parts(lambda k, t: hn[:, t, k * P:(k + 1) * P], c.at(8 * K1, KD * SEQ), hr[0], hr[1], m,
                       gain=lambda k: c.col("mem_g", k))
    to_q = lambda j, cnt, ps, r: [c.evac(qT[:, j:j + cnt, :], ps.rearrange("p (a b) -> p a b", b=SEQ), r)]
    queries = lambda a, k: hr[a][:, k * SEQ:(k + 1) * SEQ]
    c.split_cols(I["w_q_mem_2"][0], 0, 512, queries, m_h, to_q)
    VV, KT = c.at(4 * K1, NT, D), c.at(8 * K1, KD, SEQ)
    s = DmaSem(c.sem("mem_values_back"))
    G = c.G
    G.wait(c.mem_kv_stored, PE.last())
    m_v = s.done(nc.gpsimd.dma_start(VV, dr["memv"]))
    s = DmaSem(c.sem("mem_keys_back"))
    G.wait(m_h.marks[-1])
    m_k = s.done(nc.gpsimd.dma_start(KT, dr["memk"]))
    c.split_cols(I["w_q_mem_2"][0], 512, D, queries, m_h,
                 lambda j, cnt, ps, r: to_q(4 + j, cnt, ps, r))
    m_q = [V.last(), A.last()]
    PE.wait(m_q, m_k)
    KH = MEM_HD // P
    banks = []
    for h in range(MEM_HEADS):
        i = c.lin.take()
        PE.wait(c.lin.free[i])
        for t in range(NT):
            for k in range(KH):
                mm = nc.tensor.matmul(c.lin.banks[i][:, t * SEQ:(t + 1) * SEQ], qT[:, h * KH + k, t * P:(t + 1) * P],
                                      KT[:, h * KH + k, :], start=(k == 0), stop=(k == KH - 1))
        banks.append((i, PE.done(mm)))
    for h, (i, m) in enumerate(banks):
        marks = []
        for t in range(NT):
            mp, me = softmax_rows(c, c.lin.banks[i][:, t * SEQ:(t + 1) * SEQ], m, MEM_HD ** -0.5,
                                  prob[:, h, t, :], SEQ, sm[:, h * NT + t, :])
            marks.append(me)
        c.lin.free[i] = marks
        i = c.aux.take()
        PE.wait(c.aux.free[i], mp)
        for k in range(NT):
            for t in range(NT):
                mm = nc.tensor.transpose(c.aux.banks[i][:, (k * NT + t) * P:(k * NT + t + 1) * P],
                                         prob[:, h, t, k * P:(k + 1) * P], c.ident[:, :])
        m = PE.done(mm)
        e = c.evac(probT[:, h, :, :], c.aux.banks[i][:, :].rearrange("p (a b) -> p a b", a=NT), m)
        c.aux.free[i] = [e]
        PE.wait(e, m_v)
        for j in range(KH):
            if j % 2 == 0:
                i = c.aux.take()
                PE.wait(c.aux.free[i])
            d = (h * KH + j) * P
            for k in range(NT):
                mm = nc.tensor.matmul(c.aux.banks[i][:, (j % 2) * SEQ:(j % 2 + 1) * SEQ], VV[:, k, d:d + P],
                                      probT[:, h, k, :], start=(k == 0), stop=(k == NT - 1))
            if j % 2:
                m = PE.done(mm)
                c.aux.free[i] = [c.evac(oT[:, h * KH + j - 1:h * KH + j + 1, :],
                                        c.aux.banks[i][:, :].rearrange("p (a b) -> p a b", a=2), m)]
    add_product(c, I["w_o_mem_2"][0], c.at(16 * K1, KD * SEQ), c.at_r(24 * K1, KD * SEQ), c.at_r(16 * K1, KD * SEQ),
                [V.last(), A.last()], H)


def top16(c, lists, vals, idx, n):
    nc, V = c.nc, c.V
    passes = (
        lambda q: nc.vector.max(vals(q)[:, 0:8], lists(q)),
        lambda q: nc.vector.max_index(idx(q)[:, 0:8], vals(q)[:, 0:8], lists(q)),
        lambda q: nc.vector.match_replace(lists(q), vals(q)[:, 0:8], lists(q), LOWEST),
        lambda q: nc.vector.max(vals(q)[:, 8:16], lists(q)),
        lambda q: nc.vector.max_index(idx(q)[:, 8:16], vals(q)[:, 8:16], lists(q)),
    )
    for one in passes:
        V.wait(V.last())
        for q in range(n):
            V.done(one(q))
            if q % 4 == 3:
                yield True
    V.wait(V.last())


def stage_experts(c, I, H, out):
    nc, PE, V, A, G = c.nc, c.PE, c.V, c.A, c.G
    K1 = 1024
    hn = c.at(4 * K1, NT, D)
    hT = c.at(8 * K1, KD * SEQ)
    hr = [c.at_r(26 * K1, KD * SEQ), c.at_r(8 * K1, KD * SEQ)]
    qT = c.at(12 * K1, E_HEADS, SEQ)
    keys = c.at(14 * K1, E_HEADS, E_KEYS)
    c.rms_rows(lambda t: H[:, t, :], None, None, known=True)
    g_row, arrived, slot = c.load(I["norm_ffn_g_2"][0].partition_broadcast(P), D)
    V.wait(arrived)
    m = []
    for n in range(0, D, 512):
        b = slice(n, n + 512)
        for t in range(NT):
            V.done(nc.vector.scalar_tensor_tensor(out=hn[:, t, b], in0=H[:, t, b], scalar=c.st[:, t:t + 1],
                                                  in1=g_row[:, b], op0=ALU.mult, op1=ALU.mult))
        m.append(V.last())
    c.release(slot, V.last())
    m_h = c.turn_parts(lambda k, t: hn[:, t, k * P:(k + 1) * P], hT, hr[0], hr[1], m)
    s = DmaSem(c.sem("keys_loaded"))
    m_keys = s.done(nc.scalar.dma_start(keys, I["keysT"]))
    sc = c.at(15 * K1, E_HEADS * 2, E_KEYS)
    cand = c.at(17 * K1, E_HEADS, TOPK, TOPK)
    eq = c.at(19 * K1, E_HEADS, TOPK, TOPK)
    small = c.at(21 * K1, 16, 256)
    v1 = small[:, 0, :].rearrange("p (h s k) -> p h s k", h=8, s=2)
    i1 = small[:, 1, :].bitcast(U32)
    i1f = small[:, 2, :].rearrange("p (h s k) -> p h s k", h=8, s=2)
    top = small[:, 3, 0:E_SLOTS]
    pos = small[:, 4, 0:E_SLOTS].bitcast(U32)
    pi = small[:, 5, 0:E_SLOTS].bitcast(U32)
    pj = small[:, 6, 0:E_SLOTS].bitcast(U32)
    pif = small[:, 7, 0:E_SLOTS].rearrange("p (h k) -> p h k", h=8)
    pjf = small[:, 8, 0:E_SLOTS].rearrange("p (h k) -> p h k", h=8)
    e1 = small[:, 9, 0:E_SLOTS].rearrange("p (h k) -> p h k", h=8)
    e2 = small[:, 10, 0:E_SLOTS].rearrange("p (h k) -> p h k", h=8)
    idxf = small[:, 11, 0:E_SLOTS]
    hsum = small[:, 12, 0:E_HEADS]
    g = c.at(25 * K1, NT, E_SLOTS)
    act = c.at(25 * K1 + 256, NT, E_SLOTS)
    idx = c.at(25 * K1 + 512, NT, E_SLOTS).bitcast(U32)
    HH = 2
    GROUPS = E_HEADS // HH
    m_q, m_idx, m_gate = {}, {}, {}

    def choose(t, group):
        h0 = group * HH
        hs = slice(h0, h0 + HH)
        ks = slice(h0 * TOPK, (h0 + HH) * TOPK)
        ls = slice(2 * h0 * TOPK, 2 * (h0 + HH) * TOPK)
        scv = sc.rearrange("p (h s) n -> p h s n", s=2)
        V.wait(V.last(), A.last())
        for sd in range(2):
            i = c.aux.take()
            PE.wait(c.aux.free[i], m_keys, m_q[group])
            r = slice(sd * E_HALF, (sd + 1) * E_HALF)
            for h in range(HH):
                mm = nc.tensor.matmul(c.aux.banks[i][:, h * E_KEYS:(h + 1) * E_KEYS],
                                      qT[r, h0 + h, t * P:(t + 1) * P], keys[r, h0 + h, :],
                                      start=True, stop=True, skip_group_check=True)
            m = PE.done(mm)
            V.wait(m)
            c.aux.free[i] = [V.done(nc.vector.tensor_copy(
                scv[:, hs, sd, :], c.aux.banks[i][:, 0:HH * E_KEYS].rearrange("p (a b) -> p a b", a=HH)))]
        V.wait(V.last())
        yield True
        i1q = i1.rearrange("p (q k) -> p q k", k=TOPK)
        v1q = small[:, 0, :].rearrange("p (q k) -> p q k", k=TOPK)
        yield from top16(c, lambda q: sc[:, 2 * h0 + q, :], lambda q: v1q[:, 2 * h0 + q, :],
                         lambda q: i1q[:, 2 * h0 + q, :], 2 * HH)
        V.done(nc.vector.tensor_copy(small[:, 2, ls], i1[:, ls]))
        V.wait(V.done(nc.vector.tensor_tensor(
            cand[:, hs], v1[:, hs, 0, :].unsqueeze(3).broadcast_to([P, HH, TOPK, TOPK]),
            v1[:, hs, 1, :].unsqueeze(2).broadcast_to([P, HH, TOPK, TOPK]), ALU.add)))
        tv = top.rearrange("p (h k) -> p h k", h=8)
        pv = pos.rearrange("p (h k) -> p h k", h=8)
        yield from top16(c, lambda q: cand[:, h0 + q, :, :].rearrange("p a b -> p (a b)"),
                         lambda q: tv[:, h0 + q, :], lambda q: pv[:, h0 + q, :], HH)
        V.done(nc.vector.tensor_scalar(pi[:, ks], pos[:, ks], 4, None, ALU.logical_shift_right))
        V.wait(V.done(nc.vector.tensor_scalar(pj[:, ks], pos[:, ks], 15, None, ALU.bitwise_and)))
        V.done(nc.vector.tensor_copy(small[:, 7, ks], pi[:, ks]))
        V.wait(V.done(nc.vector.tensor_copy(small[:, 8, ks], pj[:, ks])))
        iot = c.iota[:, :].unsqueeze(1).broadcast_to([P, TOPK, TOPK])
        for f, sd, e in ((pif, 0, e1), (pjf, 1, e2)):
            for h in range(h0, h0 + HH):
                V.done(nc.vector.tensor_tensor(eq[:, h], f[:, h, :].unsqueeze(2).broadcast_to([P, TOPK, TOPK]), iot, ALU.is_equal))
            V.wait(V.last())
            V.wait(V.done(nc.vector.tensor_tensor(
                eq[:, hs], eq[:, hs], i1f[:, hs, sd, :].unsqueeze(2).broadcast_to([P, HH, TOPK, TOPK]), ALU.mult)))
            V.wait(V.done(nc.vector.tensor_reduce(e[:, hs, :], eq[:, hs], AX_X, ALU.add)))
            yield True
        V.wait(V.done(nc.vector.scalar_tensor_tensor(out=idxf[:, ks], in0=small[:, 9, ks], scalar=float(E_KEYS),
                                                     in1=small[:, 10, ks], op0=ALU.mult, op1=ALU.add)))
        m_idx[t, group] = V.done(nc.vector.tensor_copy(idx[:, t, ks], idxf[:, ks]))
        yield True
        gt = g[:, t, ks].rearrange("p (h k) -> p h k", h=HH)
        th = tv[:, hs, :]
        m = V.done(nc.vector.tensor_tensor(gt, th, th[:, :, 0:1].broadcast_to([P, HH, TOPK]), ALU.subtract))
        A.wait(m)
        m = A.done(nc.scalar.activation(g[:, t, ks], g[:, t, ks], ACT.Exp))
        V.wait(m)
        V.wait(V.done(nc.vector.tensor_reduce(hsum[:, hs], gt, AX_X, ALU.add)))
        V.wait(V.done(nc.vector.reciprocal(hsum[:, hs], hsum[:, hs])))
        m_gate[t, group] = V.done(nc.vector.tensor_tensor(gt, gt, hsum[:, hs].unsqueeze(2).broadcast_to([P, HH, TOPK]),
                                                         ALU.mult))
        V.wait(m_gate[t, group])

    for group in range(GROUPS):
        n0 = group * HH * 2 * E_HALF
        c.split_cols(I["peer_w_q_2"][0], n0, n0 + HH * 2 * E_HALF, lambda a, k: hr[a][:, k * SEQ:(k + 1) * SEQ], m_h,
                     lambda j, cnt, ps, r: [c.evac(qT[:, group * HH + j:group * HH + j + cnt, :],
                                                   ps.rearrange("p (a b) -> p a b", b=SEQ), r)])
        m_q[group] = [V.last(), A.last()]
        if group == 0:
            c.background = [choose(0, 0)]
            c.steps = 2
    c.step(0)
    later = [choose(t, group) for t in range(NT) for group in range(GROUPS) if t or group]

    def step_later():
        while later and next(later[0], None) is None:
            later.pop(0)

    c.give_slot_back()
    STEP_EVERY = 3
    NG = 2 * RING
    bufs = [c.ring[:, i // 2, (i % 2) * D:(i % 2 + 1) * D] for i in range(NG)]
    gsem = [DmaSem(c.sem(f"gather{i}")) for i in range(NG)]
    read = [None] * NG
    for i in range(RING):
        read[2 * i] = read[2 * i + 1] = c.ring_free[i]
    n = 0
    store = DmaSem(c.sem("out_stored"))
    f_row = c.at(10 * K1, D)
    s = DmaSem(c.sem("final_g_loaded"))
    c.S.wait(V.last(), A.last(), PE.last())
    m_f = s.done(nc.sync.dma_start(f_row, I["final_norm_g_2"].partition_broadcast(P)))
    U, VT = I["peer_u_2"][0], I["peer_v_2"][0]
    for t in range(NT):
        for table in (U, VT):
            for k in range(E_SLOTS):
                q = n % NG
                n += 1
                while (t, k // (HH * TOPK)) not in m_idx:
                    step_later()
                G.wait(m_idx[t, k // (HH * TOPK)])
                G.wait(read[q])
                m = gsem[q].done(nc.gpsimd.indirect_dma_start(
                    bufs[q], None, table, bass.IndirectOffsetOnAxis(ap=idx[:, t, k:k + 1], axis=0)))
                V.wait(m)
                if table is U:
                    m = V.done(nc.vector.tensor_tensor_reduce(
                        out=bufs[q], in0=bufs[q], in1=hn[:, t, :], scale=1.0, scalar=0.0, op0=ALU.mult, op1=ALU.add,
                        accum_out=act[:, t, k:k + 1]))
                else:
                    V.wait(V.last())
                    m = V.done(nc.vector.scalar_tensor_tensor(
                        out=H[:, t, :], in0=bufs[q], scalar=act[:, t, k:k + 1], in1=H[:, t, :],
                        op0=ALU.mult, op1=ALU.add))
                read[q] = m
                if k % STEP_EVERY == 0:
                    step_later()
            if table is U:
                while (t, GROUPS - 1) not in m_gate:
                    step_later()
                A.wait(V.last())
                m = A.done(nc.scalar.activation(act[:, t, :], act[:, t, :], ACT.Gelu_apprx_tanh))
                V.wait(m)
                V.wait(V.done(nc.vector.tensor_tensor(act[:, t, :], act[:, t, :], g[:, t, :], ALU.mult)))
        c.rms_rows(lambda t: H[:, t, :], None, V.last(), tiles=range(t, t + 1))
        V.wait(m_f)
        m = V.done(nc.vector.scalar_tensor_tensor(out=H[:, t, :], in0=H[:, t, :], scalar=c.st[:, t:t + 1], in1=f_row,
                                                  op0=ALU.mult, op1=ALU.mult))
        c.S.wait(m)
        m = store.done(nc.sync.dma_start(out[0, t * P:(t + 1) * P, :], H[:, t, :]))
    c.S.wait(m)


def program(nc, I, out):
    with ExitStack() as ctx:
        dr = {
            "memk": nc.dram_tensor("mem_keys", (P, KD, SEQ), F32, kind="Internal").ap(),
            "memv": nc.dram_tensor("mem_values", (P, NT, D), F32, kind="Internal").ap(),
            "phase": nc.dram_tensor("phases", (S_TILES // S_BATCH, P, 2 * S_BATCH * SEQ), F32, kind="Internal").ap(),
        }
        c = Core(nc, ctx)
        constants(c, I)
        stage_phases(c, I, dr)
        stage_start(c, I, dr)
        gT = stage_attention(c, I)
        H = stage_attention_out(c, I, gT)
        c.step(0)
        c.barrier()
        stage_fourier(c, I, H)
        stage_mixer(c, I, dr, H)
        stage_memory(c, I, dr, H)
        stage_experts(c, I, H, out)


def _columns(v):
    return np.ascontiguousarray(np.asarray(v).reshape(-1, P).T)


def kernel(**inputs):
    import numpy as _np
    import concourse.bacc as _bacc
    from concourse import mybir as _mybir
    from concourse.bass_utils import run_bass_kernel_spmd as _run

    X = {k: _np.asarray(v) for k, v in inputs.items()}
    f = _np.float32
    pos = _np.arange(SEQ)

    def angles(rot):
        nf = rot // 4
        inv = (f(10000.0) ** (-_np.arange(nf, dtype=f) / f(nf))).astype(f)
        return _np.concatenate([(pos // 64).astype(f)[:, None] * inv, (pos % 64).astype(f)[:, None] * inv], 1)

    aa, ab = angles(ROPE_A), angles(HD)
    rope = _np.concatenate([_np.cos(aa), _np.sin(aa), _np.cos(ab), _np.sin(ab)], 1).astype(f)
    jk = (_np.arange(256)[:, None] * _np.arange(256)[None, :]) % 256 * (2 * _np.pi / 256)
    cb = X["conv_w_2"][0].T.reshape(8, P, TAPS).transpose(1, 0, 2).reshape(P, 8 * TAPS)
    packed = {
        "cvec": _np.concatenate([_columns(X["c"]), _columns(X["c_ctx"])], 1),
        "ada_b0": _columns(X["ada_b"][0]), "ada_b1": _columns(X["ada_b"][1]),
        "q_lora": _columns(X["q_lora_norm"]), "kv_lora": _columns(X["kv_lora_norm"]),
        "mix_g": _columns(X["norm_mix_g_2"]), "conv_b": _columns(X["conv_b_2"]),
        "conv_ln_g": _columns(X["conv_ln_g_2"]), "conv_ln_b": _columns(X["conv_ln_b_2"]),
        "grp_conv": _columns(X["grp_norm_conv_g_2"]), "grp_ssm": _columns(X["grp_norm_ssm_g_2"]),
        "ssm_d": _columns(X["ssm_d_2"]), "mem_g": _columns(X["norm_mem_g_2"]),
        "memn_g": _columns(X["mem_norm_g_2"]), "conv_w": cb,
        "lam_re": _columns(X["ssm_lam_re_2"]), "lam_im": _columns(X["ssm_lam_im_2"]),
        "log_dt": _columns(_np.repeat(X["ssm_log_dt_2"][0], S_STATE)),
    }
    Bd = _np.zeros((S_TILES, 2, S_DIM, 2, 2, S_STATE), f)
    Cd = _np.zeros((2, S_STATE, 2, S_TILES, 2, S_DIM), f)
    for part, s in enumerate(("re", "im")):
        b = X[f"ssm_b_{s}_2"][0].reshape(S_TILES, 2, S_STATE, S_DIM)
        cc = X[f"ssm_c_{s}_2"][0].reshape(S_TILES, 2, S_DIM, S_STATE)
        for gl in range(2):
            Bd[:, gl, :, part, gl, :] = b[:, gl].transpose(0, 2, 1)
            Cd[gl, :, part, :, gl, :] = cc[:, gl].transpose(2, 0, 1)
    arrays = {
        "colpack": _np.concatenate([packed[n] for n in COLS], 1),
        "ident": _np.eye(P, dtype=f), "ones": _np.ones((P, P), f),
        "iota": _np.tile(_np.arange(16, dtype=f), (P, 1)),
        "rope": rope.reshape(NT, P, 192).transpose(1, 0, 2),
        "dft": _np.concatenate([_np.cos(jk), _np.sin(jk)], 1).astype(f) / f(16),
        "ndft": -_np.sin(jk).astype(f) / f(16),
        "s5_b": Bd.reshape(S_TILES * 32, 2 * P),
        "s5_c": Cd.reshape(P, 2 * S_TILES * 32),
        "keysT": X["peer_keys_2"][0].transpose(1, 3, 0, 2).reshape(P, E_HEADS, E_KEYS),
    }
    for name in ("x", "ctx", "ada_w", "ln_g", "ln_b", "w_in_attn", "wq_b", "wkv_b", "q_norm_b", "k_norm_b",
                 "w_out_attn", "w_in_fourier", "w_out_fourier", "mem_2", "w_in_2", "ssm_glu_w_2", "w_out_2",
                 "w_q_mem_2", "w_kv_mem_2", "w_o_mem_2", "norm_ffn_g_2", "peer_w_q_2", "peer_u_2", "peer_v_2",
                 "final_norm_g_2"):
        arrays[name] = X[name]
    nc = _bacc.Bacc("TRN2", target_bir_lowering=False, num_devices=1)
    in_map, I = {}, {}
    for name, a in arrays.items():
        a = _np.ascontiguousarray(a)
        in_map[f"in_{name}"] = a
        I[name] = nc.dram_tensor(f"in_{name}", a.shape, _mybir.dt.from_np(a.dtype), kind="ExternalInput").ap()
    out = nc.dram_tensor("out_0", (1, SEQ, D), F32, kind="ExternalOutput").ap()
    program(nc, I, out)
    r = _run(nc, [in_map], core_ids=[0])
    return r.results[0]["out_0"]
```
